# Optimizing a Trainium2 kernel written in Bass

```python
import math
import jax, jax.numpy as jnp
from jax import lax
import numpy as np

D_MODEL = 1024
BATCH = 1
SEQ = 128
DEPTH = 4
DEC_BATCH = 1
DEC_SEQ = 256
PAST_LEN = 128

GRID_W = 64
N_MIXERS = 3
N_LAYERS_DA = (DEPTH + 2) // 3
N_LAYERS_RWKV = (DEPTH + 1) // 3
N_LAYERS_SWA = DEPTH // 3
Q_BLOCK = 128
ROPE_BASE = 10000.0
NORM_EPS = 1e-6
D_FF = 4 * D_MODEL
NEG_INF = -1e30
DA_HEAD_DIM = 64
DA_HEADS = D_MODEL // (2 * DA_HEAD_DIM)
RWKV_HEAD = 64
RWKV_HEADS = D_MODEL // RWKV_HEAD
RWKV_DECAY_LORA = 64
RWKV_ICLR_LORA = 64
RWKV_GATE_LORA = 128
RWKV_GN_EPS = 64e-5
SWA_HEAD_DIM = 64
SWA_HEADS = D_MODEL // SWA_HEAD_DIM
SWA_KV_HEADS = SWA_HEADS // 4
SWA_GROUP = SWA_HEADS // SWA_KV_HEADS
WINDOW = 128

kernel_name = 'hybrid_diffusion_prefix_trunk_step'

f32 = jnp.float32

def rms_norm(x, gain=None):
    xf = x.astype(f32)
    y = xf * lax.rsqrt(jnp.mean(xf * xf, axis=-1, keepdims=True) + NORM_EPS)
    if gain is not None:
        y = y * gain.astype(f32)
    return y.astype(x.dtype)

def modulation(cond, ada_w, ada_b):
    m = jax.nn.silu(cond) @ ada_w + ada_b
    return jnp.split(m[:, None, :], 6, axis=-1)

def adaln(x, shift, scale):
    return rms_norm(x) * (1 + scale) + shift

def squared_relu_mlp(h, w1, w2):
    return jnp.square(jax.nn.relu(h @ w1)) @ w2

def axial_rope(n_tok, head_dim):
    n_rows = n_tok // GRID_W
    rows = jnp.broadcast_to(jnp.arange(n_rows, dtype=f32)[:, None], (n_rows, GRID_W)).reshape(-1)
    cols = jnp.broadcast_to(jnp.arange(GRID_W, dtype=f32)[None, :], (n_rows, GRID_W)).reshape(-1)
    n_freq = head_dim // 4
    inv = ROPE_BASE ** (-jnp.arange(n_freq, dtype=f32) / n_freq)
    ang = jnp.concatenate([rows[:, None] * inv, cols[:, None] * inv], axis=-1)
    return jnp.cos(ang), jnp.sin(ang)

def apply_rope(x, cos, sin):
    shape = (cos.shape[0],) + (1,) * (x.ndim - 3) + (cos.shape[1],)
    cos = cos.reshape(shape)
    sin = sin.reshape(shape)
    x1, x2 = jnp.split(x.astype(f32), 2, axis=-1)
    return jnp.concatenate([x1 * cos - x2 * sin, x2 * cos + x1 * sin], axis=-1).astype(x.dtype)

def map_query_blocks(fn, q):
    b, t = q.shape[:2]
    nb = t // Q_BLOCK
    qb = jnp.moveaxis(q.reshape(b, nb, Q_BLOCK, *q.shape[2:]), 1, 0)
    out = jnp.moveaxis(lax.map(fn, qb), 0, 1)
    return out.reshape(b, t, *out.shape[3:])

def da_project(h, p):
    b, t, _ = h.shape
    q, k, v = jnp.split(h @ p['wqkv'], 3, axis=-1)
    q = rms_norm(q.reshape(b, t, DA_HEADS, 2, DA_HEAD_DIM), p['q_norm'])
    k = rms_norm(k.reshape(b, t, DA_HEADS, 2, DA_HEAD_DIM), p['k_norm'])
    v = v.reshape(b, t, DA_HEADS, 2 * DA_HEAD_DIM)
    return q, k, v

def da_lambda_value(lam, lam_init):
    lp = lam.astype(f32)
    return jnp.exp(jnp.sum(lp[0] * lp[1])) - jnp.exp(jnp.sum(lp[2] * lp[3])) + lam_init

def diff_attention(q, k, v, lam):
    scale = DA_HEAD_DIM ** -0.5

    def block(qb):
        s = jnp.einsum('bqhmd,bshmd->bhmqs', qb, k).astype(f32) * scale
        pr = jax.nn.softmax(s, axis=-1)
        pr = pr[:, :, 0] - lam * pr[:, :, 1]
        return jnp.einsum('bhqs,bshe->bqhe', pr, v).astype(v.dtype)

    return map_query_blocks(block, q)

def da_output(o, p, lam_init):
    b, t = o.shape[:2]
    o = rms_norm(o, p['subln']) * (1.0 - lam_init)
    return o.reshape(b, t, -1) @ p['wo']

def da_context(h, p, lam_init):
    b, t, _ = h.shape
    q, k, v = da_project(h, p)
    lam = da_lambda_value(p['lam'], lam_init)
    o = diff_attention(q, k, v, lam)
    return da_output(o, p, lam_init), k.reshape(b, t, DA_HEADS, 2 * DA_HEAD_DIM), v

def da_latent(h, ctx_k, ctx_v, cos, sin, p, lam_init):
    b = h.shape[0]
    q, k, v = da_project(h, p)
    q = apply_rope(q, cos, sin)
    k = apply_rope(k, cos, sin)
    n_ctx = ctx_k.shape[1]
    keys = jnp.concatenate([ctx_k.reshape(b, n_ctx, DA_HEADS, 2, DA_HEAD_DIM).astype(k.dtype), k], axis=1)
    vals = jnp.concatenate([ctx_v.astype(v.dtype), v], axis=1)
    lam = da_lambda_value(p['lam'], lam_init)
    o = diff_attention(q, keys, vals, lam)
    return da_output(o, p, lam_init)

def swa_project(h, p):
    b, t, _ = h.shape
    nq = SWA_HEADS * SWA_HEAD_DIM
    nk = SWA_KV_HEADS * SWA_HEAD_DIM
    q, k, v = jnp.split(h @ p['wqkv'], [nq, nq + nk], axis=-1)
    q = rms_norm(q.reshape(b, t, SWA_KV_HEADS, SWA_GROUP, SWA_HEAD_DIM), p['q_norm'])
    k = rms_norm(k.reshape(b, t, SWA_KV_HEADS, SWA_HEAD_DIM), p['k_norm'])
    v = v.reshape(b, t, SWA_KV_HEADS, SWA_HEAD_DIM)
    return q, k, v

def swa_context(h, p):
    b, t, _ = h.shape
    q, k, v = swa_project(h, p)
    scale = SWA_HEAD_DIM ** -0.5
    sink = p['sink'].astype(f32).reshape(SWA_KV_HEADS, SWA_GROUP)

    def block(qb):
        s = jnp.einsum('bqjgd,bsjd->bjgqs', qb, k).astype(f32) * scale
        sk = jnp.broadcast_to(sink[None, :, :, None, None], s.shape[:-1] + (1,))
        pr = jax.nn.softmax(jnp.concatenate([s, sk], axis=-1), axis=-1)[..., :-1]
        return jnp.einsum('bjgqs,bsjd->bqjgd', pr, v).astype(v.dtype)

    o = map_query_blocks(block, q)
    return o.reshape(b, t, -1) @ p['wo'], k, v

def swa_latent(h, ctx_k, ctx_v, cos, sin, p):
    b, t, _ = h.shape
    q, k, v = swa_project(h, p)
    q = apply_rope(q, cos, sin)
    k = apply_rope(k, cos, sin)
    scale = SWA_HEAD_DIM ** -0.5
    nb = t // WINDOW
    qb = q.reshape(b, nb, WINDOW, SWA_KV_HEADS, SWA_GROUP, SWA_HEAD_DIM)
    pad = ((0, 0), (WINDOW, WINDOW), (0, 0), (0, 0))
    kp = jnp.pad(k, pad).reshape(b, nb + 2, WINDOW, SWA_KV_HEADS, SWA_HEAD_DIM)
    vp = jnp.pad(v, pad).reshape(b, nb + 2, WINDOW, SWA_KV_HEADS, SWA_HEAD_DIM)
    kband = jnp.concatenate([kp[:, :-2], kp[:, 1:-1], kp[:, 2:]], axis=2)
    vband = jnp.concatenate([vp[:, :-2], vp[:, 1:-1], vp[:, 2:]], axis=2)
    s_loc = jnp.einsum('bnqjgd,bnsjd->bnjgqs', qb, kband).astype(f32) * scale
    qi = jnp.arange(WINDOW)[:, None]
    si = jnp.arange(3 * WINDOW)[None, :]
    rel = si - qi
    in_window = (rel >= 0) & (rel <= 2 * WINDOW)
    key_pos = (jnp.arange(nb)[:, None, None] - 1) * WINDOW + si[None]
    valid = in_window[None] & (key_pos >= 0) & (key_pos < t)
    s_loc = jnp.where(valid[None, :, None, None], s_loc, NEG_INF)
    s_ctx = jnp.einsum('bnqjgd,bljd->bnjgql', qb, ctx_k.astype(q.dtype)).astype(f32) * scale
    sink = p['sink'].astype(f32).reshape(SWA_KV_HEADS, SWA_GROUP)
    sk = jnp.broadcast_to(sink[None, None, :, :, None, None], s_loc.shape[:-1] + (1,))
    n_ctx = ctx_k.shape[1]
    pr = jax.nn.softmax(jnp.concatenate([s_ctx, s_loc, sk], axis=-1), axis=-1)
    o = (jnp.einsum('bnjgql,bljd->bnqjgd', pr[..., :n_ctx], ctx_v.astype(f32))
         + jnp.einsum('bnjgqs,bnsjd->bnqjgd', pr[..., n_ctx:n_ctx + 3 * WINDOW], vband))
    return o.reshape(b, t, -1).astype(h.dtype) @ p['wo']

def token_shift_delta(x):
    xp = jnp.pad(x, ((0, 0), (1, 1), (0, 0)))
    return 0.5 * (xp[:, :-2] + xp[:, 2:]) - x

def wkv_scan(s0, r, w, k, v, a, bb, reverse):
    seq = tuple(jnp.moveaxis(z.astype(f32), 1, 0) for z in (r, w, k, v, a, bb))

    def step(s, inp):
        rt, wt, kt, vt, at, bt = inp
        sa = jnp.einsum('bhvk,bhk->bhv', s, at)
        s = s * wt[:, :, None, :] + sa[..., None] * bt[:, :, None, :] + vt[..., None] * kt[:, :, None, :]
        return s, jnp.einsum('bhvk,bhk->bhv', s, rt)

    s_fin, ys = lax.scan(step, s0.astype(f32), seq, reverse=reverse)
    return s_fin, jnp.moveaxis(ys, 0, 1)

def rwkv_mixer(h, s0, p):
    b, t, d = h.shape
    heads = lambda z: z.reshape(*z.shape[:-1], RWKV_HEADS, RWKV_HEAD)
    xx = token_shift_delta(h)
    xs = h[None] + xx[None] * p['mu'][:, None, None, :]
    r, k, v = jnp.einsum('mbtd,mde->mbte', xs[:3], p['wrkv'])
    xw, xa, xg = xs[3], xs[4], xs[5]
    w_lora = jnp.einsum('zbtr,zrd->zbtd', jnp.tanh(jnp.einsum('btd,zdr->zbtr', xw, p['w1'])), p['w2'])
    w_log = -jax.nn.softplus(-(p['w0'][:, None, None, :] + w_lora).astype(f32)) - 0.5
    decay = jnp.exp(-jnp.exp(w_log))
    a_lora = jnp.einsum('zbtr,zrd->zbtd', jnp.einsum('btd,zdr->zbtr', xa, p['a1']), p['a2'])
    a = jax.nn.sigmoid((p['a0'][:, None, None, :] + a_lora).astype(f32))
    g = jax.nn.sigmoid(xg @ p['g1']) @ p['g2']
    kk = heads((k * p['k_k']).astype(f32))
    kk = kk * lax.rsqrt(jnp.maximum(jnp.sum(kk * kk, axis=-1, keepdims=True), 1e-24))
    kd = heads(k.astype(f32)[None] * (1 + (a - 1) * p['k_a'].astype(f32)))
    b_vec = kk[None] * heads(a)
    r_h = heads(r.astype(f32))
    v_h = heads(v.astype(f32))
    s_f, y_f = wkv_scan(s0[:, 0], r_h, heads(decay[0]), kd[0], v_h, -kk, b_vec[0], False)
    s_b, y_b = wkv_scan(s0[:, 1], r_h, heads(decay[1]), kd[1], v_h, -kk, b_vec[1], True)
    y = y_f + y_b
    mu = jnp.mean(y, axis=-1, keepdims=True)
    var = jnp.mean(jnp.square(y - mu), axis=-1, keepdims=True)
    y = (y - mu) * lax.rsqrt(var + RWKV_GN_EPS) * heads(p['ln_w'].astype(f32)) + heads(p['ln_b'].astype(f32))
    bonus = jnp.sum(r_h[None] * kd * p['r_k'].astype(f32), axis=-1, keepdims=True).sum(axis=0) * v_h
    out = ((y + bonus).reshape(b, t, d).astype(h.dtype) * g) @ p['wo']
    return out, jnp.stack([s_f, s_b], axis=1).astype(h.dtype)

def setup_inputs(seed: int = 0) -> dict:
    key = jax.random.key(seed)
    ks = iter(jax.random.split(key, 64))
    D = D_MODEL

    def nrm(shape, scale):
        return scale * jax.random.normal(next(ks), shape, f32)

    def uni(shape, lo, hi):
        return jax.random.uniform(next(ks), shape, f32, lo, hi)

    nq = SWA_HEADS * SWA_HEAD_DIM
    return {
        'x_prompt': nrm((BATCH, SEQ, D), 1.0),
        'x_sample': nrm((DEC_BATCH, DEC_SEQ, D), 1.0),
        'cache_da_k': nrm((DEC_BATCH, N_LAYERS_DA, PAST_LEN, DA_HEADS, 2 * DA_HEAD_DIM), 1.0),
        'cache_da_v': nrm((DEC_BATCH, N_LAYERS_DA, PAST_LEN, DA_HEADS, 2 * DA_HEAD_DIM), 1.0),
        'state_rwkv': nrm((DEC_BATCH, N_LAYERS_RWKV, 2, RWKV_HEADS, RWKV_HEAD, RWKV_HEAD), 1.0),
        'cache_swa_k': nrm((DEC_BATCH, N_LAYERS_SWA, PAST_LEN, SWA_KV_HEADS, SWA_HEAD_DIM), 1.0),
        'cache_swa_v': nrm((DEC_BATCH, N_LAYERS_SWA, PAST_LEN, SWA_KV_HEADS, SWA_HEAD_DIM), 1.0),
        'c': nrm((DEC_BATCH, D), 1.0),
        'c_ctx': nrm((D,), 1.0),
        'ada_w': nrm((DEPTH, D, 6 * D), 0.5 * D ** -0.5),
        'ada_b': nrm((DEPTH, 6 * D), 0.02),
        'mlp_w1': nrm((DEPTH, D, D_FF), D ** -0.5),
        'mlp_w2': nrm((DEPTH, D_FF, D), D_FF ** -0.5),
        'da_wqkv': nrm((N_LAYERS_DA, D, 3 * D), D ** -0.5),
        'da_q_norm': 1.0 + nrm((N_LAYERS_DA, DA_HEAD_DIM), 0.02),
        'da_k_norm': 1.0 + nrm((N_LAYERS_DA, DA_HEAD_DIM), 0.02),
        'da_lambda': nrm((N_LAYERS_DA, 4, DA_HEAD_DIM), 0.1),
        'da_subln': 1.0 + nrm((N_LAYERS_DA, 2 * DA_HEAD_DIM), 0.02),
        'da_wo': nrm((N_LAYERS_DA, D, D), D ** -0.5),
        'rwkv_mu': uni((N_LAYERS_RWKV, 6, D), 0.0, 1.0),
        'rwkv_wrkv': nrm((N_LAYERS_RWKV, 3, D, D), D ** -0.5),
        'rwkv_w0': uni((N_LAYERS_RWKV, 2, D), -6.0, 1.0),
        'rwkv_w1': nrm((N_LAYERS_RWKV, 2, D, RWKV_DECAY_LORA), D ** -0.5),
        'rwkv_w2': nrm((N_LAYERS_RWKV, 2, RWKV_DECAY_LORA, D), 0.5 * RWKV_DECAY_LORA ** -0.5),
        'rwkv_a0': nrm((N_LAYERS_RWKV, 2, D), 0.1),
        'rwkv_a1': nrm((N_LAYERS_RWKV, 2, D, RWKV_ICLR_LORA), D ** -0.5),
        'rwkv_a2': nrm((N_LAYERS_RWKV, 2, RWKV_ICLR_LORA, D), 0.5 * RWKV_ICLR_LORA ** -0.5),
        'rwkv_g1': nrm((N_LAYERS_RWKV, D, RWKV_GATE_LORA), D ** -0.5),
        'rwkv_g2': nrm((N_LAYERS_RWKV, RWKV_GATE_LORA, D), RWKV_GATE_LORA ** -0.5),
        'rwkv_k_k': 0.85 + nrm((N_LAYERS_RWKV, D), 0.02),
        'rwkv_k_a': 1.0 + nrm((N_LAYERS_RWKV, D), 0.02),
        'rwkv_r_k': nrm((N_LAYERS_RWKV, RWKV_HEADS, RWKV_HEAD), 0.1),
        'rwkv_ln_w': 1.0 + nrm((N_LAYERS_RWKV, D), 0.02),
        'rwkv_ln_b': nrm((N_LAYERS_RWKV, D), 0.02),
        'rwkv_wo': nrm((N_LAYERS_RWKV, D, D), D ** -0.5),
        'swa_wqkv': nrm((N_LAYERS_SWA, D, nq + 2 * SWA_KV_HEADS * SWA_HEAD_DIM), D ** -0.5),
        'swa_q_norm': 1.0 + nrm((N_LAYERS_SWA, SWA_HEAD_DIM), 0.02),
        'swa_k_norm': 1.0 + nrm((N_LAYERS_SWA, SWA_HEAD_DIM), 0.02),
        'swa_sink': nrm((N_LAYERS_SWA, SWA_HEADS), 0.5),
        'swa_wo': nrm((N_LAYERS_SWA, nq, D), nq ** -0.5),
    }

def reference(x_prompt, x_sample, cache_da_k, cache_da_v, state_rwkv, cache_swa_k, cache_swa_v, c,
              c_ctx, ada_w, ada_b, mlp_w1, mlp_w2,
              da_wqkv, da_q_norm, da_k_norm, da_lambda, da_subln, da_wo,
              rwkv_mu, rwkv_wrkv, rwkv_w0, rwkv_w1, rwkv_w2, rwkv_a0, rwkv_a1, rwkv_a2,
              rwkv_g1, rwkv_g2, rwkv_k_k, rwkv_k_a, rwkv_r_k, rwkv_ln_w, rwkv_ln_b, rwkv_wo,
              swa_wqkv, swa_q_norm, swa_k_norm, swa_sink, swa_wo):
    x_ctx = x_prompt
    x_lat = x_sample
    n_lat = x_sample.shape[1]
    cos_da, sin_da = axial_rope(n_lat, DA_HEAD_DIM)
    cos_swa, sin_swa = axial_rope(n_lat, SWA_HEAD_DIM)
    b_ctx = x_prompt.shape[0]
    da_k_list, da_v_list, rwkv_list, swa_k_list, swa_v_list = [], [], [], [], []
    for i in range(DEPTH):
        kind = i % N_MIXERS
        j = i // N_MIXERS
        sh_m_c, sc_m_c, g_m_c, sh_f_c, sc_f_c, g_f_c = modulation(c_ctx[None, :], ada_w[i], ada_b[i])
        sh_m_l, sc_m_l, g_m_l, sh_f_l, sc_f_l, g_f_l = modulation(c, ada_w[i], ada_b[i])
        h_ctx = adaln(x_ctx, sh_m_c, sc_m_c)
        h_lat = adaln(x_lat, sh_m_l, sc_m_l)
        if kind == 0:
            p = {'wqkv': da_wqkv[j], 'q_norm': da_q_norm[j], 'k_norm': da_k_norm[j],
                 'lam': da_lambda[j], 'subln': da_subln[j], 'wo': da_wo[j]}
            lam_init = 0.8 - 0.6 * math.exp(-0.3 * i)
            o_ctx, k_new, v_new = da_context(h_ctx, p, lam_init)
            o_lat = da_latent(h_lat, cache_da_k[:, j], cache_da_v[:, j], cos_da, sin_da, p, lam_init)
            da_k_list.append(k_new)
            da_v_list.append(v_new)
        elif kind == 1:
            p = {'mu': rwkv_mu[j], 'wrkv': rwkv_wrkv[j], 'w0': rwkv_w0[j], 'w1': rwkv_w1[j],
                 'w2': rwkv_w2[j], 'a0': rwkv_a0[j], 'a1': rwkv_a1[j], 'a2': rwkv_a2[j],
                 'g1': rwkv_g1[j], 'g2': rwkv_g2[j], 'k_k': rwkv_k_k[j], 'k_a': rwkv_k_a[j],
                 'r_k': rwkv_r_k[j], 'ln_w': rwkv_ln_w[j], 'ln_b': rwkv_ln_b[j], 'wo': rwkv_wo[j]}
            s_zero = jnp.zeros((b_ctx, 2, RWKV_HEADS, RWKV_HEAD, RWKV_HEAD), f32)
            o_ctx, s_new = rwkv_mixer(h_ctx, s_zero, p)
            o_lat, _ = rwkv_mixer(h_lat, state_rwkv[:, j], p)
            rwkv_list.append(s_new)
        else:
            p = {'wqkv': swa_wqkv[j], 'q_norm': swa_q_norm[j], 'k_norm': swa_k_norm[j],
                 'sink': swa_sink[j], 'wo': swa_wo[j]}
            o_ctx, k_new, v_new = swa_context(h_ctx, p)
            o_lat = swa_latent(h_lat, cache_swa_k[:, j], cache_swa_v[:, j], cos_swa, sin_swa, p)
            swa_k_list.append(k_new)
            swa_v_list.append(v_new)
        x_ctx = x_ctx + g_m_c * o_ctx
        x_lat = x_lat + g_m_l * o_lat
        x_ctx = x_ctx + g_f_c * squared_relu_mlp(adaln(x_ctx, sh_f_c, sc_f_c), mlp_w1[i], mlp_w2[i])
        x_lat = x_lat + g_f_l * squared_relu_mlp(adaln(x_lat, sh_f_l, sc_f_l), mlp_w1[i], mlp_w2[i])
    new_da_k = jnp.stack(da_k_list, axis=1)
    new_da_v = jnp.stack(da_v_list, axis=1)
    new_state_rwkv = jnp.stack(rwkv_list, axis=1)
    new_swa_k = jnp.stack(swa_k_list, axis=1)
    new_swa_v = jnp.stack(swa_v_list, axis=1)
    return (x_ctx, x_lat, new_da_k, new_da_v, new_state_rwkv, new_swa_k, new_swa_v)


_drawn_inputs = setup_inputs


def setup_inputs(seed=0):
    import zlib

    import numpy as np

    out = dict(_drawn_inputs(seed))
    spreads = {}
    factors = {'cache_swa_k': 4.654,
     'cache_swa_v': 3.754,
     'da_q_norm': 8.0,
     'da_k_norm': 2.801,
     'da_subln': 6.579,
     'rwkv_ln_w': 8.0,
     'rwkv_ln_b': 8.0,
     'swa_q_norm': 8.0,
     'swa_sink': 64.0,
     'cache_da_k': 8.0,
     'cache_da_v': 8.0}
    for name, (base, spread) in spreads.items():
        noise = np.random.default_rng([zlib.crc32(name.encode()), seed]).standard_normal(out[name].shape)
        drawn = base * np.exp(spread * noise) if base else spread * noise
        out[name] = __import__('jax').numpy.asarray(drawn.astype(out[name].dtype))
    for name, factor in factors.items():
        out[name] = (out[name] * factor).astype(out[name].dtype)
    return out
```

```python
import math
from contextlib import ExitStack

import numpy as np

import concourse.bass as bass
from concourse import mybir

F32 = mybir.dt.float32
ACT = mybir.ActivationFunctionType
ALU = mybir.AluOpType
AX_X = mybir.AxisListType.X

P = 128
D = 1024
KT = D // P
CTX, LAT, PAST = 128, 256, 128
TOK = CTX + LAT
TT = TOK // P
DEPTH = 4
FF = 4 * D
FT = FF // P
HD = 64
GRID_W = 64
CH = 64
NCH = TOK // CH
LEVELS = 6
EPS = 1e-6
GN_EPS = 64e-5
DECAY = math.exp(-0.5)
NEG_INF = -1e30
SCALE = HD ** -0.5
GROUPS = ((0, slice(0, CTX)), (1, slice(CTX, TOK)))
SLAB = 256
SLOTS = 4
ADA_SLOTS = 3
ADA_UNITS = 6 * D // SLAB

CONST_COLS = {}
_at = 0
for _name, _n in (("ident", P), ("blocks", P), ("ones", P), ("swap32", P), ("swap64", P), ("cos", LAT), ("sin", LAT),
                  ("band", 2 * TOK), ("eye64", 64), ("first", 2 * 64), ("levels", 2 * LEVELS * 64),
                  ("causal", 2 * 128), ("restart", TOK), ("eps", 1), ("gn_eps", 1)):
    CONST_COLS[_name] = slice(_at, _at + _n)
    _at += _n
CONST_N = _at


def constants():
    c = np.zeros((P, CONST_N), np.float32)
    p = np.arange(P)[:, None]
    q = np.arange(P)[None, :]
    c[:, CONST_COLS["ident"]] = p == q
    c[:, CONST_COLS["blocks"]] = p // 64 == q // 64
    c[:, CONST_COLS["ones"]] = 1
    c[:, CONST_COLS["swap32"]] = p == (q ^ 32)
    c[:, CONST_COLS["swap64"]] = p == (q ^ 64)
    t = np.arange(LAT)
    n_freq = HD // 4
    inv = (np.float32(10000.0) ** (-np.arange(n_freq, dtype=np.float32) / n_freq)).astype(np.float32)
    ang = np.concatenate([(t // GRID_W).astype(np.float32)[:, None] * inv,
                          (t % GRID_W).astype(np.float32)[:, None] * inv], axis=1).astype(np.float32)
    d = np.arange(P) % HD
    c[:, CONST_COLS["cos"]] = np.cos(ang.astype(np.float64))[:, d % 32].T
    c[:, CONST_COLS["sin"]] = (np.sin(ang.astype(np.float64))[:, d % 32] * np.where(d < 32, -1, 1)).T
    band = np.zeros((P, 2, TOK))
    for b in range(2):
        far = np.abs(np.arange(LAT)[None, :] - (np.arange(P)[:, None] + b * P)) > 128
        band[:, b, :LAT][far] = NEG_INF
    c[:, CONST_COLS["band"]] = band.reshape(P, -1)
    r = np.arange(P)[:, None] % 64
    s = np.arange(64)[None, :]
    c[:, CONST_COLS["eye64"]] = r == s
    first, levels, causal = np.zeros((P, 2, 64)), np.zeros((P, 2, LEVELS, 64)), np.zeros((P, 2, 2, 64))
    for z in range(2):
        row, col = (r, s) if z == 0 else (63 - r, 63 - s)
        first[:, z] = (row // 2 == col // 2) & (row > col)
        for n in range(LEVELS):
            w = 1 << n
            levels[:, z, n] = (row // (2 * w) == col // (2 * w)) & (row // w < col // w)
        causal[:, z, 0] = row < col
        causal[:, z, 1] = row <= col
    c[:, CONST_COLS["first"]] = first.reshape(P, -1)
    c[:, CONST_COLS["levels"]] = levels.reshape(P, -1)
    c[:, CONST_COLS["causal"]] = causal.reshape(P, -1)
    c[:, CONST_COLS["restart"]] = (np.arange(TOK) % CH != 0)[None, :]
    c[:, CONST_COLS["eps"]] = EPS
    c[:, CONST_COLS["gn_eps"]] = GN_EPS
    return c


def over(ap, n):
    return ap.unsqueeze(1).to_broadcast([ap.shape[0], n, ap.shape[1]])


def build(nc, I, O):
    ctx = ExitStack()
    with ctx:
        def sb(name, *shape):
            return ctx.enter_context(nc.sbuf_tensor(name, [P, *shape], F32))

        sems = {}

        def sem(name):
            if name not in sems:
                sems[name] = ctx.enter_context(nc.semaphore(name))
            return sems[name]

        const = sb("const", CONST_N)
        K = {n: const[:, s] for n, s in CONST_COLS.items()}
        band = K["band"].rearrange("p (b t) -> p b t", b=2)
        first = K["first"].rearrange("p (z t) -> p z t", z=2)
        levels = K["levels"].rearrange("p (z n t) -> p z n t", z=2, n=LEVELS)
        causal = K["causal"].rearrange("p (z t) -> p z t", z=2)
        xT = sb("xT", KT, TOK)
        hT = sb("hT", KT, TOK)
        slab = sb("slab", SLOTS, KT, SLAB)
        ada_slab = sb("ada_slab", ADA_SLOTS, KT, SLAB)
        mod = sb("mod", DEPTH, 48, 2)
        ada_b = sb("ada_b", DEPTH * 48)
        cond = sb("cond", KT, 2)
        rstd = sb("rstd", TOK)
        small = sb("small", 8)
        vecs = sb("vecs", 120)
        lam = sb("lam", 8)
        arena = sb("arena", 27900)
        psum = ctx.enter_context(nc.psum_tensor("psum", [P, 8, 512], F32))

        def bank(b, *shape):
            n = int(np.prod(shape))
            v = psum[:, b, 0:n]
            return v if len(shape) == 1 else v.rearrange("p (a b) -> p a b", a=shape[0])

        class Carve:

            def __init__(self, of=None):
                self.at, self.of = 0, arena[:, :] if of is None else of

            def __call__(self, *shape):
                n = int(np.prod(shape))
                v = self.of[:, self.at:self.at + n]
                self.at += n
                assert self.at <= self.of.shape[1], self.at
                names = "abcd"[:len(shape)]
                if len(shape) > 1:
                    v = v.rearrange(f"p ({' '.join(names)}) -> p {' '.join(names)}",
                                    **dict(zip(names[:-1], shape)))
                return v

        count = {}

        def base(name):
            return count.get(name, 0)

        def add(**kw):
            for k, v in kw.items():
                count[k] = count.get(k, 0) + v

        class Link:

            def __init__(self, eng, name, start=None):
                self.eng, self.name, self.sem, self.n = eng, name, sem(name), 0
                self.start = base(name) if start is None else start

            def __call__(self, ins):
                self.n += 1
                ins.then_inc(self.sem, 1)
                self.eng.wait_ge(self.sem, self.start + self.n)

            def close(self):
                add(**{self.name: self.n})

        def alone(eng):
            eng.wait_ge(sem("const_in"), 16)

        def start_at(eng, name, value):
            if not (isinstance(value, int) and value <= 0):
                eng.wait_ge(sem(name), value)
                if not isinstance(value, int):
                    alone(eng)

        slab_ready = [sem(f"slab_ready{s}") for s in range(SLOTS)]
        run_done, acc_taken = sem("run_done"), sem("acc_taken")
        run_after = []
        phases = {}

        def phase(name, runs, src):
            phases[name] = (len(run_after), len(runs), src)
            for r in runs:
                run_after.append((run_after[-1] if run_after else 0) + r)

        def cols(w, at):
            return w.rearrange("(k p) n -> p k n", p=P)[:, :, bass.ds(at, SLAB)]

        def load_unit(sp, name, u):
            start, _, src = phases[name]
            g = start + u
            if g >= SLOTS:
                sp.wait_ge(run_done, run_after[g - SLOTS])
            sp.dma_start(slab[:, g % SLOTS], src(u)).then_inc(slab_ready[g % SLOTS], 16)

        def load_phase(sp, name, following):
            for u in range(SLOTS, phases[name][1]):
                load_unit(sp, name, u)
            load_first(sp, following)

        def load_first(sp, following):
            if following:
                for u in range(min(SLOTS, phases[following][1])):
                    load_unit(sp, following, u)

        def has_slab(pe, u, it=0):
            pe.wait_ge(slab_ready[u % SLOTS], 16 * (u // SLOTS + 1) + it * 16)

        ADA_STEPS = ADA_UNITS // ADA_SLOTS

        def ada_load(sp, layer, it):
            for s in range(ADA_SLOTS):
                a = layer * ADA_STEPS + it
                start_at(sp, "ada_used", (a - 1) * ADA_SLOTS + (s + 1))
                sp.dma_start(ada_slab[:, s], cols(I["ada_w"][layer], (it * ADA_SLOTS + s) * SLAB))\
                    .then_inc(sem(f"ada_ready{s}"), 16)

        def ada_products(pe, layer, it, s):
            a = layer * ADA_STEPS + it
            pe.wait_ge(sem(f"ada_ready{s}"), (a + 1) * 16)
            if s == 0:
                start_at(pe, "mod_step", a)
            for j in range(2):
                at = 2 * (2 * s + j)
                for k in range(KT):
                    mm = nc.tensor.matmul(psum[:, 6, at:at + 2], ada_slab[:, s, k, j * P:(j + 1) * P], cond[:, k, :],
                                          start=k == 0, stop=k == KT - 1)
            mm.then_inc(sem("ada_used"), 1)

        def ada_take(dve, layer, it):
            a = layer * ADA_STEPS + it
            dve.wait_ge(sem("ada_used"), (a + 1) * ADA_SLOTS)
            n = 2 * ADA_SLOTS
            nc.vector.tensor_tensor(
                mod[:, layer, bass.ds(it * n, n), :], bank(6, n, 2),
                ada_b[:, bass.ds(it * n + layer * 48, n)].unsqueeze(2).to_broadcast([P, n, 2]),
                ALU.add).then_inc(sem("mod_step"), 1)

        def ada_scale(dve, layer):
            dve.wait_ge(sem("mod_step"), (layer + 1) * ADA_STEPS)
            for c in (1, 4):
                m = mod[:, layer, c * KT:(c + 1) * KT, :]
                nc.vector.tensor_scalar(m, m, 1.0, None, ALU.add).then_inc(sem("mod_ready"), 1)

        def norm_act(act, layer, half, out):
            b = base("sq_ready")
            act.wait_ge(sem("mod_ready"), 2 * (layer + 1))
            for k in range(KT):
                nc.scalar.activation(hT[:, k], xT[:, k], ACT.Square).then_inc(sem("sq_ready"), 1)
            act.wait_ge(sem("sum_done"), base("sum_done") + 1)
            nc.scalar.activation(rstd[:, :], bank(7, TOK), ACT.Sqrt, scale=1.0 / D, bias=K["eps"])\
                .then_inc(sem("std_ready"), 1)
            for k in range(KT):
                act.wait_ge(sem("xn_ready"), b + k + 1)
                for g, t in GROUPS:
                    ins = nc.scalar.activation(out(k, g), hT[:, k, t], ACT.Identity,
                                               scale=mod[:, layer, (3 * half + 1) * KT + k, g:g + 1],
                                               bias=mod[:, layer, 3 * half * KT + k, g:g + 1])
                ins.then_inc(sem("h_ready"), 1)

        def norm_pe(pe):
            for k in range(KT):
                pe.wait_ge(sem("sq_ready"), base("sq_ready") + k + 1)
                mm = nc.tensor.matmul(bank(7, TOK), K["ones"], hT[:, k], start=k == 0, stop=k == KT - 1)
            mm.then_inc(sem("sum_done"), 1)

        def norm_dve(dve, link):
            dve.wait_ge(sem("std_ready"), base("sum_done") + 1)
            link(nc.vector.reciprocal(rstd[:, :], rstd[:, :]))
            for k in range(KT):
                nc.vector.tensor_tensor(hT[:, k], xT[:, k], rstd[:, :], ALU.mult).then_inc(sem("xn_ready"), 1)

        def norm_counts():
            add(sq_ready=KT, sum_done=1)

        def in_place(k, g):
            return hT[:, k, GROUPS[g][1]]

        def has_h(pe, k):
            pe.wait_ge(sem("h_ready"), base("sq_ready") + k + 1)

        def flat(ap):
            return ap.rearrange("p a b -> p (a b)")

        def residual(layer, half, n, acc):
            for g, t in GROUPS:
                gate = flat(mod[:, layer, bass.ds(n + (3 * half + 2) * KT, 1), g:g + 1])
                x = flat(xT[:, bass.ds(n, 1), t])
                ins = nc.vector.scalar_tensor_tensor(x, acc[:, t], gate, x, ALU.mult, ALU.add)
            return ins

        def lambda_init(i):
            return 0.8 - 0.6 * math.exp(-0.3 * i)

        def setup(following):
            carve = Carve()
            xtok = carve(TT, D)
            rows = carve(4, P)
            lam_in = carve(2, 4, HD)
            sg = carve(16)
            n_rows = (96, 96, 120, 24)

            def row(v):
                return v.rearrange("(r p) -> r p", p=P)

            ab = row(I["ada_b"].rearrange("l n -> (l n)"))
            loads = [(rows[0:96, 0], ab[0:96]), (rows[0:96, 1], ab[96:192])]
            at = 0
            for v in (I["rwkv_mu"].rearrange("l m d -> (l m d)"), I["rwkv_w0"].rearrange("l z d -> (l z d)"),
                      I["rwkv_a0"].rearrange("l z d -> (l z d)"), I["rwkv_k_k"][0], I["rwkv_k_a"][0],
                      I["rwkv_r_k"][0].rearrange("h d -> (h d)"), I["rwkv_ln_w"][0], I["rwkv_ln_b"][0]):
                m = v.shape[0] // P
                loads.append((rows[at:at + m, 2], row(v)))
                at += m
            assert at == 120
            loads += [(rows[0:8, 3], row(I["c_ctx"])), (rows[8:16, 3], row(I["c"][0]))]
            at = 16
            for v in (I["da_q_norm"][0], I["da_k_norm"][0], I["da_q_norm"][1], I["da_k_norm"][1],
                      I["swa_q_norm"][0], I["swa_k_norm"][0]):
                one = v.unsqueeze(0)
                loads += [(rows[at:at + 1, 3, 0:HD], one), (rows[at:at + 1, 3, HD:P], one)]
                at += 1
            for j in range(2):
                loads.append((rows[at:at + 1, 3], I["da_subln"][j:j + 1]))
                at += 1
            loads.append((lam_in, I["da_lambda"].unsqueeze(0).to_broadcast([P, 2, 4, HD])))
            x_loads = [(xtok[:, 0], I["x_prompt"][0])] + [
                (xtok[:, 1 + t], I["x_sample"][0, t * P:(t + 1) * P]) for t in range(2)]
            with nc.Block() as block:
                @block.sync
                def _(sp):
                    sp.dma_start(const[:, :], I["consts"]).then_inc(sem("const_in"), 16)
                    ada_load(sp, 0, 0)
                    with sp.Fori(1, ADA_STEPS) as it:
                        ada_load(sp, 0, it)
                    load_first(sp, following)

                @block.scalar
                def _(act):
                    for dst, s in loads:
                        act.dma_start(dst, s).then_inc(sem("rows_in"), 16)
                    for dst, s in x_loads:
                        act.dma_start(dst, s).then_inc(sem("x_in"), 16)
                    act.wait_ge(sem("rows_done"), 4)
                    nc.scalar.activation(sg[:, :], bank(3, 24)[:, 0:16], ACT.Sigmoid).then_inc(sem("sig_cond"), 1)
                    for j in range(2):
                        act.wait_ge(sem("lam_dots"), 2 * (j + 1))
                        nc.scalar.activation(lam[:, 4 * j:4 * j + 2], lam[:, 4 * j:4 * j + 2], ACT.Exp)\
                            .then_inc(sem("lam_exps"), 1)

                @block.tensor
                def _(pe):
                    pe.wait_ge(sem("const_in"), 16)
                    pe.wait_ge(sem("rows_in"), 16 * len(loads))
                    for i, n in enumerate(n_rows):
                        nc.tensor.transpose(bank(i, n), rows[0:n, i], K["ident"][0:n, 0:n])\
                            .then_inc(sem("rows_done"), 1)
                    pe.wait_ge(sem("x_in"), 16 * TT)
                    for k in range(KT):
                        if k >= 2:
                            pe.wait_ge(sem("x_taken"), k - 1)
                        for t in range(TT):
                            mm = nc.tensor.transpose(bank(4 + k % 2, TT, P)[:, t], xtok[:, t, k * P:(k + 1) * P],
                                                     K["ident"])
                        mm.then_inc(sem("x_turned"), 1)
                    pe.wait_ge(sem("cond_ready"), 1)
                    for s in range(ADA_SLOTS):
                        ada_products(pe, 0, 0, s)
                    with pe.Fori(1, ADA_STEPS) as it:
                        for s in range(ADA_SLOTS):
                            ada_products(pe, 0, it, s)

                @block.vector
                def _(dve):
                    link = Link(dve, "dve_step")
                    dve.wait_ge(sem("rows_done"), 4)
                    nc.vector.tensor_copy(ada_b[:, 0:96], bank(0, 96))
                    nc.vector.tensor_copy(ada_b[:, 96:192], bank(1, 96))
                    link(nc.vector.tensor_copy(vecs[:, :], bank(2, 120)))
                    dve.wait_ge(sem("sig_cond"), 1)
                    link(nc.vector.tensor_copy(small[:, :], bank(3, 24)[:, 16:24]))
                    nc.vector.tensor_tensor(cond[:, :, :].rearrange("p k g -> p g k"),
                                            bank(3, 24)[:, 0:16].rearrange("p (g k) -> p g k", g=2),
                                            sg.rearrange("p (g k) -> p g k", g=2), ALU.mult)\
                        .then_inc(sem("cond_ready"), 1)
                    for k in range(KT):
                        dve.wait_ge(sem("x_turned"), k + 1)
                        nc.vector.tensor_copy(xT[:, k], bank(4 + k % 2, TOK)).then_inc(sem("x_taken"), 1)
                    for j in range(2):
                        s = small[:, 6 + j:7 + j]
                        link(nc.vector.tensor_scalar(s, s, 1.0 - lambda_init(3 * j), None, ALU.mult))
                    for j in range(2):
                        for m in range(2):
                            link(nc.vector.tensor_tensor(lam_in[:, j, 2 * m], lam_in[:, j, 2 * m],
                                                         lam_in[:, j, 2 * m + 1], ALU.mult))
                            nc.vector.tensor_reduce(lam[:, 4 * j + m:4 * j + m + 1], lam_in[:, j, 2 * m], AX_X,
                                                    ALU.add).then_inc(sem("lam_dots"), 1)
                        dve.wait_ge(sem("lam_exps"), j + 1)
                        link(nc.vector.tensor_scalar(lam[:, 4 * j + 2:4 * j + 3], lam[:, 4 * j:4 * j + 1],
                                                     lam[:, 4 * j + 1:4 * j + 2], lambda_init(3 * j),
                                                     ALU.subtract, ALU.add))
                    ada_take(dve, 0, 0)
                    with dve.Fori(1, ADA_STEPS) as it:
                        ada_take(dve, 0, it)
                    ada_scale(dve, 0)
                    link.close()

        UP_STEPS, DOWN_STEPS = FF // SLAB // SLOTS, D // SLAB

        def mlp_phases(layer):
            w2 = I["mlp_w2"][layer].rearrange("(g k p) n -> g p k n", g=SLOTS, p=P)
            phase(f"up{layer}", [2] * (FF // SLAB), lambda u: cols(I["mlp_w1"][layer], u * SLAB))
            phase(f"down{layer}", [2] * (SLOTS * DOWN_STEPS),
                  lambda u: w2[u % SLOTS, :, :, (u // SLOTS) * SLAB:(u // SLOTS + 1) * SLAB])

        def mlp(layer, following):
            carve = Carve()
            hid = carve(FT, TOK)
            more = layer + 1 < DEPTH
            up, down = phases[f"up{layer}"][0], phases[f"down{layer}"][0]
            w2 = I["mlp_w2"][layer].rearrange("(g k p) n -> g p k n", g=SLOTS, p=P)
            runs = run_after[up - 1]
            runs_down = run_after[down - 1]
            taken, hid_base = base("acc_taken"), base("hid_ready")

            def tile(n):
                return flat(hid[:, bass.ds(n, 1), :])

            with nc.Block() as block:
                @block.sync
                def _(sp):
                    if more:
                        ada_load(sp, layer + 1, 0)
                    with sp.Fori(1, UP_STEPS) as i:
                        for s in range(SLOTS):
                            sp.wait_ge(run_done, runs + (i - 1) * 2 * SLOTS + 2 * (s + 1))
                            alone(sp)
                            sp.dma_start(slab[:, (up + s) % SLOTS], cols(I["mlp_w1"][layer], (i * SLOTS + s) * SLAB))\
                                .then_inc(slab_ready[(up + s) % SLOTS], 16)
                        if more:
                            ada_load(sp, layer + 1, i)
                    for s in range(SLOTS):
                        load_unit(sp, f"down{layer}", s)
                    if more:
                        ada_load(sp, layer + 1, UP_STEPS)
                    with sp.Fori(1, DOWN_STEPS) as i:
                        for s in range(SLOTS):
                            sp.wait_ge(run_done, runs_down + (i - 1) * 2 * SLOTS + 2 * (s + 1))
                            alone(sp)
                            sp.dma_start(slab[:, (down + s) % SLOTS], w2[s][:, :, bass.ds(i * SLAB, SLAB)])\
                                .then_inc(slab_ready[(down + s) % SLOTS], 16)
                        if more:
                            ada_load(sp, layer + 1, i + UP_STEPS)
                    load_first(sp, following)

                @block.tensor
                def _(pe):
                    norm_pe(pe)
                    for k in range(KT):
                        has_h(pe, k)
                    with pe.Fori(0, UP_STEPS) as i:
                        for s in range(SLOTS):
                            has_slab(pe, up + s, i)
                            for j in range(2):
                                pe.wait_ge(acc_taken, taken - 1 + i * 2 * SLOTS + (2 * s + j))
                                for k in range(KT):
                                    mm = nc.tensor.matmul(bank(j, TOK), slab[:, (up + s) % SLOTS, k, j * P:(j + 1) * P],
                                                          hT[:, k], start=k == 0, stop=k == KT - 1)
                                mm.then_inc(run_done, 1)
                            if more and s < ADA_SLOTS:
                                ada_products(pe, layer + 1, i, s)
                    with pe.Fori(0, DOWN_STEPS) as i:
                        for s in range(SLOTS):
                            has_slab(pe, down + s, i)
                            pe.wait_ge(sem("hid_ready"), hid_base + KT * (s + 1))
                            for j in range(2):
                                if s == 0:
                                    pe.wait_ge(acc_taken, taken + FT - 1 + i * 2 + j)
                                for k in range(KT):
                                    mm = nc.tensor.matmul(bank(j, TOK), slab[:, (down + s) % SLOTS, k, j * P:(j + 1) * P],
                                                          hid[:, s * KT + k], start=s == 0 and k == 0,
                                                          stop=s == SLOTS - 1 and k == KT - 1)
                                mm.then_inc(run_done, 1)
                            if more and s < ADA_SLOTS:
                                ada_products(pe, layer + 1, i + UP_STEPS, s)

                @block.scalar
                def _(act):
                    norm_act(act, layer, 1, in_place)
                    with act.Fori(0, UP_STEPS) as i:
                        for n in range(2 * SLOTS):
                            act.wait_ge(run_done, runs + i * 2 * SLOTS + (n + 1))
                            nc.scalar.activation(tile(i * 2 * SLOTS + n), bank(n % 2, TOK), ACT.Relu)\
                                .then_inc(acc_taken, 1)

                @block.gpsimd
                def _(pool):
                    with pool.Fori(0, UP_STEPS) as i:
                        for n in range(2 * SLOTS):
                            h = tile(i * 2 * SLOTS + n)
                            pool.wait_ge(acc_taken, taken + i * 2 * SLOTS + (n + 1))
                            nc.gpsimd.tensor_tensor(h, h, h, ALU.mult).then_inc(sem("hid_ready"), 1)

                @block.vector
                def _(dve):
                    link = Link(dve, "dve_step")
                    norm_dve(dve, link)
                    link.close()
                    if more:
                        with dve.Fori(0, UP_STEPS) as i:
                            ada_take(dve, layer + 1, i)
                    with dve.Fori(0, DOWN_STEPS) as i:
                        for j in range(2):
                            dve.wait_ge(run_done, runs_down + i * 2 * SLOTS + 2 * SLOTS - 1 + j)
                            residual(layer, 1, i * 2 + j, bank(j, TOK)).then_inc(acc_taken, 1)
                        if more:
                            ada_take(dve, layer + 1, i + UP_STEPS)
                    if more:
                        ada_scale(dve, layer + 1)
            norm_counts()
            add(acc_taken=FT + KT, hid_ready=FT)

        def wo_phase(name, w):
            phase(name, [2] * (D // SLAB), lambda u: cols(w, u * SLAB))

        def wo_pe(pe, name, src, ready):
            start, n, _ = phases[name]
            for u in range(n):
                has_slab(pe, start + u)
                for j in range(2):
                    g = 2 * u + j
                    start_at(pe, "acc_taken", base("acc_taken") + g - 1)
                    for k in range(KT):
                        if g == 0:
                            ready(k)
                        mm = nc.tensor.matmul(bank(j, TOK), slab[:, (start + u) % SLOTS, k, j * P:(j + 1) * P],
                                              src[:, k], start=k == 0, stop=k == KT - 1)
                    mm.then_inc(run_done, 1)

        def wo_dve(dve, name, layer):
            runs = run_after[phases[name][0] - 1]
            for g in range(KT):
                dve.wait_ge(run_done, runs + g + 1)
                residual(layer, 0, g, bank(g % 2, TOK)).then_inc(acc_taken, 1)

        def qk_pe(pe, start, n_tiles, dst, ws):
            for n in range(n_tiles + 2):
                if n < n_tiles:
                    if n % 2 == 0:
                        has_slab(pe, start + n // 2)
                    start_at(pe, "acc_taken", base("acc_taken") + n - 1)
                    for k in range(KT):
                        if n == 0:
                            has_h(pe, k)
                        at = (n % 2) * P
                        mm = nc.tensor.matmul(bank(n % 2, TOK), slab[:, (start + n // 2) % SLOTS, k, at:at + P],
                                              hT[:, k], start=k == 0, stop=k == KT - 1)
                    mm.then_inc(run_done, 1)
                if 1 <= n <= n_tiles:
                    m = n - 1
                    pe.wait_ge(sem("head_sq"), base("head_sq") + m + 1)
                    start_at(pe, "head_std", base("head_sq") + m - 1)
                    nc.tensor.matmul(bank(2 + m % 2, TOK), K["blocks"], ws["sq"][:, m % 2], start=True, stop=True)\
                        .then_inc(sem("head_sum"), 1)
                if n >= 2:
                    m = n - 2
                    pe.wait_ge(sem("head_norm"), base("head_sq") + m + 1)
                    start_at(pe, "partner_taken", base("head_sq") + m - 1)
                    nc.tensor.matmul(bank(4 + m % 2, LAT), K["swap32"], dst(m)[:, CTX:TOK], start=True, stop=True)\
                        .then_inc(sem("partner"), 1)

        def qk_act(act, start, n_tiles, ws):
            runs, hb = run_after[start - 1] if start else 0, base("head_sq")
            for n in range(n_tiles + 1):
                if n < n_tiles:
                    act.wait_ge(run_done, runs + n + 1)
                    start_at(act, "head_norm", hb + n - 1)
                    nc.scalar.activation(ws["raw"][:, n % 2], bank(n % 2, TOK), ACT.Copy).then_inc(acc_taken, 1)
                    start_at(act, "head_sum", hb + n - 1)
                    act.wait_ge(acc_taken, base("acc_taken") + n + 1)
                    nc.scalar.activation(ws["sq"][:, n % 2], ws["raw"][:, n % 2], ACT.Square)\
                        .then_inc(sem("head_sq"), 1)
                if n >= 1:
                    m = n - 1
                    act.wait_ge(sem("head_sum"), hb + m + 1)
                    start_at(act, "head_norm", hb + m - 1)
                    nc.scalar.activation(ws["rinv"][:, m % 2], bank(2 + m % 2, TOK), ACT.Sqrt, scale=1.0 / HD,
                                         bias=K["eps"]).then_inc(sem("head_std"), 1)

        def qk_dve(dve, link, n_tiles, dst, gain, ws):
            hb = base("head_sq")
            for n in range(n_tiles + 1):
                if n < n_tiles:
                    dve.wait_ge(sem("head_std"), hb + n + 1)
                    link(nc.vector.reciprocal(ws["rinv"][:, n % 2], ws["rinv"][:, n % 2]))
                    nc.vector.scalar_tensor_tensor(dst(n), ws["raw"][:, n % 2], gain(n), ws["rinv"][:, n % 2],
                                                   ALU.mult, ALU.mult).then_inc(sem("head_norm"), 1)
                if n >= 1:
                    m = n - 1
                    x = dst(m)[:, CTX:TOK]
                    dve.wait_ge(sem("partner"), hb + m + 1)
                    nc.vector.tensor_tensor(ws["turn"][:, m % 2], bank(4 + m % 2, LAT), K["sin"], ALU.mult)\
                        .then_inc(sem("partner_taken"), 1)
                    link(nc.vector.tensor_tensor(x, x, K["cos"], ALU.mult))
                    link(nc.vector.tensor_tensor(x, x, ws["turn"][:, m % 2], ALU.add))

        def v_pe(pe, start, units, g):
            for u in units:
                has_slab(pe, start + u)
                for t in range(TT):
                    start_at(pe, "acc_taken", base("acc_taken") + g - 1)
                    for k in range(KT):
                        mm = nc.tensor.matmul(bank(g % 2, SLAB), hT[:, k, t * P:(t + 1) * P],
                                              slab[:, (start + u) % SLOTS, k], start=k == 0, stop=k == KT - 1)
                    mm.then_inc(run_done, 1)
                    g += 1

        def v_act(act, start, units, g, v):
            runs = run_after[start - 1] if start else 0
            for i, u in enumerate(units):
                for t in range(TT):
                    act.wait_ge(run_done, runs + g + 1)
                    nc.scalar.activation(v[:, t, i * SLAB:(i + 1) * SLAB], bank(g % 2, SLAB), ACT.Copy)\
                        .then_inc(acc_taken, 1)
                    g += 1

        def turn_keys_pe(pe, kc, k, n, before):
            pe.wait_ge(sem("cache_in"), cache_loads[0])
            pe.wait_ge(sem("sum_done"), base("sum_done") + 1)
            pe.wait_ge(sem("std_ready"), base("sum_done") + 1)
            pe.wait_ge(sem("head_std"), base("head_sq") + before)
            for src, b0 in ((lambda c: kc[:, c * P:(c + 1) * P], 6), (lambda c: k[:, c, 0:CTX], 2)):
                for c in range(n):
                    mm = nc.tensor.transpose(bank(b0 + c // 4, 4, P)[:, c % 4], src(c), K["ident"])
                mm.then_inc(sem("keys_turned"), 1)

        cache_loads = [0]

        def turn_keys_act(act, k, kout, n):
            b = base("keys_turned")
            for i in range(2):
                act.wait_ge(sem("keys_turned"), b + i + 1)
                for q in range(0, n, 4):
                    m = min(4, n - q)
                    src = bank((6, 2)[i] + q // 4, m, P)
                    dst = k[:, q:q + m, TOK:TOK + PAST] if i == 0 else \
                        kout[:, q * P:(q + m) * P].rearrange("p (c t) -> p c t", c=m)
                    ins = nc.scalar.activation(dst, src, ACT.Copy)
            ins.then_inc(sem("kout_ready"), 1)

        def da_phases(layer):
            j = layer // 3
            phase(f"qkv{layer}", [2] * 8 + [3] * 4, lambda u: cols(I["da_wqkv"][j], u * SLAB))
            wo_phase(f"wo{layer}", I["da_wo"][j])

        def da(layer, following):
            j = layer // 3
            c = Carve()
            q, k, v, o = c(KT, TOK), c(KT, TOK + PAST), c(TT + 1, D), c(KT, TOK)
            ws = {"raw": c(2, TOK), "sq": c(2, TOK), "rinv": c(2, TOK), "turn": c(2, LAT)}
            kc, kout = c(D), c(D)
            probs, pr, prT = c(2, 2, TOK), c(2, TOK), c(2, TOK)
            neg, total, inv = c(2, 4), c(2, 2), c(2, 2)
            name = f"qkv{layer}"
            start = phases[name][0]
            n_tiles, v_units = 2 * KT, range(8, 12)
            cache_loads[0] += 32

            def dst(n):
                return q[:, n] if n < KT else k[:, n - KT, 0:TOK]

            def gain(n):
                at = 2 * j + n // KT
                return small[:, at:at + 1]

            with nc.Block() as block:
                @block.sync
                def _(sp):
                    load_phase(sp, name, f"wo{layer}")
                    sp.wait_ge(sem("kout_ready"), base("kout_ready") + 1)
                    sp.dma_start(O["new_da_k"][0, j].rearrange("t h d -> t (h d)"), kout).then_inc(sem("kv_stored"), 16)
                    sp.dma_start(O["new_da_v"][0, j].rearrange("t h d -> t (h d)"), v[:, 0])\
                        .then_inc(sem("kv_stored"), 16)

                @block.tensor
                def _(pe):
                    norm_pe(pe)
                    qk_pe(pe, start, n_tiles, dst, ws)
                    v_pe(pe, start, v_units, n_tiles)
                    turn_keys_pe(pe, kc, k, KT, n_tiles)

                @block.scalar
                def _(act):
                    act.dma_start(kc, I["cache_da_k"][0, j].rearrange("t h d -> t (h d)")).then_inc(sem("cache_in"), 16)
                    act.dma_start(v[:, TT], I["cache_da_v"][0, j].rearrange("t h d -> t (h d)"))\
                        .then_inc(sem("cache_in"), 16)
                    norm_act(act, layer, 0, in_place)
                    qk_act(act, start, n_tiles, ws)
                    v_act(act, start, v_units, n_tiles, v)
                    turn_keys_act(act, k, kout, KT)

                @block.vector
                def _(dve):
                    link = Link(dve, "dve_step")
                    norm_dve(dve, link)
                    qk_dve(dve, link, n_tiles, dst, gain, ws)
                    link.close()
            norm_counts()
            add(acc_taken=n_tiles + TT * 4, head_sq=n_tiles, keys_turned=2, kout_ready=1, kv_stored=32)

            units = [(h, t) for h in range(KT) for t in range(TT)]
            N = len(units)
            ub, eb = base("unit"), base("exp_done")

            def keys(t):
                return (slice(0, CTX), (0,)) if t == 0 else (slice(CTX, TOK + PAST), (1, 2, 3))

            with nc.Block() as block:
                @block.tensor
                def _(pe):
                    for i in range(N + 2):
                        if i < N:
                            h, t = units[i]
                            ks, vb = keys(t)
                            start_at(pe, "exp_done", eb + 2 * (i - 1))
                            for m in range(2):
                                r = slice(HD * m, HD * m + HD)
                                mm = nc.tensor.matmul(bank(2 * (i % 2) + m, P * len(vb)), q[r, h, t * P:(t + 1) * P],
                                                      k[r, h, ks], start=True, stop=True)
                            mm.then_inc(sem("scores"), 1)
                        if 1 <= i <= N:
                            u = i - 1
                            _, vb = keys(units[u][1])
                            pe.wait_ge(sem("pr_ready"), ub + u + 1)
                            start_at(pe, "prT_ready", ub + u - 1)
                            for b in range(len(vb)):
                                mm = nc.tensor.transpose(bank(4 + u % 2, TT, P)[:, b], pr[:, u % 2, b * P:(b + 1) * P],
                                                         K["ident"])
                            mm.then_inc(sem("pr_turned"), 1)
                        if i >= 2:
                            u = i - 2
                            h, t = units[u]
                            _, vb = keys(t)
                            pe.wait_ge(sem("prT_ready"), ub + u + 1)
                            if t == 0:
                                start_at(pe, "o_ready", ub // TT + h - 1)
                            for b, w in enumerate(vb):
                                mm = nc.tensor.matmul(bank(6 + h % 2, TOK)[:, t * P:(t + 1) * P],
                                                      v[:, w if w else 0, h * P:(h + 1) * P],
                                                      prT[:, u % 2, b * P:(b + 1) * P], start=b == 0, stop=b == len(vb) - 1)
                            mm.then_inc(sem("pv_done"), 1)

                @block.vector
                def _(dve):
                    link = Link(dve, "dve_step")
                    for i in range(N + 1):
                        if i < N:
                            n = P * len(keys(units[i][1])[1])
                            dve.wait_ge(sem("scores"), ub + i + 1)
                            for m in range(2):
                                ins = nc.vector.tensor_reduce(neg[:, i % 2, m:m + 1], bank(2 * (i % 2) + m, n), AX_X,
                                                              ALU.max, negate=True)
                            link(ins)
                            nc.vector.tensor_scalar(neg[:, i % 2, 2:4], neg[:, i % 2, 0:2], SCALE, None, ALU.mult)\
                                .then_inc(sem("max_ready"), 1)
                        if i >= 1:
                            u = i - 1
                            n = P * len(keys(units[u][1])[1])
                            dve.wait_ge(sem("exp_done"), eb + 2 * (u + 1))
                            link(nc.vector.reciprocal(inv[:, u % 2], total[:, u % 2]))
                            link(nc.vector.tensor_scalar(inv[:, u % 2, 1:2], inv[:, u % 2, 1:2],
                                                         lam[:, 4 * j + 2:4 * j + 3], None, ALU.mult))
                            p0, p1 = (probs[:, u % 2, m, 0:n] for m in range(2))
                            link(nc.vector.tensor_scalar(p1, p1, inv[:, u % 2, 1:2], None, ALU.mult))
                            start_at(dve, "pr_turned", ub + u - 1)
                            nc.vector.scalar_tensor_tensor(pr[:, u % 2, 0:n], p0, inv[:, u % 2, 0:1], p1, ALU.mult,
                                                           ALU.subtract).then_inc(sem("pr_ready"), 1)
                    link.close()

                @block.scalar
                def _(act):
                    for i in range(N + 2):
                        if i < N:
                            n = P * len(keys(units[i][1])[1])
                            act.wait_ge(sem("max_ready"), ub + i + 1)
                            start_at(act, "pr_ready", ub + i - 1)
                            for m in range(2):
                                nc.scalar.activation(probs[:, i % 2, m, 0:n], bank(2 * (i % 2) + m, n), ACT.Exp,
                                                     scale=SCALE, bias=neg[:, i % 2, 2 + m:3 + m],
                                                     accum_out=total[:, i % 2, m:m + 1]).then_inc(sem("exp_done"), 1)
                        if 1 <= i <= N:
                            u = i - 1
                            n = P * len(keys(units[u][1])[1])
                            act.wait_ge(sem("pr_turned"), ub + u + 1)
                            start_at(act, "pv_done", ub + u - 1)
                            nc.scalar.activation(prT[:, u % 2, 0:n], bank(4 + u % 2, n), ACT.Copy)\
                                .then_inc(sem("prT_ready"), 1)
                        if i >= 2 and units[i - 2][1] == TT - 1:
                            h = units[i - 2][0]
                            act.wait_ge(sem("pv_done"), ub + i - 1)
                            nc.scalar.activation(o[:, h], bank(6 + h % 2, TOK), ACT.Copy).then_inc(sem("o_ready"), 1)
            add(unit=N, exp_done=2 * N)

            sb_ = base("o_sq")
            with nc.Block() as block:
                @block.sync
                def _(sp):
                    load_phase(sp, f"wo{layer}", following)

                @block.tensor
                def _(pe):
                    for h in range(KT):
                        pe.wait_ge(sem("o_sq"), sb_ + h + 1)
                        start_at(pe, "o_std", sb_ + h - 1)
                        nc.tensor.matmul(bank(2 + h % 2, TOK), K["ones"], hT[:, h], start=True, stop=True)\
                            .then_inc(sem("o_sum"), 1)
                    wo_pe(pe, f"wo{layer}", o, lambda k: pe.wait_ge(sem("o_norm"), sb_ + k + 1))

                @block.scalar
                def _(act):
                    for h in range(KT):
                        nc.scalar.activation(hT[:, h], o[:, h], ACT.Square).then_inc(sem("o_sq"), 1)
                    for h in range(KT):
                        act.wait_ge(sem("o_sum"), sb_ + h + 1)
                        start_at(act, "o_norm", sb_ + h - 1)
                        nc.scalar.activation(ws["rinv"][:, h % 2], bank(2 + h % 2, TOK), ACT.Sqrt, scale=1.0 / P,
                                             bias=K["eps"]).then_inc(sem("o_std"), 1)

                @block.vector
                def _(dve):
                    link = Link(dve, "dve_step")
                    for h in range(KT):
                        dve.wait_ge(sem("o_std"), sb_ + h + 1)
                        link(nc.vector.reciprocal(ws["rinv"][:, h % 2], ws["rinv"][:, h % 2]))
                        nc.vector.scalar_tensor_tensor(o[:, h], o[:, h], small[:, 6 + j:7 + j], ws["rinv"][:, h % 2],
                                                       ALU.mult, ALU.mult).then_inc(sem("o_norm"), 1)
                    link.close()
                    wo_dve(dve, f"wo{layer}", layer)
            add(o_sq=KT, acc_taken=KT)
            stored["kv_stored"] = base("kv_stored")

        def swa_phases(layer):
            phase(f"qkv{layer}", [2] * 5 + [3], lambda u: cols(I["swa_wqkv"][0], u * SLAB))
            wo_phase(f"wo{layer}", I["swa_wo"][0])

        def swa(layer, following):
            c = Carve()
            KV = SLAB
            q, k, k2, v, o = c(KT, TOK), c(2, TOK + PAST), c(2, TOK + PAST), c(TT + 1, KV), c(KT, TOK)
            ws = {"raw": c(2, TOK), "sq": c(2, TOK), "rinv": c(2, TOK), "turn": c(2, LAT)}
            kc, kout = c(KV), c(KV)
            probs, prT = c(2, 2, TOK), c(2, 2, TOK)
            sink, nsink = c(16), c(16)
            neg, total, inv = c(2, 6), c(2, 4), c(2, 2)
            name = f"qkv{layer}"
            start = phases[name][0]
            n_tiles, v_units = KT + 2, (5,)
            cache_loads[0] += 48

            def dst(n):
                return q[:, n] if n < KT else k[:, n - KT, 0:TOK]

            def gain(n):
                at = 4 + n // KT
                return small[:, at:at + 1]

            with nc.Block() as block:
                @block.sync
                def _(sp):
                    load_phase(sp, name, f"wo{layer}")
                    sp.wait_ge(sem("kout_ready"), base("kout_ready") + 1)
                    sp.dma_start(O["new_swa_k"][0, 0].rearrange("t h d -> t (h d)"), kout)\
                        .then_inc(sem("kv_stored"), 16)
                    sp.dma_start(O["new_swa_v"][0, 0].rearrange("t h d -> t (h d)"), v[:, 0])\
                        .then_inc(sem("kv_stored"), 16)

                @block.tensor
                def _(pe):
                    norm_pe(pe)
                    qk_pe(pe, start, n_tiles, dst, ws)
                    v_pe(pe, start, v_units, n_tiles)
                    turn_keys_pe(pe, kc, k, 2, n_tiles)
                    pe.wait_ge(sem("kout_ready"), base("kout_ready") + 1)
                    pe.wait_ge(sem("keys_roped"), 1)
                    for i in range(2):
                        nc.tensor.matmul(bank(2 + i, TOK + PAST), K["swap64"], k[:, i], start=True, stop=True)\
                            .then_inc(sem("keys_swapped"), 1)

                @block.scalar
                def _(act):
                    act.dma_start(kc, I["cache_swa_k"][0, 0].rearrange("t h d -> t (h d)")).then_inc(sem("cache_in"), 16)
                    act.dma_start(v[:, TT], I["cache_swa_v"][0, 0].rearrange("t h d -> t (h d)"))\
                        .then_inc(sem("cache_in"), 16)
                    act.dma_start(sink, I["swa_sink"][0:1].to_broadcast([P, 16])).then_inc(sem("cache_in"), 16)
                    norm_act(act, layer, 0, in_place)
                    qk_act(act, start, n_tiles, ws)
                    v_act(act, start, v_units, n_tiles, v)
                    turn_keys_act(act, k, kout, 2)
                    for i in range(2):
                        act.wait_ge(sem("keys_swapped"), i + 1)
                        nc.scalar.activation(k2[:, i], bank(2 + i, TOK + PAST), ACT.Copy)

                @block.vector
                def _(dve):
                    link = Link(dve, "dve_step")
                    norm_dve(dve, link)
                    qk_dve(dve, link, n_tiles, dst, gain, ws)
                    link.close()
                    dve.wait_ge(sem("cache_in"), cache_loads[0])
                    nc.vector.tensor_scalar(nsink, sink, -1.0, None, ALU.mult).then_inc(sem("keys_roped"), 1)
            norm_counts()
            add(acc_taken=n_tiles + TT, head_sq=n_tiles, keys_turned=2, kout_ready=1, kv_stored=32)

            units = [(h, t) for h in range(KT) for t in range(TT)]
            N = len(units)
            ub, eb = base("unit"), base("exp_done")

            def keys(t):
                return (slice(0, CTX), (0,)) if t == 0 else (slice(CTX, TOK + PAST), (1, 2, 3))

            with nc.Block() as block:
                @block.tensor
                def _(pe):
                    for i in range(N + 2):
                        if i < N:
                            h, t = units[i]
                            ks, vb = keys(t)
                            g = h // 2
                            start_at(pe, "max_ready", ub + i - 1)
                            for m in range(2):
                                r = slice(HD * m, HD * m + HD)
                                keys_at = (k if g % 2 == m else k2)[r, g // 2, ks]
                                mm = nc.tensor.matmul(bank(2 * (i % 2) + m, P * len(vb)), q[r, h, t * P:(t + 1) * P],
                                                      keys_at, start=True, stop=True)
                            mm.then_inc(sem("scores"), 1)
                        if 1 <= i <= N:
                            u = i - 1
                            _, vb = keys(units[u][1])
                            pe.wait_ge(sem("pr_ready"), ub + u + 1)
                            start_at(pe, "prT_ready", ub + u)
                            for m in range(2):
                                for b in range(len(vb)):
                                    mm = nc.tensor.transpose(bank(4 + m, TT, P)[:, b],
                                                             probs[:, u % 2, m, b * P:(b + 1) * P], K["ident"])
                            mm.then_inc(sem("pr_turned"), 1)
                        if i >= 2:
                            u = i - 2
                            h, t = units[u]
                            _, vb = keys(t)
                            g = h // 2
                            pe.wait_ge(sem("prT_ready"), ub + u + 1)
                            if t == 0:
                                start_at(pe, "o_ready", ub // TT + h - 1)
                            for m in range(2):
                                for b, w in enumerate(vb):
                                    mm = nc.tensor.matmul(psum[HD * m:HD * m + HD, 6 + h % 2, t * P:(t + 1) * P],
                                                          v[:, w, g * HD:(g + 1) * HD],
                                                          prT[:, u % 2, m, b * P:(b + 1) * P],
                                                          start=b == 0, stop=b == len(vb) - 1)
                            mm.then_inc(sem("pv_done"), 1)

                @block.vector
                def _(dve):
                    link = Link(dve, "dve_step")
                    for i in range(N + 1):
                        if i < N:
                            h, t = units[i]
                            n = P * len(keys(t)[1])
                            x = neg[:, i % 2]
                            dve.wait_ge(sem("scores"), ub + i + 1)
                            start_at(dve, "pr_turned", ub + i - 1)
                            for m in range(2):
                                s = bank(2 * (i % 2) + m, n)
                                if t == 0:
                                    ins = nc.vector.tensor_scalar(probs[:, i % 2, m, 0:n], s, SCALE, None, ALU.mult)
                                else:
                                    ins = nc.vector.scalar_tensor_tensor(probs[:, i % 2, m], s, SCALE, band[:, t - 1],
                                                                         ALU.mult, ALU.add)
                            link(ins)
                            link(nc.vector.tensor_reduce(x[:, 0:2], probs[:, i % 2, :, 0:n], AX_X, ALU.max, negate=True))
                            link(nc.vector.tensor_tensor(x[:, 2:4], x[:, 0:2], nsink[:, 2 * h:2 * h + 2], ALU.min))
                            nc.vector.tensor_tensor(x[:, 4:6], x[:, 2:4], sink[:, 2 * h:2 * h + 2], ALU.add)\
                                .then_inc(sem("max_ready"), 1)
                        if i >= 1:
                            u = i - 1
                            n = P * len(keys(units[u][1])[1])
                            dve.wait_ge(sem("exp_done"), eb + 3 * (u + 1))
                            link(nc.vector.tensor_tensor(total[:, u % 2, 0:2], total[:, u % 2, 0:2],
                                                         total[:, u % 2, 2:4], ALU.add))
                            link(nc.vector.reciprocal(inv[:, u % 2], total[:, u % 2, 0:2]))
                            for m in range(2):
                                p = probs[:, u % 2, m, 0:n]
                                ins = nc.vector.tensor_scalar(p, p, inv[:, u % 2, m:m + 1], None, ALU.mult)
                            ins.then_inc(sem("pr_ready"), 1)
                    link.close()

                @block.scalar
                def _(act):
                    for i in range(N + 2):
                        if i < N:
                            n = P * len(keys(units[i][1])[1])
                            x = neg[:, i % 2]
                            act.wait_ge(sem("max_ready"), ub + i + 1)
                            start_at(act, "pr_ready", ub + i - 1)
                            for m in range(2):
                                p = probs[:, i % 2, m, 0:n]
                                nc.scalar.activation(p, p, ACT.Exp, bias=x[:, 2 + m:3 + m],
                                                     accum_out=total[:, i % 2, m:m + 1]).then_inc(sem("exp_done"), 1)
                            nc.scalar.activation(total[:, i % 2, 2:4], x[:, 4:6], ACT.Exp).then_inc(sem("exp_done"), 1)
                        if 1 <= i <= N:
                            u = i - 1
                            n = P * len(keys(units[u][1])[1])
                            act.wait_ge(sem("pr_turned"), ub + u + 1)
                            start_at(act, "pv_done", ub + u - 1)
                            nc.scalar.activation(prT[:, u % 2, :, 0:n], psum[:, 4:6, 0:n], ACT.Copy)\
                                .then_inc(sem("prT_ready"), 1)
                        if i >= 2 and units[i - 2][1] == TT - 1:
                            h = units[i - 2][0]
                            act.wait_ge(sem("pv_done"), ub + i - 1)
                            nc.scalar.activation(o[:, h], bank(6 + h % 2, TOK), ACT.Copy).then_inc(sem("o_ready"), 1)
            add(unit=N, exp_done=3 * N)

            with nc.Block() as block:
                @block.sync
                def _(sp):
                    load_phase(sp, f"wo{layer}", following)

                @block.tensor
                def _(pe):
                    wo_pe(pe, f"wo{layer}", o, lambda k: None)

                @block.vector
                def _(dve):
                    wo_dve(dve, f"wo{layer}", layer)
            add(acc_taken=KT)
            stored["kv_stored"] = base("kv_stored")

        V_MU, V_W0, V_A0, V_KK, V_KA, V_RK, V_LNW, V_LNB, V_1KA = 0, 6, 8, 10, 11, 12, 13, 14, 15

        def flat3(ap):
            return ap.rearrange("a v k -> (a v) k")

        S_NEW = {(z, s): 2 * s + z + 1 for z in range(2) for s in range(3)}
        DSTEPS, PSTEPS = 17, 5

        def step_loads(sp, j, stage_in):
            if j == 0:
                sp.wait_ge(run_done, run_after[phases["wo1"][0] - 1])
                sp.wait_ge(sem("stage_zero"), 1)
            else:
                sp.wait_ge(sem("proj"), j * 8)
                sp.wait_ge(sem("s0_turned"), j * 2)
            for i, w in enumerate((I["rwkv_w2"][0].rearrange("z r d -> (z r) d"),
                                   I["rwkv_a2"][0].rearrange("z r d -> (z r) d"), I["rwkv_g2"][0])):
                sp.dma_start(slab[:, 3, i, 0:P], w[:, bass.ds(j * P, P)]).then_inc(sem("l_in"), 16)
            for m in (1, 0, 2):
                sp.dma_start(slab[:, m, :, 0:P],
                             I["rwkv_wrkv"][0, m].rearrange("(k p) n -> p k n", p=P)[:, :, bass.ds(j * P, P)])\
                    .then_inc(sem("w_in"), 16)
            for z in range(2):
                for hh in range(2):
                    r = slice(64 * hh, 64 * hh + 64)
                    sp.dma_start(stage_in[r, z, r], flat3(I["state_rwkv"][0, 0, z, bass.ds(j * 2 + hh, 1)]))\
                        .then_inc(sem("state_in"), 16)

        def rwkv_phases(layer):
            wo_phase(f"wo{layer}", I["rwkv_wo"][0])

        def rwkv(layer, following):
            c = Carve()
            xs = c(3, KT, TOK)
            mids = c(3, TOK)
            stage_in, stage_out, S = c(2, P), c(2, P), c(2, 2, P)
            shared = c.at
            PAD = TOK + 4
            hP, mixed, delta, w_mid = c(KT, PAD), c(2, 3, TOK), c(2, TOK), c(3, KT, P)
            PADS = (0, CTX + 2)

            with nc.Block() as block:
                @block.gpsimd
                def _(pool):
                    for at in (0, CTX + 1, CTX + 2, PAD - 1):
                        ins = nc.gpsimd.memset(hP[:, :, at:at + 1], 0.0)
                    ins.then_inc(sem("pads_zero"), 1)
                    nc.gpsimd.memset(stage_in, 0.0).then_inc(sem("stage_zero"), 1)
                    nc.gpsimd.memset(S, 0.0)

                @block.scalar
                def _(act):
                    for i, w in enumerate((I["rwkv_w1"][0], I["rwkv_a1"][0])):
                        for z in range(2):
                            act.dma_start(w_mid[:, i, :, 64 * z:64 * z + 64], w[z].rearrange("(k p) r -> p k r", p=P))\
                                .then_inc(sem("w_mid_in"), 16)
                    act.dma_start(w_mid[:, 2], I["rwkv_g1"][0].rearrange("(k p) r -> p k r", p=P))\
                        .then_inc(sem("w_mid_in"), 16)
                    norm_act(act, layer, 0, lambda k, g: hP[:, k, PADS[g] + 1:PADS[g] + 1 + (CTX, LAT)[g]])
                    act.wait_ge(sem("mids_done"), 1)
                    for i, f in enumerate((ACT.Tanh, ACT.Copy, ACT.Sigmoid)):
                        ins = nc.scalar.activation(mids[:, i], bank(2 + i, TOK), f)
                    ins.then_inc(sem("tile_done"), 1)

                @block.vector
                def _(dve):
                    link = Link(dve, "dve_step")
                    norm_dve(dve, link)
                    dve.wait_ge(sem("pads_zero"), 1)
                    for k in range(KT):
                        dve.wait_ge(sem("h_ready"), base("sq_ready") + k + 1)
                        d = delta[:, k % 2]
                        for g, t in GROUPS:
                            n = t.stop - t.start
                            ins = nc.vector.tensor_tensor(d[:, t], hP[:, k, PADS[g]:PADS[g] + n],
                                                          hP[:, k, PADS[g] + 2:PADS[g] + 2 + n], ALU.add)
                        link(ins)
                        for g, t in GROUPS:
                            n = t.stop - t.start
                            ins = nc.vector.scalar_tensor_tensor(d[:, t], d[:, t], 0.5, hP[:, k, PADS[g] + 1:PADS[g] + 1 + n],
                                                                 ALU.mult, ALU.subtract)
                        link(ins)
                        if k >= 2:
                            dve.wait_ge(sem("mix_used"), k - 1)
                        for m in (3, 4, 5, 0, 1, 2):
                            dst = xs[:, m, k] if m < 3 else mixed[:, k % 2, m - 3]
                            for g, t in GROUPS:
                                n = t.stop - t.start
                                ins = nc.vector.scalar_tensor_tensor(
                                    dst[:, t], d[:, t], vecs[:, (V_MU + m) * KT + k:(V_MU + m) * KT + k + 1],
                                    hP[:, k, PADS[g] + 1:PADS[g] + 1 + n], ALU.mult, ALU.add)
                            if m == 5:
                                ins.then_inc(sem("mix_ready"), 1)
                    link.close()

                @block.tensor
                def _(pe):
                    norm_pe(pe)
                    pe.wait_ge(sem("w_mid_in"), 80)
                    for k in range(KT):
                        pe.wait_ge(sem("mix_ready"), k + 1)
                        for i in range(3):
                            mm = nc.tensor.matmul(bank(2 + i, TOK), w_mid[:, i, k], mixed[:, k % 2, i],
                                                  start=k == 0, stop=k == KT - 1)
                        mm.then_inc(sem("mix_used" if k < KT - 1 else "mids_done"), 1)

                @block.sync
                def _(sp):
                    step_loads(sp, 0, stage_in)
            norm_counts()

            c.at = shared
            spare = Carve(ada_slab[:, :, :, :].rearrange("p s k n -> p (s k n)"))
            rT, kT, vtok, vT, gT, kn, bonus = c(TOK), c(TOK), c(TT, P), c(TOK), c(TOK), c(TOK), c(TOK)
            par = c(16)
            sq, inv, yT, tmp = c(TOK), c(TOK), c(TOK), c(TOK)
            decay, rate, kd = c(2, TOK), c(2, TOK), c(2, TOK)
            cum = c(2, TOK)
            pp, pi = c(2, NCH, CH + 1), c(2, TOK)
            AR, bT, kTil = c(2, NCH, 2, CH), c(2, TOK), c(2, TOK)
            LB, MC = spare(2, 6, 2 * CH), spare(2, 6, 2 * CH)
            T, TTr, X = c(2, 6, CH), c(2, 6, CH), c(2, 6, CH)
            LM = spare(2, 2, 6, CH)
            tok = spare(2, 2, TT, P)
            R, U = c(2, 2 * P), c(2, 2 * P)
            fresh = c(2, 2, P)

            def own(ap):
                return ap.rearrange("p (c t) -> p c t", c=NCH)

            PER = dict(raw=9, tile_done=1, proj=8, pj=1, kk_sum=1, kk_sq=1, kk_std=1, kk_max=1, v_turned=1, s0_turned=2,
                       s0_ready=2, scan=2, powers=4, ar_ready=2, r_ready=2, bt_ready=2, kt_ready=2, kd_ready=2,
                       prod1=2, prod2=2, low=2, lb_ready=2, mc_ready=2, t_ready=2, tt_ready=2, lm_ready=10,
                       x_done=10, x_ready=10, inv_done=10, inv_ready=10, tok_turned=2, tok_ready=2,
                       r_done=8, r_in=8, u_done=8, u_in=8, s_done=8, s_new=6, y_in=1, y_sum=1, mean=1, yc=1, yc_sq=1,
                       var=1, gn_std=1, bonus_in=1, bonus_sum=1, fin_turned=1, fin_ready=1, zero=1, bb=2,
                       state_in=64, state_out=64, w_in=48, l_in=48, dstep=0, pstep=0)

            class Step:

                def __init__(self, eng, j):
                    self.eng, self.j, self.made = eng, j, {}

                def wait(self, name, k, back=0):
                    v = self.j * PER[name] + (k + START.get(name, 0) - back * PER[name])
                    self.eng.wait_ge(sem(name), v)

                def inc(self, name, ins):
                    self.made[name] = self.made.get(name, 0) + 1
                    ins.then_inc(sem(name), 1)

                def link(self, name, ins):
                    self.inc(name, ins)
                    self.wait(name, self.made[name])

                def close(self):
                    for n, m in self.made.items():
                        assert m == PER[n], (n, m, PER[n])

            START = {"tile_done": 1}
            PER["dstep"], PER["pstep"] = DSTEPS, PSTEPS

            def chunks(z, s):
                lat = (0, CTX // CH + s if z == 0 else NCH - 1 - s)
                return [lat] + ([(1, s if z == 0 else CTX // CH - 1 - s)] if s < 2 else [])

            def half(z, s):
                cp = s % 2 if z == 0 else 1 - s % 2
                return slice(CH * cp, CH * cp + CH)

            idx = [(hh, tt) for hh in range(2) for tt in range(TT)]

            with nc.Block() as block:
                @block.sync
                def _(sp):
                    sp.wait_ge(sem("proj"), PER["proj"])
                    for j in range(1, KT):
                        step_loads(sp, j, stage_in)
                    sp.wait_ge(sem("proj"), KT * PER["proj"])
                    load_first(sp, f"wo{layer}")

                @block.tensor
                def _(pe):
                    for j in range(KT):
                        st = Step(pe, j)
                        st.wait("tile_done", 0)
                        st.wait("l_in", 48)
                        for i, (kind, z, b) in enumerate(((0, 0, 2), (0, 1, 5), (1, 0, 3), (1, 1, 6), (2, 0, 7))):
                            r = slice(0, P) if kind == 2 else slice(64 * z, 64 * z + 64)
                            st.inc("proj", nc.tensor.matmul(bank(b, TOK), slab[r, 3, kind, 0:P], mids[r, kind],
                                                            start=True, stop=True))
                        st.wait("w_in", 48)
                        for m, b in ((1, 1), (0, 0)):
                            for k in range(KT):
                                mm = nc.tensor.matmul(bank(b, TOK), slab[:, m, k, 0:P], xs[:, m, k],
                                                      start=k == 0, stop=k == KT - 1)
                            st.inc("proj", mm)
                        for t in range(TT):
                            for k in range(KT):
                                mm = nc.tensor.matmul(bank(4, TT, P)[:, t], xs[:, 2, k, t * P:(t + 1) * P],
                                                      slab[:, 2, k, 0:P], start=k == 0, stop=k == KT - 1)
                        st.inc("proj", mm)
                        st.wait("state_in", 64)
                        for z in range(2):
                            st.wait("raw", 4)
                            st.inc("s0_turned", nc.tensor.transpose(bank((2, 6)[z], P), stage_in[:, z], K["ident"]))
                        st.wait("kk_sq", 1)
                        st.wait("raw", 5)
                        st.inc("kk_sum", nc.tensor.matmul(bank(1, TOK), K["blocks"], sq, start=True, stop=True))
                        st.wait("raw", 8)
                        for t in range(TT):
                            mm = nc.tensor.transpose(bank(0, TT, P)[:, t], vtok[:, t], K["ident"])
                        st.inc("v_turned", mm)
                        for z in range(2):
                            st.wait("raw", 9)
                            st.wait("kk_max", 1)
                            st.wait("s0_ready", 2)
                            st.wait("zero", 1)
                            st.wait("bt_ready", z + 1)
                            st.wait("ar_ready", z + 1)
                            st.wait("r_ready", z + 1)
                            for half_, (name, src, b) in enumerate((("prod1", bT, 0), ("prod2", kTil, 2))):
                                if half_:
                                    st.wait("kt_ready", z + 1)
                                for hh in range(2):
                                    r = slice(64 * hh, 64 * hh + 64)
                                    for ch in range(NCH):
                                        q = slice(CH * (ch % 2), CH * (ch % 2) + CH)
                                        at = (ch // 2) * P
                                        mm = nc.tensor.matmul(psum[q, 4 * z + b + hh, at:at + P],
                                                              src[r, z, ch * CH:(ch + 1) * CH],
                                                              AR[r, z, ch].rearrange("p a t -> p (a t)"),
                                                              start=True, stop=True)
                                st.inc(name, mm)
                        for z in range(2):
                            st.wait("lb_ready", z + 1)
                            for hh in range(2):
                                r = slice(64 * hh, 64 * hh + 64)
                                for ch in range(NCH):
                                    q = slice(CH * (ch % 2), CH * (ch % 2) + CH)
                                    at = (ch // 2) * CH
                                    mm = nc.tensor.matmul(psum[q, 4 * z + hh, at:at + CH], AR[r, z, ch, 0],
                                                          bT[r, z, ch * CH:(ch + 1) * CH], start=True, stop=True)
                            st.inc("low", mm)
                        for z in range(2):
                            st.wait("mc_ready", z + 1)
                            for i, src in enumerate((bT, kTil)):
                                for t in range(TT):
                                    mm = nc.tensor.transpose(bank(4 * z + 2 + i, TT, P)[:, t],
                                                             src[:, z, t * P:(t + 1) * P], K["ident"])
                            st.inc("tok_turned", mm)
                        for n in range(1, LEVELS):
                            for z in range(2):
                                m = 2 * (n - 1) + z + 1
                                if n == 1:
                                    st.wait("t_ready", z + 1)
                                    st.wait("tt_ready", z + 1)
                                else:
                                    st.wait("inv_ready", m - 2)
                                    st.wait("x_ready", m - 2)
                                st.wait("lm_ready", m)
                                for i in range(6):
                                    for cp in range(2):
                                        q = slice(CH * cp, CH * cp + CH)
                                        mm = nc.tensor.matmul(psum[q, 4 * z, i * CH:(i + 1) * CH], LM[q, z, n % 2, i],
                                                              T[q, z, i], start=True, stop=True)
                                st.inc("x_done", mm)
                            for z in range(2):
                                m = 2 * (n - 1) + z + 1
                                st.wait("x_ready", m)
                                if n == 1:
                                    st.wait("tok_ready", z + 1)
                                for i in range(6):
                                    for cp in range(2):
                                        q = slice(CH * cp, CH * cp + CH)
                                        if n < LEVELS - 1:
                                            nc.tensor.matmul(psum[q, 4 * z + 2, i * CH:(i + 1) * CH], TTr[q, z, i],
                                                             X[q, z, i], start=True, stop=True)
                                        mm = nc.tensor.matmul(psum[q, 4 * z + 1, i * CH:(i + 1) * CH], X[q, z, i],
                                                              TTr[q, z, i], start=True, stop=True)
                                st.inc("inv_done", mm)
                        new = [0, 0]
                        for s in range(4):
                            for z in range(2):
                                q = half(z, s)
                                st.wait("x_ready", 9 + z)
                                if s:
                                    st.wait("s_new", S_NEW[(z, s - 1)])
                                    st.wait("r_in", 2 * (s - 1) + z + 1)
                                for stream, ch in chunks(z, s):
                                    at = stream * P
                                    nc.tensor.matmul(psum[q, 4 * z, at:at + P], AR[:, z, ch, 0], S[:, z, stream],
                                                     start=True, stop=False)
                                    for hh in range(2):
                                        mm = nc.tensor.matmul(psum[q, 4 * z, at + 64 * hh:at + 64 * hh + 64],
                                                              MC[q, z, 3 * hh + ch // 2, 0:CH],
                                                              vtok[q, ch // 2, 64 * hh:64 * hh + 64],
                                                              start=False, stop=hh == 1)
                                st.inc("r_done", mm)
                            for z in range(2):
                                q = half(z, s)
                                st.wait("r_in", 2 * s + z + 1)
                                st.wait("inv_ready", 9 + z)
                                if s:
                                    st.wait("u_in", 2 * (s - 1) + z + 1)
                                for stream, ch in chunks(z, s):
                                    for hh in range(2):
                                        at = stream * P + 64 * hh
                                        mm = nc.tensor.matmul(psum[q, 4 * z + 1, at:at + 64],
                                                              TTr[q, z, 3 * hh + ch // 2], R[q, z, at:at + 64],
                                                              start=True, stop=True)
                                st.inc("u_done", mm)
                            for z in range(2):
                                q = half(z, s)
                                st.wait("u_in", 2 * s + z + 1)
                                for stream, ch in chunks(z, s):
                                    t, at = ch // 2, ch * CH
                                    nc.tensor.matmul(psum[:, 4 * z + 3, at:at + CH], S[:, z, stream], AR[:, z, ch, 1],
                                                     start=True, stop=False)
                                    for hh in range(2):
                                        r = slice(64 * hh, 64 * hh + 64)
                                        a2 = stream * P + 64 * hh
                                        nc.tensor.matmul(psum[r, 4 * z + 3, at:at + CH], U[q, z, a2:a2 + 64],
                                                         LB[q, z, 3 * hh + t, CH:2 * CH], start=False, stop=False)
                                        mm = nc.tensor.matmul(psum[r, 4 * z + 3, at:at + CH],
                                                              vtok[q, t, 64 * hh:64 * hh + 64],
                                                              MC[q, z, 3 * hh + t, CH:2 * CH], start=False,
                                                              stop=True)
                                    if s < 3:
                                        a2 = stream * P
                                        nc.tensor.matmul(psum[:, 4 * z + 2, a2:a2 + P], tok[q, z, 0, t],
                                                         U[q, z, a2:a2 + P], start=True, stop=False)
                                        mm = nc.tensor.matmul(psum[:, 4 * z + 2, a2:a2 + P], tok[q, z, 1, t],
                                                              vtok[q, t], start=False, stop=True)
                                st.inc("s_done", mm)
                        st.wait("y_in", 1)
                        st.inc("mean", nc.tensor.matmul(bank(0, TOK), K["blocks"], yT, start=True, stop=True))
                        st.wait("bonus_in", 1)
                        st.inc("bonus_sum", nc.tensor.matmul(bank(4, TOK), K["blocks"], bonus, start=True, stop=True))
                        st.wait("s_new", 6)
                        for z in range(2):
                            mm = nc.tensor.transpose(bank(2, 2, P)[:, z], S[:, z, 1], K["ident"])
                        st.inc("fin_turned", mm)
                        st.wait("yc_sq", 1)
                        st.inc("var", nc.tensor.matmul(bank(1, TOK), K["blocks"], sq, start=True, stop=True))
                        st.close()

                @block.scalar
                def _(act):
                    act.wait_ge(sem("ends_one"), 1)
                    for j in range(KT):
                        st = Step(act, j)
                        st.wait("tile_done", 0)
                        st.wait("pj", 1)
                        for i, (dst, v, b) in enumerate(((decay, V_W0, 2), (decay, V_W0, 5), (rate, V_A0, 3), (rate, V_A0, 6))):
                            z = i % 2
                            st.wait("proj", i + 1)
                            st.inc("raw", nc.scalar.activation(dst[:, z], bank(b, TOK), ACT.Sigmoid,
                                                               bias=par[:, v + z:v + z + 1]))
                        st.wait("proj", 6)
                        st.inc("kk_sq", nc.scalar.activation(sq, bank(1, TOK), ACT.Square, scale=par[:, V_KK:V_KK + 1]))
                        st.inc("raw", nc.scalar.activation(kT, bank(1, TOK), ACT.Copy))
                        st.inc("raw", nc.scalar.activation(gT, bank(7, TOK), ACT.Copy))
                        st.wait("proj", 7)
                        st.inc("raw", nc.scalar.activation(rT, bank(0, TOK), ACT.Copy))
                        for z in range(2):
                            st.wait("scan", z + 1)
                            st.inc("powers", nc.scalar.activation(pp[:, z, :, 1 - z:CH + 1 - z], own(cum[:, z]), ACT.Exp,
                                                                  scale=-DECAY))
                            st.inc("powers", nc.scalar.activation(pi[:, z], cum[:, z], ACT.Exp, scale=DECAY))
                        st.wait("kk_max", 1)
                        st.inc("kk_std", nc.scalar.activation(inv, inv, ACT.Sqrt))
                        st.wait("proj", 8)
                        st.inc("raw", nc.scalar.activation(vtok.rearrange("p t c -> p (t c)"), bank(4, TOK), ACT.Copy))
                        for z in range(2):
                            st.wait("s0_turned", z + 1)
                            st.inc("s0_ready", nc.scalar.activation(S[:, z, 0], bank((2, 6)[z], P), ACT.Copy))
                        st.wait("v_turned", 1)
                        st.inc("raw", nc.scalar.activation(vT, bank(0, TOK), ACT.Copy))
                        for z in range(2):
                            st.wait("tok_turned", z + 1)
                            st.inc("tok_ready", nc.scalar.activation(
                                tok[:, z].rearrange("p a t c -> p a (t c)"), psum[:, 4 * z + 2:4 * z + 4, 0:TOK], ACT.Copy))
                        for n in range(1, LEVELS):
                            for z in range(2):
                                m = 2 * (n - 1) + z + 1
                                st.wait("x_done", m)
                                if n > 1:
                                    st.wait("inv_done", m - 2)
                                st.inc("x_ready", nc.scalar.activation(X[:, z].rearrange("p i t -> p (i t)"),
                                                                       bank(4 * z, TOK), ACT.Copy))
                        for s in range(4):
                            for z in range(2):
                                q = half(z, s)
                                n = P * len(chunks(z, s))
                                st.wait("r_done", 2 * s + z + 1)
                                if s:
                                    st.wait("u_done", 2 * (s - 1) + z + 1)
                                st.inc("r_in", nc.scalar.activation(R[q, z, 0:n], psum[q, 4 * z, 0:n], ACT.Copy))
                            for z in range(2):
                                q = half(z, s)
                                n = P * len(chunks(z, s))
                                st.wait("u_done", 2 * s + z + 1)
                                if s:
                                    st.wait("s_done", 2 * (s - 1) + z + 1)
                                st.inc("u_in", nc.scalar.activation(U[q, z, 0:n], psum[q, 4 * z + 1, 0:n], ACT.Copy))
                        st.wait("s_done", 8)
                        st.inc("y_sum", nc.scalar.activation(yT, bank(3, TOK), ACT.Copy))
                        st.wait("yc", 1)
                        st.inc("yc_sq", nc.scalar.activation(sq, tmp, ACT.Square))
                        st.wait("fin_turned", 1)
                        st.inc("fin_ready", nc.scalar.activation(stage_out.rearrange("p z c -> p (z c)"), bank(2, 2 * P),
                                                                 ACT.Copy))
                        st.wait("var", 1)
                        st.inc("gn_std", nc.scalar.activation(inv, bank(1, TOK), ACT.Sqrt, scale=1.0 / HD,
                                                              bias=K["gn_eps"]))
                        st.close()
                        act.wait_ge(sem("fin_ready"), j + 1)
                        for z in range(2):
                            for hh in range(2):
                                r = slice(64 * hh, 64 * hh + 64)
                                act.dma_start(flat3(O["new_state_rwkv"][0, 0, z, bass.ds(j * 2 + hh, 1)]),
                                              stage_out[r, z, r]).then_inc(sem("state_out"), 16)
                        act.wait_ge(sem("state_out"), j * 64 + 64)

                @block.gpsimd
                def _(pool):
                    nc.gpsimd.memset(pp, 1.0).then_inc(sem("ends_one"), 1)
                    vec3 = vecs[:, :].rearrange("p (v k) -> p v k", k=KT)
                    for j in range(KT):
                        st = Step(pool, j)
                        st.wait("tile_done", 0)
                        st.link("pstep", nc.gpsimd.tensor_copy(par[:, 0:15], vec3[:, :, bass.ds(j, 1)].rearrange("p v k -> p (v k)")))
                        st.inc("pj", nc.gpsimd.tensor_scalar(par[:, V_1KA:V_1KA + 1], par[:, V_KA:V_KA + 1], -1.0, 1.0,
                                                             ALU.mult, ALU.add))
                        st.inc("zero", nc.gpsimd.memset(S[:, :, 1], 0.0))
                        st.wait("raw", 5)
                        for z in range(2):
                            st.wait("bb", z + 1)
                            st.inc("kd_ready", nc.gpsimd.tensor_tensor(kd[:, z], kT, kd[:, z], ALU.mult))
                        st.wait("raw", 7)
                        for z in range(2):
                            st.wait("powers", 2 * z + 1)
                            st.inc("r_ready", nc.gpsimd.tensor_tensor(AR[:, z, :, 1], own(rT), pp[:, z, :, 1 - z:CH + 1 - z],
                                                                      ALU.mult))
                        eye = over(K["eye64"], 6)
                        for z in range(2):
                            st.wait("lb_ready", z + 1)
                            st.link("pstep", nc.gpsimd.tensor_tensor(TTr[:, z], LB[:, z, :, 0:CH], over(levels[:, z, 0], 6),
                                                                     ALU.mult))
                            st.inc("tt_ready", nc.gpsimd.tensor_tensor(TTr[:, z], TTr[:, z], eye, ALU.add))
                            st.inc("lm_ready", nc.gpsimd.tensor_tensor(LM[:, z, 1], LB[:, z, :, 0:CH],
                                                                       over(levels[:, z, 1], 6), ALU.mult))
                        for n in range(2, LEVELS):
                            for z in range(2):
                                if n >= 3:
                                    st.wait("x_done", 2 * (n - 3) + z + 1)
                                st.inc("lm_ready", nc.gpsimd.tensor_tensor(LM[:, z, n % 2], LB[:, z, :, 0:CH],
                                                                           over(levels[:, z, n], 6), ALU.mult))
                        st.link("pstep", nc.gpsimd.tensor_tensor(bonus, kd[:, 0], kd[:, 1], ALU.add))
                        st.link("pstep", nc.gpsimd.tensor_tensor(bonus, bonus, rT, ALU.mult))
                        st.inc("bonus_in", nc.gpsimd.tensor_scalar(bonus, bonus, par[:, V_RK:V_RK + 1], None, ALU.mult))
                        st.close()

                @block.vector
                def _(dve):
                    for j in range(KT):
                        st = Step(dve, j)

                        def link(ins):
                            st.link("dstep", ins)

                        st.wait("pj", 1)
                        for z in range(2):
                            st.wait("raw", z + 1)
                            rev = slice(None) if z == 0 else slice(None, None, -1)
                            st.inc("scan", nc.vector.tensor_tensor_scan(cum[:, z, rev], K["restart"], decay[:, z, rev], 0.0,
                                                                        ALU.mult, ALU.add))
                        for z in range(2):
                            st.wait("raw", 3 + z)
                            st.inc("bb", nc.vector.tensor_scalar(kd[:, z], rate[:, z], par[:, V_KA:V_KA + 1],
                                                                 par[:, V_1KA:V_1KA + 1], ALU.mult, ALU.add))
                        st.wait("kk_sum", 1)
                        st.inc("kk_max", nc.vector.tensor_scalar(inv, bank(1, TOK), 1e-24, None, ALU.max))
                        st.wait("kk_std", 1)
                        link(nc.vector.reciprocal(inv, inv))
                        st.wait("raw", 5)
                        link(nc.vector.scalar_tensor_tensor(kn, kT, par[:, V_KK:V_KK + 1], inv, ALU.mult, ALU.mult))
                        for z in range(2):
                            link(nc.vector.tensor_tensor(rate[:, z], rate[:, z], kn, ALU.mult))
                            st.wait("powers", 2 * z + 2)
                            st.inc("bt_ready", nc.vector.tensor_tensor(bT[:, z], rate[:, z], pi[:, z], ALU.mult))
                            before = pp[:, z, :, 0:CH] if z == 0 else pp[:, z, :, 1:CH + 1]
                            st.inc("ar_ready", nc.vector.scalar_tensor_tensor(AR[:, z, :, 0], own(kn), -1.0, before,
                                                                              ALU.mult, ALU.mult))
                            st.wait("kd_ready", z + 1)
                            st.inc("kt_ready", nc.vector.tensor_tensor(kTil[:, z], kd[:, z], pi[:, z], ALU.mult))
                        for z in range(2):
                            for name, dst, b, prod in (("lb_ready", LB, 0, "prod1"), ("mc_ready", MC, 2, "prod2")):
                                st.wait(prod, z + 1)
                                src = psum[:, 4 * z + b:4 * z + b + 2, 0:TOK].rearrange("p h (t c) -> p h t c", t=TT)
                                m = causal[:, z].unsqueeze(1).unsqueeze(1).to_broadcast([P, 2, TT, 2 * CH])
                                st.inc(name, nc.vector.tensor_tensor(
                                    dst[:, z].rearrange("p (h t) c -> p h t c", h=2), src, m, ALU.mult))
                        for z in range(2):
                            st.wait("low", z + 1)
                            src = psum[:, 4 * z:4 * z + 2, 0:TT * CH].rearrange("p h (t c) -> p h t c", t=TT)
                            m = first[:, z].unsqueeze(1).unsqueeze(1).to_broadcast([P, 2, TT, CH])
                            link(nc.vector.tensor_tensor(T[:, z].rearrange("p (h t) c -> p h t c", h=2), src, m, ALU.mult))
                            st.inc("t_ready", nc.vector.tensor_tensor(T[:, z], T[:, z], over(K["eye64"], 6), ALU.add))
                        st.wait("t_ready", 2)
                        for n in range(1, LEVELS):
                            for z in range(2):
                                st.wait("inv_done", 2 * (n - 1) + z + 1)
                                if n == 1:
                                    st.wait("tt_ready", z + 1)
                                else:
                                    st.wait("inv_ready", 2 * (n - 2) + z + 1)
                                if n < LEVELS - 1:
                                    t = T[:, z].rearrange("p i t -> p (i t)")
                                    nc.vector.tensor_tensor(t, bank(4 * z + 2, TOK), t, ALU.add)
                                t = TTr[:, z].rearrange("p i t -> p (i t)")
                                st.inc("inv_ready", nc.vector.tensor_tensor(t, bank(4 * z + 1, TOK), t, ALU.add))
                        for s in range(3):
                            for z in range(2):
                                st.wait("s_done", 2 * s + z + 1)
                                cs = chunks(z, s)
                                end = CH if z == 0 else 0
                                for stream, ch in cs:
                                    pc = pp[:, z, ch, end:end + 1]
                                    ins = nc.vector.scalar_tensor_tensor(fresh[:, z, stream], psum[:, 4 * z + 2, stream * P:(stream + 1) * P],
                                                                         pc, K["blocks"], ALU.mult, ALU.mult)
                                link(ins)
                                for stream, ch in cs:
                                    pc = pp[:, z, ch, end:end + 1]
                                    ins = nc.vector.scalar_tensor_tensor(S[:, z, stream], S[:, z, stream], pc, fresh[:, z, stream],
                                                                         ALU.mult, ALU.add)
                                st.inc("s_new", ins)
                        st.wait("s_done", 8)
                        st.wait("y_sum", 1)
                        st.inc("y_in", nc.vector.tensor_tensor(yT, bank(7, TOK), yT, ALU.add))
                        st.wait("mean", 1)
                        st.inc("yc", nc.vector.scalar_tensor_tensor(tmp, bank(0, TOK), -1.0 / HD, yT, ALU.mult, ALU.add))
                        st.wait("bonus_sum", 1)
                        st.wait("raw", 9)
                        st.wait("yc", 1)
                        link(nc.vector.tensor_tensor(yT, bank(4, TOK), vT, ALU.mult))
                        st.wait("gn_std", 1)
                        link(nc.vector.reciprocal(inv, inv))
                        link(nc.vector.tensor_tensor(tmp, tmp, inv, ALU.mult))
                        link(nc.vector.tensor_scalar(tmp, tmp, par[:, V_LNW:V_LNW + 1], par[:, V_LNB:V_LNB + 1],
                                                     ALU.mult, ALU.add))
                        link(nc.vector.tensor_tensor(tmp, tmp, yT, ALU.add))
                        st.wait("fin_ready", 1)
                        st.inc("tile_done", nc.vector.tensor_tensor(flat(hT[:, bass.ds(j, 1), :]), tmp, gT, ALU.mult))
                        st.close()
            stored["state_out"] = 64 * KT

            with nc.Block() as block:
                @block.sync
                def _(sp):
                    load_phase(sp, f"wo{layer}", following)

                @block.tensor
                def _(pe):
                    wo_pe(pe, f"wo{layer}", hT, lambda k: None)

                @block.vector
                def _(dve):
                    wo_dve(dve, f"wo{layer}", layer)
            add(acc_taken=KT)


        def finish():
            carve = Carve()
            ytok = carve(TT, D)
            with nc.Block() as block:
                @block.tensor
                def _(pe):
                    for t in range(TT):
                        for q in range(2):
                            n = 2 * t + q
                            if n >= 2:
                                pe.wait_ge(sem("y_taken"), n - 1)
                            for k in range(4):
                                mm = nc.tensor.transpose(bank(n % 2, 4, P)[:, k], xT[:, 4 * q + k, t * P:(t + 1) * P],
                                                         K["ident"])
                            mm.then_inc(sem("y_turned"), 1)

                @block.vector
                def _(dve):
                    for n in range(2 * TT):
                        dve.wait_ge(sem("y_turned"), n + 1)
                        nc.vector.tensor_copy(ytok[:, n // 2, (n % 2) * 512:(n % 2 + 1) * 512], bank(n % 2, 512))\
                            .then_inc(sem("y_taken"), 1)

                @block.sync
                def _(sp):
                    for t in range(TT):
                        sp.wait_ge(sem("y_taken"), 2 * (t + 1))
                        dst = O["y_prompt"][0] if t == 0 else O["y_sample"][0, (t - 1) * P:t * P]
                        sp.dma_start(dst, ytok[:, t]).then_inc(sem("out"), 16)
                    sp.wait_ge(sem("out"), 16 * TT)
                    for n, v in stored.items():
                        sp.wait_ge(sem(n), v)

        stored = {}

        for layer in range(DEPTH):
            (da_phases, rwkv_phases, swa_phases)[layer % 3](layer)
            mlp_phases(layer)
        setup("qkv0")
        for layer in range(DEPTH):
            (da, rwkv, swa)[layer % 3](layer, f"up{layer}")
            follow = {0: None, 1: "qkv2", 2: "qkv3", 3: None}[layer]
            mlp(layer, follow)
        finish()


INPUTS = ("x_prompt x_sample cache_da_k cache_da_v state_rwkv cache_swa_k cache_swa_v c c_ctx ada_w ada_b mlp_w1 mlp_w2 "
          "da_wqkv da_q_norm da_k_norm da_lambda da_subln da_wo rwkv_mu rwkv_wrkv rwkv_w0 rwkv_w1 rwkv_w2 rwkv_a0 "
          "rwkv_a1 rwkv_a2 rwkv_g1 rwkv_g2 rwkv_k_k rwkv_k_a rwkv_r_k rwkv_ln_w rwkv_ln_b rwkv_wo swa_wqkv "
          "swa_q_norm swa_k_norm swa_sink swa_wo").split()
OUTPUTS = {"y_prompt": (1, CTX, D), "y_sample": (1, LAT, D), "new_da_k": (1, 2, CTX, 8, P), "new_da_v": (1, 2, CTX, 8, P),
           "new_state_rwkv": (1, 1, 2, 16, HD, HD), "new_swa_k": (1, 1, CTX, 4, HD), "new_swa_v": (1, 1, CTX, 4, HD)}


def kernel(**inputs):
    import concourse.bacc as bacc
    from concourse.bass_utils import run_bass_kernel_spmd

    nc = bacc.Bacc("TRN2", target_bir_lowering=False, num_devices=1)
    arrays = {f"in_{n}": np.ascontiguousarray(inputs[n]) for n in INPUTS}
    arrays["in_consts"] = constants()
    I = {n[3:]: nc.dram_tensor(n, a.shape, mybir.dt.from_np(a.dtype), kind="ExternalInput").ap()
         for n, a in arrays.items()}
    O = {n: nc.dram_tensor(f"out_{n}", s, F32, kind="ExternalOutput").ap() for n, s in OUTPUTS.items()}
    build(nc, I, O)
    r = run_bass_kernel_spmd(nc, [arrays], core_ids=[0])
    return tuple(r.results[0][f"out_{n}"] for n in OUTPUTS)
```

```python
import math
from contextlib import ExitStack

import numpy as np

import concourse.bass as bass
from concourse import mybir

F32 = mybir.dt.float32
F32R = mybir.dt.float32r
ACT = mybir.ActivationFunctionType
ALU = mybir.AluOpType
AX_X = mybir.AxisListType.X

P = 128
D = 1024
KT = D // P
CTX, LAT, PAST = 128, 256, 128
TOK = CTX + LAT
TT = TOK // P
DEPTH = 4
FF = 4 * D
FT = FF // P
HD = 64
GRID_W = 64
CH = 64
NCH = TOK // CH
LEVELS = 6
EPS = 1e-6
GN_EPS = 64e-5
DECAY = math.exp(-0.5)
NEG_INF = -1e30
SCALE = HD ** -0.5
GROUPS = ((0, slice(0, CTX)), (1, slice(CTX, TOK)))
SLAB = 256
SLOTS = 4
ADA_SLOTS = 3
ADA_UNITS = 6 * D // SLAB

CONST_COLS = {}
_at = 0
for _name, _n in (("ident", P), ("blocks", P), ("ones", P), ("swap32", P), ("swap64", P), ("cos", LAT), ("sin", LAT),
                  ("band", 2 * TOK), ("eye64", 64), ("first", 2 * 64), ("levels", 2 * LEVELS * 64),
                  ("causal", 2 * 128), ("add_parts", 12), ("restart", TOK), ("eps", 1), ("gn_eps", 1)):
    CONST_COLS[_name] = slice(_at, _at + _n)
    _at += _n
CONST_N = _at


def constants():
    c = np.zeros((P, CONST_N), np.float32)
    p = np.arange(P)[:, None]
    q = np.arange(P)[None, :]
    c[:, CONST_COLS["ident"]] = p == q
    c[:, CONST_COLS["blocks"]] = p // 64 == q // 64
    c[:, CONST_COLS["ones"]] = 1
    c[:, CONST_COLS["swap32"]] = p == (q ^ 32)
    c[:, CONST_COLS["swap64"]] = p == (q ^ 64)
    t = np.arange(LAT)
    n_freq = HD // 4
    inv = (np.float32(10000.0) ** (-np.arange(n_freq, dtype=np.float32) / n_freq)).astype(np.float32)
    ang = np.concatenate([(t // GRID_W).astype(np.float32)[:, None] * inv,
                          (t % GRID_W).astype(np.float32)[:, None] * inv], axis=1).astype(np.float32)
    d = np.arange(P) % HD
    c[:, CONST_COLS["cos"]] = np.cos(ang.astype(np.float64))[:, d % 32].T
    c[:, CONST_COLS["sin"]] = (np.sin(ang.astype(np.float64))[:, d % 32] * np.where(d < 32, -1, 1)).T
    band = np.zeros((P, 2, TOK))
    for b in range(2):
        far = np.abs(np.arange(LAT)[None, :] - (np.arange(P)[:, None] + b * P)) > 128
        band[:, b, :LAT][far] = NEG_INF
    c[:, CONST_COLS["band"]] = band.reshape(P, -1)
    r = np.arange(P)[:, None] % 64
    s = np.arange(64)[None, :]
    c[:, CONST_COLS["eye64"]] = r == s
    first, levels, causal = np.zeros((P, 2, 64)), np.zeros((P, 2, LEVELS, 64)), np.zeros((P, 2, 2, 64))
    for z in range(2):
        row, col = (r, s) if z == 0 else (63 - r, 63 - s)
        first[:, z] = (row // 2 == col // 2) & (row > col)
        for n in range(LEVELS):
            w = 1 << n
            levels[:, z, n] = (row // (2 * w) == col // (2 * w)) & (row // w < col // w)
        causal[:, z, 0] = row < col
        causal[:, z, 1] = row <= col
    c[:, CONST_COLS["first"]] = first.reshape(P, -1)
    c[:, CONST_COLS["levels"]] = levels.reshape(P, -1)
    c[:, CONST_COLS["causal"]] = causal.reshape(P, -1)
    c[:, CONST_COLS["add_parts"]] = (p < 24) & (p // 4 == q[:, :12] // 2) & (p % 2 == q[:, :12] % 2)
    c[:, CONST_COLS["restart"]] = (np.arange(TOK) % CH != 0)[None, :]
    c[:, CONST_COLS["eps"]] = EPS
    c[:, CONST_COLS["gn_eps"]] = GN_EPS
    return c


def over(ap, n):
    return ap.unsqueeze(1).to_broadcast([ap.shape[0], n, ap.shape[1]])


def build(nc, I, O):
    ctx = ExitStack()
    with ctx:
        def sb(name, *shape):
            return ctx.enter_context(nc.sbuf_tensor(name, [P, *shape], F32))

        sems = {}

        def sem(name):
            if name not in sems:
                sems[name] = ctx.enter_context(nc.semaphore(name))
            return sems[name]

        const = sb("const", CONST_N)
        K = {n: const[:, s] for n, s in CONST_COLS.items()}
        band = K["band"].rearrange("p (b t) -> p b t", b=2)
        first = K["first"].rearrange("p (z t) -> p z t", z=2)
        levels = K["levels"].rearrange("p (z n t) -> p z n t", z=2, n=LEVELS)
        causal = K["causal"].rearrange("p (z t) -> p z t", z=2)
        xT = sb("xT", KT, TOK)
        hT = sb("hT", KT, TOK)
        slab = sb("slab", SLOTS, KT, SLAB)
        ada_slab = sb("ada_slab", ADA_SLOTS, KT, SLAB)
        mod = sb("mod", DEPTH, 48, 2)
        ada_b = sb("ada_b", DEPTH * 48)
        cond = sb("cond", KT, 2)
        rstd = sb("rstd", TOK)
        small = sb("small", 8)
        vecs = sb("vecs", 120)
        lam = sb("lam", 8)
        ROOM = 27900
        psum = ctx.enter_context(nc.psum_tensor("psum", [P, 8, 512], F32))

        def bank(b, *shape):
            n = int(np.prod(shape))
            v = psum[:, b, 0:n]
            return v if len(shape) == 1 else v.rearrange("p (a b) -> p a b", a=shape[0])

        class Carve:

            def __init__(self, of):
                self.at, self.of = 0, of

            def __call__(self, *shape):
                n = int(np.prod(shape))
                v = self.of[:, self.at:self.at + n]
                self.at += n
                assert self.at <= self.of.shape[1], self.at
                names = "abcd"[:len(shape)]
                if len(shape) > 1:
                    v = v.rearrange(f"p ({' '.join(names)}) -> p {' '.join(names)}",
                                    **dict(zip(names[:-1], shape)))
                return v

        count = {}

        def base(name):
            return count.get(name, 0)

        def add(**kw):
            for k, v in kw.items():
                count[k] = count.get(k, 0) + v

        class Link:

            def __init__(self, eng, name, start=None):
                self.eng, self.name, self.sem, self.n = eng, name, sem(name), 0
                self.start = base(name) if start is None else start

            def __call__(self, ins):
                self.n += 1
                ins.then_inc(self.sem, 1)
                self.eng.wait_ge(self.sem, self.start + self.n)

            def close(self):
                add(**{self.name: self.n})

        def alone(eng):
            eng.wait_ge(sem("const_in"), 16)

        def start_at(eng, name, value):
            if not (isinstance(value, int) and value <= 0):
                eng.wait_ge(sem(name), value)
                if not isinstance(value, int):
                    alone(eng)

        slab_ready = [sem(f"slab_ready{s}") for s in range(SLOTS)]
        run_done, acc_taken, split_ready = sem("run_done"), sem("acc_taken"), sem("split_ready")
        run_after = []
        phases = {}

        def phase(name, runs, src):
            phases[name] = (len(run_after), len(runs), src)
            for r in runs:
                run_after.append((run_after[-1] if run_after else 0) + r)

        def cols(w, at):
            return w.rearrange("(k p) n -> p k n", p=P)[:, :, bass.ds(at, SLAB)]

        def load_unit(sp, name, u):
            start, _, src = phases[name]
            g = start + u
            if g >= SLOTS:
                sp.wait_ge(run_done, run_after[g - SLOTS])
            sp.dma_start(slab[:, g % SLOTS], src(u)).then_inc(slab_ready[g % SLOTS], 16)

        def load_phase(sp, name, following):
            for u in range(SLOTS, phases[name][1]):
                load_unit(sp, name, u)
            load_first(sp, following)

        def load_first(sp, following):
            if following:
                for u in range(min(SLOTS, phases[following][1])):
                    load_unit(sp, following, u)

        def has_slab(pe, u, it=0):
            pe.wait_ge(slab_ready[u % SLOTS], 16 * (u // SLOTS + 1) + it * 16)

        ADA_GROUP = 6
        ADA_GROUPS = ADA_UNITS // ADA_GROUP
        PAD4 = 4 * (ADA_GROUP - 1)
        CONDW = 2 * PAD4 + 4

        def window(cw, k, s):
            return cw[:, k, PAD4 - 4 * s:PAD4 - 4 * s + 4 * ADA_GROUP]

        def ada_load(sp, layer, it, s):
            start_at(sp, "ada_free", layer * ADA_UNITS + s + 1 - ADA_SLOTS + it * ADA_GROUP)
            sp.dma_start(ada_slab[:, s % ADA_SLOTS], cols(I["ada_w"][layer], (it * ADA_GROUP + s) * SLAB))\
                .then_inc(sem(f"ada_ready{s % ADA_SLOTS}"), 16)

        def ada_ready(eng, layer, it, s):
            loads = (layer * ADA_UNITS + s) // ADA_SLOTS + 1
            eng.wait_ge(sem(f"ada_ready{s % ADA_SLOTS}"), loads * 16 + it * (16 * ADA_GROUP // ADA_SLOTS))

        def ada_rows(act, layer, it, done, first, rows):
            act.wait_ge(sem(done), first + it * ADA_GROUP)
            nc.scalar.activation(rows[0:4 * ADA_GROUP, :], psum[0:4 * ADA_GROUP, 6, 0:SLAB], ACT.Copy)\
                .then_inc(sem("rows_ready"), 1)

        def mod_cols(h):
            return psum[:, 7, 2 * ADA_GROUP * h:2 * ADA_GROUP * (h + 1)]

        def ada_turn(pe, layer, it, rows):
            g = layer * ADA_GROUPS + it
            pe.wait_ge(sem("rows_ready"), g + 1)
            start_at(pe, "mod_step", g)
            for h in range(2):
                mm = nc.tensor.matmul(mod_cols(h), rows[0:4 * ADA_GROUP, h * P:(h + 1) * P],
                                      K["add_parts"][0:4 * ADA_GROUP], start=True, stop=True)
            mm.then_inc(sem("rows_turned"), 1)

        def ada_take(dve, layer, it):
            g = layer * ADA_GROUPS + it
            dve.wait_ge(sem("rows_turned"), g + 1)
            n = 2 * ADA_GROUP
            dst = mod[:, layer, bass.ds(it * n, n), :].rearrange("p (s h) g -> p h s g", h=2)
            b = ada_b[:, bass.ds(it * n + layer * 48, n)].rearrange("p (s h) -> p h s", h=2)
            for h in range(2):
                ins = nc.vector.tensor_tensor(dst[:, h], mod_cols(h).rearrange("p (s g) -> p s g", g=2),
                                              b[:, h].unsqueeze(2).to_broadcast([P, ADA_GROUP, 2]), ALU.add)
            ins.then_inc(sem("mod_step"), 1)

        def ada_scale(dve, layer):
            dve.wait_ge(sem("mod_step"), (layer + 1) * ADA_GROUPS)
            for c in (1, 4):
                m = mod[:, layer, c * KT:(c + 1) * KT, :]
                nc.vector.tensor_scalar(m, m, 1.0, None, ALU.add).then_inc(sem("mod_ready"), 1)

        def norm_act(act, layer, half, out, upper=None):
            b = base("sq_ready")
            act.wait_ge(sem("mod_ready"), 2 * (layer + 1))
            for k in range(KT):
                nc.scalar.activation(hT[:, k], xT[:, k], ACT.Square).then_inc(sem("sq_ready"), 1)
            act.wait_ge(sem("sum_done"), base("sum_done") + 1)
            nc.scalar.activation(rstd[:, :], bank(7, TOK), ACT.Sqrt, scale=1.0 / D, bias=K["eps"])\
                .then_inc(sem("std_ready"), 1)
            for k in range(KT):
                act.wait_ge(sem("xn_ready"), b + k + 1)
                for g, t in GROUPS:
                    ins = nc.scalar.activation(out(k, g), hT[:, k, t], ACT.Identity,
                                               scale=mod[:, layer, (3 * half + 1) * KT + k, g:g + 1],
                                               bias=mod[:, layer, 3 * half * KT + k, g:g + 1])
                ins.then_inc(sem("h_ready"), 1)
                if upper is not None and k >= 1:
                    act.wait_ge(sem("h_ready"), b + k)
                    nc.scalar.activation(upper[:, 0, k - 1], hT[:, k - 1], ACT.Copy).then_inc(sem("h_hi"), 1)
            if upper is not None:
                act.wait_ge(sem("h_ready"), b + KT)
                nc.scalar.activation(upper[:, 0, KT - 1], hT[:, KT - 1], ACT.Copy).then_inc(sem("h_hi"), 1)

        def norm_pe(pe):
            for k in range(KT):
                pe.wait_ge(sem("sq_ready"), base("sq_ready") + k + 1)
                mm = nc.tensor.matmul(bank(7, TOK), K["ones"], hT[:, k], start=k == 0, stop=k == KT - 1)
            mm.then_inc(sem("sum_done"), 1)

        def norm_dve(dve, link):
            dve.wait_ge(sem("std_ready"), base("sum_done") + 1)
            link(nc.vector.reciprocal(rstd[:, :], rstd[:, :]))
            for k in range(KT):
                nc.vector.tensor_tensor(hT[:, k], xT[:, k], rstd[:, :], ALU.mult).then_inc(sem("xn_ready"), 1)

        def norm_counts():
            add(sq_ready=KT, sum_done=1)

        def in_place(k, g):
            return hT[:, k, GROUPS[g][1]]

        def has_h(pe, k):
            pe.wait_ge(sem("h_ready"), base("sq_ready") + k + 1)

        def flat(ap):
            return ap.rearrange("p a b -> p (a b)")

        def residual(layer, half, n, acc):
            for g, t in GROUPS:
                gate = flat(mod[:, layer, bass.ds(n + (3 * half + 2) * KT, 1), g:g + 1])
                x = flat(xT[:, bass.ds(n, 1), t])
                ins = nc.vector.scalar_tensor_tensor(x, acc[:, t], gate, x, ALU.mult, ALU.add)
            return ins

        def lambda_init(i):
            return 0.8 - 0.6 * math.exp(-0.3 * i)

        def setup(following, room):
            carve = Carve(room)
            xtok = carve(TT, D)
            rows = carve(4, P)
            lam_in = carve(2, 4, HD)
            sg = carve(16)
            cond_pad, mod_rows = carve(KT, CONDW), carve(SLAB)
            n_rows = (96, 96, 120, 24)

            def row(v):
                return v.rearrange("(r p) -> r p", p=P)

            ab = row(I["ada_b"].rearrange("l n -> (l n)"))
            loads = [(rows[0:96, 0], ab[0:96]), (rows[0:96, 1], ab[96:192])]
            at = 0
            for v in (I["rwkv_mu"].rearrange("l m d -> (l m d)"), I["rwkv_w0"].rearrange("l z d -> (l z d)"),
                      I["rwkv_a0"].rearrange("l z d -> (l z d)"), I["rwkv_k_k"][0], I["rwkv_k_a"][0],
                      I["rwkv_r_k"][0].rearrange("h d -> (h d)"), I["rwkv_ln_w"][0], I["rwkv_ln_b"][0]):
                m = v.shape[0] // P
                loads.append((rows[at:at + m, 2], row(v)))
                at += m
            assert at == 120
            loads += [(rows[0:8, 3], row(I["c_ctx"])), (rows[8:16, 3], row(I["c"][0]))]
            at = 16
            for v in (I["da_q_norm"][0], I["da_k_norm"][0], I["da_q_norm"][1], I["da_k_norm"][1],
                      I["swa_q_norm"][0], I["swa_k_norm"][0]):
                one = v.unsqueeze(0)
                loads += [(rows[at:at + 1, 3, 0:HD], one), (rows[at:at + 1, 3, HD:P], one)]
                at += 1
            for j in range(2):
                loads.append((rows[at:at + 1, 3], I["da_subln"][j:j + 1]))
                at += 1
            loads.append((lam_in, I["da_lambda"].unsqueeze(0).to_broadcast([P, 2, 4, HD])))
            x_loads = [(xtok[:, 0], I["x_prompt"][0])] + [
                (xtok[:, 1 + t], I["x_sample"][0, t * P:(t + 1) * P]) for t in range(2)]
            with nc.Block() as block:
                @block.sync
                def _(sp):
                    sp.dma_start(const[:, :], I["consts"]).then_inc(sem("const_in"), 16)
                    for s in range(ADA_GROUP):
                        ada_load(sp, 0, 0, s)
                    with sp.Fori(1, ADA_GROUPS) as it:
                        for s in range(ADA_GROUP):
                            ada_load(sp, 0, it, s)
                    load_first(sp, following)

                @block.scalar
                def _(act):
                    for dst, s in loads:
                        act.dma_start(dst, s).then_inc(sem("rows_in"), 16)
                    for dst, s in x_loads:
                        act.dma_start(dst, s).then_inc(sem("x_in"), 16)
                    act.wait_ge(sem("rows_done"), 4)
                    nc.scalar.activation(sg[:, :], bank(3, 24)[:, 0:16], ACT.Sigmoid).then_inc(sem("sig_cond"), 1)
                    for j in range(2):
                        act.wait_ge(sem("lam_dots"), 2 * (j + 1))
                        nc.scalar.activation(lam[:, 4 * j:4 * j + 2], lam[:, 4 * j:4 * j + 2], ACT.Exp)\
                            .then_inc(sem("lam_exps"), 1)
                    with act.Fori(0, ADA_GROUPS) as it:
                        ada_rows(act, 0, it, "ada_free", ADA_GROUP, mod_rows)

                @block.gpsimd
                def _(pool):
                    nc.gpsimd.memset(mod_rows, 0.0).then_inc(sem("ada_mult"), 1)
                    nc.gpsimd.memset(cond_pad, 0.0).then_inc(sem("pad_zero"), 1)

                @block.tensor
                def _(pe):
                    pe.wait_ge(sem("const_in"), 16)
                    pe.wait_ge(sem("rows_in"), 16 * len(loads))
                    for i, n in enumerate(n_rows):
                        nc.tensor.transpose(bank(i, n), rows[0:n, i], K["ident"][0:n, 0:n])\
                            .then_inc(sem("rows_done"), 1)
                    pe.wait_ge(sem("x_in"), 16 * TT)
                    for k in range(KT):
                        if k >= 2:
                            pe.wait_ge(sem("x_taken"), k - 1)
                        for t in range(TT):
                            mm = nc.tensor.transpose(bank(4 + k % 2, TT, P)[:, t], xtok[:, t, k * P:(k + 1) * P],
                                                     K["ident"])
                        mm.then_inc(sem("x_turned"), 1)
                    pe.wait_ge(sem("cond_ready"), 2)

                    def group(it):
                        for s in range(ADA_GROUP):
                            ada_ready(pe, 0, it, s)
                            for k in range(KT):
                                mm = nc.tensor.matmul(psum[0:4 * ADA_GROUP, 6, 0:SLAB], window(cond_pad, k, s),
                                                      ada_slab[:, s % ADA_SLOTS, k], start=s == 0 and k == 0,
                                                      stop=s == ADA_GROUP - 1 and k == KT - 1)
                            mm.then_inc(sem("ada_free"), 1)
                        ada_turn(pe, 0, it, mod_rows)

                    group(0)
                    with pe.Fori(1, ADA_GROUPS) as it:
                        group(it)

                @block.vector
                def _(dve):
                    link = Link(dve, "dve_step")
                    dve.wait_ge(sem("rows_done"), 4)
                    nc.vector.tensor_copy(ada_b[:, 0:96], bank(0, 96))
                    nc.vector.tensor_copy(ada_b[:, 96:192], bank(1, 96))
                    link(nc.vector.tensor_copy(vecs[:, :], bank(2, 120)))
                    dve.wait_ge(sem("sig_cond"), 1)
                    link(nc.vector.tensor_copy(small[:, :], bank(3, 24)[:, 16:24]))
                    nc.vector.tensor_tensor(cond[:, :, :].rearrange("p k g -> p g k"),
                                            bank(3, 24)[:, 0:16].rearrange("p (g k) -> p g k", g=2),
                                            sg.rearrange("p (g k) -> p g k", g=2), ALU.mult)\
                        .then_inc(sem("cond_ready"), 1)
                    dve.wait_ge(sem("cond_ready"), 1)
                    dve.wait_ge(sem("pad_zero"), 1)
                    nc.vector.tensor_copy(cond_pad[:, :, PAD4:PAD4 + 2], cond[:, :, :]).then_inc(sem("cond_ready"), 1)
                    for k in range(KT):
                        dve.wait_ge(sem("x_turned"), k + 1)
                        nc.vector.tensor_copy(xT[:, k], bank(4 + k % 2, TOK)).then_inc(sem("x_taken"), 1)
                    for j in range(2):
                        s = small[:, 6 + j:7 + j]
                        link(nc.vector.tensor_scalar(s, s, 1.0 - lambda_init(3 * j), None, ALU.mult))
                    for j in range(2):
                        for m in range(2):
                            link(nc.vector.tensor_tensor(lam_in[:, j, 2 * m], lam_in[:, j, 2 * m],
                                                         lam_in[:, j, 2 * m + 1], ALU.mult))
                            nc.vector.tensor_reduce(lam[:, 4 * j + m:4 * j + m + 1], lam_in[:, j, 2 * m], AX_X,
                                                    ALU.add).then_inc(sem("lam_dots"), 1)
                        dve.wait_ge(sem("lam_exps"), j + 1)
                        link(nc.vector.tensor_scalar(lam[:, 4 * j + 2:4 * j + 3], lam[:, 4 * j:4 * j + 1],
                                                     lam[:, 4 * j + 1:4 * j + 2], lambda_init(3 * j),
                                                     ALU.subtract, ALU.add))
                    with dve.Fori(0, ADA_GROUPS) as it:
                        ada_take(dve, 0, it)
                    ada_scale(dve, 0)
                    link.close()

        QUARTERS, UNITS = 4, 2 * SLOTS

        def mlp_phases(layer):
            def src(u):
                q, r = divmod(u, UNITS)
                return mlp_slab(layer, q, r)
            phase(f"mlp{layer}", [2] * (QUARTERS * UNITS), src)

        def mlp_slab(layer, q, r):
            if r < SLOTS:
                return cols(I["mlp_w1"][layer], (q * SLOTS + r) * SLAB)
            w2 = I["mlp_w2"][layer].rearrange("(k p) n -> p k n", p=P)
            return w2[:, bass.ds(q * KT, KT), (r - SLOTS) * SLAB:(r - SLOTS + 1) * SLAB]

        def mlp(layer, following):
            more = layer + 1 < DEPTH
            L = layer + 1
            start = phases[f"mlp{layer}"][0]
            runs = run_after[start - 1]
            taken, up_taken, sb, hb = base("acc_taken"), base("up_taken"), base("split_ready"), base("hid_ready")
            LAST = QUARTERS - 1
            ada_base = (L - 1) * ADA_UNITS
            with nc.sbuf_tensor(f"parts{layer}", [P, 4 * KT * TOK + 6 * KT * SLAB + KT * CONDW], F32R) as parts, \
                    nc.sbuf_tensor(f"room_mlp{layer}", [P, SLAB + 4 * TOK], F32) as room:
                c = Carve(parts[:, :])
                h, hid = c(2, KT, TOK), c(2, KT, TOK)
                r = Carve(room[:, :])
                mod_rows, square = r(SLAB), r(4, TOK)
                w, aw, cw = c(2, 2, KT, SLAB), c(2, KT, SLAB), c(KT, CONDW)
                with nc.Block() as block:
                    @block.sync
                    def _(sp):
                        def quarter(i, last):
                            for r in range(UNITS):
                                if not (last and r >= SLOTS):
                                    sp.wait_ge(split_ready, sb + r + 1 + i * UNITS)
                                    if not last:
                                        alone(sp)
                                    q, n = divmod(r + SLOTS, UNITS)
                                    slot = (start + r) % SLOTS
                                    sp.dma_start(slab[:, slot], mlp_slab(layer, i + q, n)).then_inc(slab_ready[slot], 16)
                                if more and r < ADA_GROUP:
                                    ada_load(sp, L, i, r)

                        with sp.Fori(0, LAST) as i:
                            quarter(i, False)
                        quarter(LAST, True)
                        load_first(sp, following)

                    @block.tensor
                    def _(pe):
                        def product(out, x, y, first, last):
                            for n, (a, b) in enumerate(((0, 0), (0, 1), (1, 0))):
                                mm = nc.tensor.matmul(out, x(a), y(b), start=first and n == 0, stop=last and n == 2)
                            return mm

                        def quarter(i):
                            for r in range(UNITS):
                                pe.wait_ge(split_ready, sb + r + 1 + i * UNITS)
                                for j in range(2):
                                    n = (2 * r + j) % KT
                                    if (n >= 2) == (r < SLOTS):
                                        pe.wait_ge(sem("up_taken"), up_taken + (n - 1 if r < SLOTS else n + 7) + i * KT)
                                    else:
                                        pe.wait_ge(acc_taken, taken + n - 1 + i * KT)
                                    for k in range(KT):
                                        if r == SLOTS and j == 0:
                                            pe.wait_ge(sem("hid_ready"), hb + k + 1 + i * KT)
                                        mm = product(bank(j, TOK), lambda a: w[:, r % 2, a, k, j * P:(j + 1) * P],
                                                     lambda b: (h if r < SLOTS else hid)[:, b, k], k == 0, k == KT - 1)
                                    mm.then_inc(run_done, 1)
                                if more and 1 <= r <= ADA_GROUP:
                                    s = r - 1
                                    pe.wait_ge(sem("ada_free"), L * ADA_UNITS + s + 1 + i * ADA_GROUP)
                                    for a in range(2):
                                        for k in range(KT):
                                            mm = nc.tensor.matmul(psum[0:4 * ADA_GROUP, 6, 0:SLAB], window(cw, k, s), aw[:, a, k],
                                                                  start=s == 0 and a == 0 and k == 0,
                                                                  stop=s == ADA_GROUP - 1 and a == 1 and k == KT - 1)
                                    mm.then_inc(sem("ada_mult"), 1)
                            if more:
                                ada_turn(pe, L, i, mod_rows)

                        norm_pe(pe)
                        for k in range(KT):
                            pe.wait_ge(sem("h_split"), base("h_split") + k + 1)
                        if more:
                            pe.wait_ge(sem("cond_split"), layer + 1)
                        with pe.Fori(0, QUARTERS) as i:
                            quarter(i)

                    @block.scalar
                    def _(act):
                        def hi(r, i):
                            g = start + r
                            act.wait_ge(slab_ready[g % SLOTS], 16 * (g // SLOTS + 1) + i * (16 * UNITS // SLOTS))
                            act.wait_ge(run_done, runs + 2 * max(r - 1, 0) + i * 2 * UNITS)
                            nc.scalar.activation(w[:, r % 2, 0], slab[:, g % SLOTS], ACT.Copy).then_inc(sem("hi_ready"), 1)

                        def hid_hi(n, i):
                            act.wait_ge(run_done, runs + n + 1 + i * 2 * UNITS)
                            nc.scalar.activation(hT[:, n], bank(n % 2, TOK), ACT.Relu).then_inc(sem("up_taken"), 1)
                            act.wait_ge(sem("up_taken"), up_taken + n + 1 + i * KT)
                            nc.scalar.activation(hid[:, 0, n], hT[:, n], ACT.Square).then_inc(sem("hid_hi"), 1)

                        def quarter(i, last):
                            for r in range(UNITS):
                                if 1 <= r <= SLOTS:
                                    hid_hi(2 * r - 1, i)
                                if not (last and r == UNITS - 1):
                                    hi(r + 1, i)
                                if more and 1 <= r <= ADA_GROUP:
                                    s = r - 1
                                    ada_ready(act, L, i, s)
                                    act.wait_ge(sem("ada_mult"), ada_base + 1 + s + i * ADA_GROUP)
                                    nc.scalar.activation(aw[:, 0], ada_slab[:, s % ADA_SLOTS], ACT.Copy)\
                                        .then_inc(sem("ada_hi"), 1)
                                if r < SLOTS:
                                    hid_hi(2 * r, i)
                            if more:
                                ada_rows(act, L, i, "ada_mult", 1 + ada_base + ADA_GROUP, mod_rows)

                        hi(0, 0)
                        norm_act(act, layer, 1, in_place, upper=h)
                        with act.Fori(0, LAST) as i:
                            quarter(i, False)
                        quarter(LAST, True)

                    @block.gpsimd
                    def _(pool):
                        if more:
                            nc.gpsimd.memset(cw.bitcast(F32), 0.0).then_inc(sem("cw_zero"), 1)
                        for k in range(KT):
                            pool.wait_ge(sem("h_hi"), base("h_split") + k + 1)
                            nc.gpsimd.tensor_tensor(h[:, 1, k], hT[:, k], h[:, 0, k].bitcast(F32), ALU.subtract)\
                                .then_inc(sem("h_split"), 1)
                        with pool.Fori(0, QUARTERS) as i:
                            for n in range(KT):
                                pool.wait_ge(sem("hid_hi"), hb + n + 1 + i * KT)
                                pool.wait_ge(sem("hid_sq"), hb + n + 1 + i * KT)
                                nc.gpsimd.tensor_tensor(hid[:, 1, n], square[:, n % 4], hid[:, 0, n].bitcast(F32), ALU.subtract)\
                                    .then_inc(sem("hid_ready"), 1)

                    @block.vector
                    def _(dve):
                        def lo(r, i):
                            dve.wait_ge(sem("hi_ready"), sb + r + 1 + i * UNITS)
                            nc.vector.tensor_tensor(w[:, r % 2, 1], slab[:, (start + r) % SLOTS], w[:, r % 2, 0].bitcast(F32),
                                                    ALU.subtract).then_inc(split_ready, 1)

                        def take(r, j, i):
                            if r < SLOTS:
                                n = 2 * r + j
                                dve.wait_ge(sem("up_taken"), up_taken + n + 1 + i * KT)
                                if n >= 4:
                                    dve.wait_ge(sem("hid_ready"), hb + n - 3 + i * KT)
                                nc.vector.tensor_tensor(square[:, n % 4], hT[:, n], hT[:, n], ALU.mult)\
                                    .then_inc(sem("hid_sq"), 1)
                            else:
                                dve.wait_ge(run_done, runs + 2 * r + j + 1 + i * 2 * UNITS)
                                residual(layer, 1, 2 * (r - SLOTS) + j, bank(j, TOK)).then_inc(acc_taken, 1)

                        def quarter(i, last):
                            for r in range(UNITS):
                                if r >= 1:
                                    take(r - 1, 1, i)
                                if not (last and r == UNITS - 1):
                                    lo(r + 1, i)
                                if more and 1 <= r <= ADA_GROUP:
                                    s = r - 1
                                    dve.wait_ge(sem("ada_hi"), ada_base + s + 1 + i * ADA_GROUP)
                                    nc.vector.tensor_tensor(aw[:, 1], ada_slab[:, s % ADA_SLOTS], aw[:, 0].bitcast(F32),
                                                            ALU.subtract).then_inc(sem("ada_free"), 1)
                                take(r, 0, i)
                            take(UNITS - 1, 1, i)
                            if more:
                                ada_take(dve, L, i)

                        lo(0, 0)
                        link = Link(dve, "dve_step")
                        if more:
                            dve.wait_ge(sem("cw_zero"), layer + 1)
                            own = cw[:, :, CONDW // 2 - 2:CONDW // 2]
                            link(nc.vector.tensor_copy(own, cond[:, :, :]))
                            nc.vector.tensor_tensor(cw[:, :, CONDW // 2:CONDW // 2 + 2], cond[:, :, :], own.bitcast(F32),
                                                    ALU.subtract).then_inc(sem("cond_split"), 1)
                        norm_dve(dve, link)
                        with dve.Fori(0, LAST) as i:
                            quarter(i, False)
                        quarter(LAST, True)
                        if more:
                            ada_scale(dve, L)
                        link.close()
            norm_counts()
            add(acc_taken=FT, up_taken=FT, hid_ready=FT, split_ready=UNITS * QUARTERS, h_split=KT)

        def wo_phase(name, w):
            phase(name, [2] * (D // SLAB), lambda u: cols(w, u * SLAB))

        def wo_pe(pe, name, src, ready):
            start, n, _ = phases[name]
            for u in range(n):
                has_slab(pe, start + u)
                for j in range(2):
                    g = 2 * u + j
                    start_at(pe, "acc_taken", base("acc_taken") + g - 1)
                    for k in range(KT):
                        if g == 0:
                            ready(k)
                        mm = nc.tensor.matmul(bank(j, TOK), slab[:, (start + u) % SLOTS, k, j * P:(j + 1) * P],
                                              src[:, k], start=k == 0, stop=k == KT - 1)
                    mm.then_inc(run_done, 1)

        def wo_dve(dve, name, layer):
            runs = run_after[phases[name][0] - 1]
            for g in range(KT):
                dve.wait_ge(run_done, runs + g + 1)
                residual(layer, 0, g, bank(g % 2, TOK)).then_inc(acc_taken, 1)

        def qk_pe(pe, start, n_tiles, dst, ws):
            for n in range(n_tiles + 2):
                if n < n_tiles:
                    if n % 2 == 0:
                        has_slab(pe, start + n // 2)
                    start_at(pe, "acc_taken", base("acc_taken") + n - 1)
                    for k in range(KT):
                        if n == 0:
                            has_h(pe, k)
                        at = (n % 2) * P
                        mm = nc.tensor.matmul(bank(n % 2, TOK), slab[:, (start + n // 2) % SLOTS, k, at:at + P],
                                              hT[:, k], start=k == 0, stop=k == KT - 1)
                    mm.then_inc(run_done, 1)
                if 1 <= n <= n_tiles:
                    m = n - 1
                    pe.wait_ge(sem("head_sq"), base("head_sq") + m + 1)
                    start_at(pe, "head_std", base("head_sq") + m - 1)
                    nc.tensor.matmul(bank(2 + m % 2, TOK), K["blocks"], ws["sq"][:, m % 2], start=True, stop=True)\
                        .then_inc(sem("head_sum"), 1)
                if n >= 2:
                    m = n - 2
                    pe.wait_ge(sem("head_norm"), base("head_sq") + m + 1)
                    start_at(pe, "partner_taken", base("head_sq") + m - 1)
                    nc.tensor.matmul(bank(4 + m % 2, LAT), K["swap32"], dst(m)[:, CTX:TOK], start=True, stop=True)\
                        .then_inc(sem("partner"), 1)

        def qk_act(act, start, n_tiles, ws):
            runs, hb = run_after[start - 1] if start else 0, base("head_sq")
            for n in range(n_tiles + 1):
                if n < n_tiles:
                    act.wait_ge(run_done, runs + n + 1)
                    start_at(act, "head_norm", hb + n - 1)
                    nc.scalar.activation(ws["raw"][:, n % 2], bank(n % 2, TOK), ACT.Copy).then_inc(acc_taken, 1)
                    start_at(act, "head_sum", hb + n - 1)
                    act.wait_ge(acc_taken, base("acc_taken") + n + 1)
                    nc.scalar.activation(ws["sq"][:, n % 2], ws["raw"][:, n % 2], ACT.Square)\
                        .then_inc(sem("head_sq"), 1)
                if n >= 1:
                    m = n - 1
                    act.wait_ge(sem("head_sum"), hb + m + 1)
                    start_at(act, "head_norm", hb + m - 1)
                    nc.scalar.activation(ws["rinv"][:, m % 2], bank(2 + m % 2, TOK), ACT.Sqrt, scale=1.0 / HD,
                                         bias=K["eps"]).then_inc(sem("head_std"), 1)

        def qk_dve(dve, link, n_tiles, dst, gain, ws):
            hb = base("head_sq")
            for n in range(n_tiles + 1):
                if n < n_tiles:
                    dve.wait_ge(sem("head_std"), hb + n + 1)
                    link(nc.vector.reciprocal(ws["rinv"][:, n % 2], ws["rinv"][:, n % 2]))
                    nc.vector.scalar_tensor_tensor(dst(n), ws["raw"][:, n % 2], gain(n), ws["rinv"][:, n % 2],
                                                   ALU.mult, ALU.mult).then_inc(sem("head_norm"), 1)
                if n >= 1:
                    m = n - 1
                    x = dst(m)[:, CTX:TOK]
                    dve.wait_ge(sem("partner"), hb + m + 1)
                    nc.vector.tensor_tensor(ws["turn"][:, m % 2], bank(4 + m % 2, LAT), K["sin"], ALU.mult)\
                        .then_inc(sem("partner_taken"), 1)
                    link(nc.vector.tensor_tensor(x, x, K["cos"], ALU.mult))
                    link(nc.vector.tensor_tensor(x, x, ws["turn"][:, m % 2], ALU.add))

        def v_pe(pe, start, units, g):
            for u in units:
                has_slab(pe, start + u)
                for t in range(TT):
                    start_at(pe, "acc_taken", base("acc_taken") + g - 1)
                    for k in range(KT):
                        mm = nc.tensor.matmul(bank(g % 2, SLAB), hT[:, k, t * P:(t + 1) * P],
                                              slab[:, (start + u) % SLOTS, k], start=k == 0, stop=k == KT - 1)
                    mm.then_inc(run_done, 1)
                    g += 1

        def v_act(act, start, units, g, v):
            runs = run_after[start - 1] if start else 0
            for i, u in enumerate(units):
                for t in range(TT):
                    act.wait_ge(run_done, runs + g + 1)
                    nc.scalar.activation(v[:, t, i * SLAB:(i + 1) * SLAB], bank(g % 2, SLAB), ACT.Copy)\
                        .then_inc(acc_taken, 1)
                    g += 1

        def turn_keys_pe(pe, kc, k, n, before):
            pe.wait_ge(sem("cache_in"), cache_loads[0])
            pe.wait_ge(sem("sum_done"), base("sum_done") + 1)
            pe.wait_ge(sem("std_ready"), base("sum_done") + 1)
            pe.wait_ge(sem("head_std"), base("head_sq") + before)
            for src, b0 in ((lambda c: kc[:, c * P:(c + 1) * P], 6), (lambda c: k[:, c, 0:CTX], 2)):
                for c in range(n):
                    mm = nc.tensor.transpose(bank(b0 + c // 4, 4, P)[:, c % 4], src(c), K["ident"])
                mm.then_inc(sem("keys_turned"), 1)

        cache_loads = [0]

        def turn_keys_act(act, k, kout, n):
            b = base("keys_turned")
            for i in range(2):
                act.wait_ge(sem("keys_turned"), b + i + 1)
                for q in range(0, n, 4):
                    m = min(4, n - q)
                    src = bank((6, 2)[i] + q // 4, m, P)
                    dst = k[:, q:q + m, TOK:TOK + PAST] if i == 0 else \
                        kout[:, q * P:(q + m) * P].rearrange("p (c t) -> p c t", c=m)
                    ins = nc.scalar.activation(dst, src, ACT.Copy)
            ins.then_inc(sem("kout_ready"), 1)

        def da_phases(layer):
            j = layer // 3
            phase(f"qkv{layer}", [2] * 8 + [3] * 4, lambda u: cols(I["da_wqkv"][j], u * SLAB))
            wo_phase(f"wo{layer}", I["da_wo"][j])

        def da(layer, following, room):
            j = layer // 3
            c = Carve(room)
            q, k, v, o = c(KT, TOK), c(KT, TOK + PAST), c(TT + 1, D), c(KT, TOK)
            ws = {"raw": c(2, TOK), "sq": c(2, TOK), "rinv": c(2, TOK), "turn": c(2, LAT)}
            kc, kout = c(D), c(D)
            probs, pr, prT = c(2, 2, TOK), c(2, TOK), c(2, TOK)
            neg, total, inv = c(2, 4), c(2, 2), c(2, 2)
            name = f"qkv{layer}"
            start = phases[name][0]
            n_tiles, v_units = 2 * KT, range(8, 12)
            cache_loads[0] += 32

            def dst(n):
                return q[:, n] if n < KT else k[:, n - KT, 0:TOK]

            def gain(n):
                at = 2 * j + n // KT
                return small[:, at:at + 1]

            with nc.Block() as block:
                @block.sync
                def _(sp):
                    load_phase(sp, name, f"wo{layer}")
                    sp.wait_ge(sem("kout_ready"), base("kout_ready") + 1)
                    sp.dma_start(O["new_da_k"][0, j].rearrange("t h d -> t (h d)"), kout).then_inc(sem("kv_stored"), 16)
                    sp.dma_start(O["new_da_v"][0, j].rearrange("t h d -> t (h d)"), v[:, 0])\
                        .then_inc(sem("kv_stored"), 16)

                @block.tensor
                def _(pe):
                    norm_pe(pe)
                    qk_pe(pe, start, n_tiles, dst, ws)
                    v_pe(pe, start, v_units, n_tiles)
                    turn_keys_pe(pe, kc, k, KT, n_tiles)

                @block.scalar
                def _(act):
                    act.dma_start(kc, I["cache_da_k"][0, j].rearrange("t h d -> t (h d)")).then_inc(sem("cache_in"), 16)
                    act.dma_start(v[:, TT], I["cache_da_v"][0, j].rearrange("t h d -> t (h d)"))\
                        .then_inc(sem("cache_in"), 16)
                    norm_act(act, layer, 0, in_place)
                    qk_act(act, start, n_tiles, ws)
                    v_act(act, start, v_units, n_tiles, v)
                    turn_keys_act(act, k, kout, KT)

                @block.vector
                def _(dve):
                    link = Link(dve, "dve_step")
                    norm_dve(dve, link)
                    qk_dve(dve, link, n_tiles, dst, gain, ws)
                    link.close()
            norm_counts()
            add(acc_taken=n_tiles + TT * 4, head_sq=n_tiles, keys_turned=2, kout_ready=1, kv_stored=32)

            units = [(h, t) for h in range(KT) for t in range(TT)]
            N = len(units)
            ub, eb = base("unit"), base("exp_done")

            def keys(t):
                return (slice(0, CTX), (0,)) if t == 0 else (slice(CTX, TOK + PAST), (1, 2, 3))

            with nc.Block() as block:
                @block.tensor
                def _(pe):
                    for i in range(N + 2):
                        if i < N:
                            h, t = units[i]
                            ks, vb = keys(t)
                            start_at(pe, "exp_done", eb + 2 * (i - 1))
                            for m in range(2):
                                r = slice(HD * m, HD * m + HD)
                                mm = nc.tensor.matmul(bank(2 * (i % 2) + m, P * len(vb)), q[r, h, t * P:(t + 1) * P],
                                                      k[r, h, ks], start=True, stop=True)
                            mm.then_inc(sem("scores"), 1)
                        if 1 <= i <= N:
                            u = i - 1
                            _, vb = keys(units[u][1])
                            pe.wait_ge(sem("pr_ready"), ub + u + 1)
                            start_at(pe, "prT_ready", ub + u - 1)
                            for b in range(len(vb)):
                                mm = nc.tensor.transpose(bank(4 + u % 2, TT, P)[:, b], pr[:, u % 2, b * P:(b + 1) * P],
                                                         K["ident"])
                            mm.then_inc(sem("pr_turned"), 1)
                        if i >= 2:
                            u = i - 2
                            h, t = units[u]
                            _, vb = keys(t)
                            pe.wait_ge(sem("prT_ready"), ub + u + 1)
                            if t == 0:
                                start_at(pe, "o_ready", ub // TT + h - 1)
                            for b, w in enumerate(vb):
                                mm = nc.tensor.matmul(bank(6 + h % 2, TOK)[:, t * P:(t + 1) * P],
                                                      v[:, w if w else 0, h * P:(h + 1) * P],
                                                      prT[:, u % 2, b * P:(b + 1) * P], start=b == 0, stop=b == len(vb) - 1)
                            mm.then_inc(sem("pv_done"), 1)

                @block.vector
                def _(dve):
                    link = Link(dve, "dve_step")
                    for i in range(N + 1):
                        if i < N:
                            n = P * len(keys(units[i][1])[1])
                            dve.wait_ge(sem("scores"), ub + i + 1)
                            for m in range(2):
                                ins = nc.vector.tensor_reduce(neg[:, i % 2, m:m + 1], bank(2 * (i % 2) + m, n), AX_X,
                                                              ALU.max, negate=True)
                            link(ins)
                            nc.vector.tensor_scalar(neg[:, i % 2, 2:4], neg[:, i % 2, 0:2], SCALE, None, ALU.mult)\
                                .then_inc(sem("max_ready"), 1)
                        if i >= 1:
                            u = i - 1
                            n = P * len(keys(units[u][1])[1])
                            dve.wait_ge(sem("exp_done"), eb + 2 * (u + 1))
                            link(nc.vector.reciprocal(inv[:, u % 2], total[:, u % 2]))
                            link(nc.vector.tensor_scalar(inv[:, u % 2, 1:2], inv[:, u % 2, 1:2],
                                                         lam[:, 4 * j + 2:4 * j + 3], None, ALU.mult))
                            p0, p1 = (probs[:, u % 2, m, 0:n] for m in range(2))
                            link(nc.vector.tensor_scalar(p1, p1, inv[:, u % 2, 1:2], None, ALU.mult))
                            start_at(dve, "pr_turned", ub + u - 1)
                            nc.vector.scalar_tensor_tensor(pr[:, u % 2, 0:n], p0, inv[:, u % 2, 0:1], p1, ALU.mult,
                                                           ALU.subtract).then_inc(sem("pr_ready"), 1)
                    link.close()

                @block.scalar
                def _(act):
                    for i in range(N + 2):
                        if i < N:
                            n = P * len(keys(units[i][1])[1])
                            act.wait_ge(sem("max_ready"), ub + i + 1)
                            start_at(act, "pr_ready", ub + i - 1)
                            for m in range(2):
                                nc.scalar.activation(probs[:, i % 2, m, 0:n], bank(2 * (i % 2) + m, n), ACT.Exp,
                                                     scale=SCALE, bias=neg[:, i % 2, 2 + m:3 + m],
                                                     accum_out=total[:, i % 2, m:m + 1]).then_inc(sem("exp_done"), 1)
                        if 1 <= i <= N:
                            u = i - 1
                            n = P * len(keys(units[u][1])[1])
                            act.wait_ge(sem("pr_turned"), ub + u + 1)
                            start_at(act, "pv_done", ub + u - 1)
                            nc.scalar.activation(prT[:, u % 2, 0:n], bank(4 + u % 2, n), ACT.Copy)\
                                .then_inc(sem("prT_ready"), 1)
                        if i >= 2 and units[i - 2][1] == TT - 1:
                            h = units[i - 2][0]
                            act.wait_ge(sem("pv_done"), ub + i - 1)
                            nc.scalar.activation(o[:, h], bank(6 + h % 2, TOK), ACT.Copy).then_inc(sem("o_ready"), 1)
            add(unit=N, exp_done=2 * N)

            sb_ = base("o_sq")
            with nc.Block() as block:
                @block.sync
                def _(sp):
                    load_phase(sp, f"wo{layer}", following)

                @block.tensor
                def _(pe):
                    for h in range(KT):
                        pe.wait_ge(sem("o_sq"), sb_ + h + 1)
                        start_at(pe, "o_std", sb_ + h - 1)
                        nc.tensor.matmul(bank(2 + h % 2, TOK), K["ones"], hT[:, h], start=True, stop=True)\
                            .then_inc(sem("o_sum"), 1)
                    wo_pe(pe, f"wo{layer}", o, lambda k: pe.wait_ge(sem("o_norm"), sb_ + k + 1))

                @block.scalar
                def _(act):
                    for h in range(KT):
                        nc.scalar.activation(hT[:, h], o[:, h], ACT.Square).then_inc(sem("o_sq"), 1)
                    for h in range(KT):
                        act.wait_ge(sem("o_sum"), sb_ + h + 1)
                        start_at(act, "o_norm", sb_ + h - 1)
                        nc.scalar.activation(ws["rinv"][:, h % 2], bank(2 + h % 2, TOK), ACT.Sqrt, scale=1.0 / P,
                                             bias=K["eps"]).then_inc(sem("o_std"), 1)

                @block.vector
                def _(dve):
                    link = Link(dve, "dve_step")
                    for h in range(KT):
                        dve.wait_ge(sem("o_std"), sb_ + h + 1)
                        link(nc.vector.reciprocal(ws["rinv"][:, h % 2], ws["rinv"][:, h % 2]))
                        nc.vector.scalar_tensor_tensor(o[:, h], o[:, h], small[:, 6 + j:7 + j], ws["rinv"][:, h % 2],
                                                       ALU.mult, ALU.mult).then_inc(sem("o_norm"), 1)
                    link.close()
                    wo_dve(dve, f"wo{layer}", layer)
            add(o_sq=KT, acc_taken=KT)
            stored["kv_stored"] = base("kv_stored")

        def swa_phases(layer):
            phase(f"qkv{layer}", [2] * 5 + [3], lambda u: cols(I["swa_wqkv"][0], u * SLAB))
            wo_phase(f"wo{layer}", I["swa_wo"][0])

        def swa(layer, following, room):
            c = Carve(room)
            KV = SLAB
            q, k, k2, v, o = c(KT, TOK), c(2, TOK + PAST), c(2, TOK + PAST), c(TT + 1, KV), c(KT, TOK)
            ws = {"raw": c(2, TOK), "sq": c(2, TOK), "rinv": c(2, TOK), "turn": c(2, LAT)}
            kc, kout = c(KV), c(KV)
            probs, prT = c(2, 2, TOK), c(2, 2, TOK)
            sink, nsink = c(16), c(16)
            neg, total, inv = c(2, 6), c(2, 4), c(2, 2)
            name = f"qkv{layer}"
            start = phases[name][0]
            n_tiles, v_units = KT + 2, (5,)
            cache_loads[0] += 48

            def dst(n):
                return q[:, n] if n < KT else k[:, n - KT, 0:TOK]

            def gain(n):
                at = 4 + n // KT
                return small[:, at:at + 1]

            with nc.Block() as block:
                @block.sync
                def _(sp):
                    load_phase(sp, name, f"wo{layer}")
                    sp.wait_ge(sem("kout_ready"), base("kout_ready") + 1)
                    sp.dma_start(O["new_swa_k"][0, 0].rearrange("t h d -> t (h d)"), kout)\
                        .then_inc(sem("kv_stored"), 16)
                    sp.dma_start(O["new_swa_v"][0, 0].rearrange("t h d -> t (h d)"), v[:, 0])\
                        .then_inc(sem("kv_stored"), 16)

                @block.tensor
                def _(pe):
                    norm_pe(pe)
                    qk_pe(pe, start, n_tiles, dst, ws)
                    v_pe(pe, start, v_units, n_tiles)
                    turn_keys_pe(pe, kc, k, 2, n_tiles)
                    pe.wait_ge(sem("kout_ready"), base("kout_ready") + 1)
                    pe.wait_ge(sem("keys_roped"), 1)
                    for i in range(2):
                        nc.tensor.matmul(bank(2 + i, TOK + PAST), K["swap64"], k[:, i], start=True, stop=True)\
                            .then_inc(sem("keys_swapped"), 1)

                @block.scalar
                def _(act):
                    act.dma_start(kc, I["cache_swa_k"][0, 0].rearrange("t h d -> t (h d)")).then_inc(sem("cache_in"), 16)
                    act.dma_start(v[:, TT], I["cache_swa_v"][0, 0].rearrange("t h d -> t (h d)"))\
                        .then_inc(sem("cache_in"), 16)
                    act.dma_start(sink, I["swa_sink"][0:1].to_broadcast([P, 16])).then_inc(sem("cache_in"), 16)
                    norm_act(act, layer, 0, in_place)
                    qk_act(act, start, n_tiles, ws)
                    v_act(act, start, v_units, n_tiles, v)
                    turn_keys_act(act, k, kout, 2)
                    for i in range(2):
                        act.wait_ge(sem("keys_swapped"), i + 1)
                        nc.scalar.activation(k2[:, i], bank(2 + i, TOK + PAST), ACT.Copy)

                @block.vector
                def _(dve):
                    link = Link(dve, "dve_step")
                    norm_dve(dve, link)
                    qk_dve(dve, link, n_tiles, dst, gain, ws)
                    link.close()
                    dve.wait_ge(sem("cache_in"), cache_loads[0])
                    nc.vector.tensor_scalar(nsink, sink, -1.0, None, ALU.mult).then_inc(sem("keys_roped"), 1)
            norm_counts()
            add(acc_taken=n_tiles + TT, head_sq=n_tiles, keys_turned=2, kout_ready=1, kv_stored=32)

            units = [(h, t) for h in range(KT) for t in range(TT)]
            N = len(units)
            ub, eb = base("unit"), base("exp_done")

            def keys(t):
                return (slice(0, CTX), (0,)) if t == 0 else (slice(CTX, TOK + PAST), (1, 2, 3))

            with nc.Block() as block:
                @block.tensor
                def _(pe):
                    for i in range(N + 2):
                        if i < N:
                            h, t = units[i]
                            ks, vb = keys(t)
                            g = h // 2
                            start_at(pe, "max_ready", ub + i - 1)
                            for m in range(2):
                                r = slice(HD * m, HD * m + HD)
                                keys_at = (k if g % 2 == m else k2)[r, g // 2, ks]
                                mm = nc.tensor.matmul(bank(2 * (i % 2) + m, P * len(vb)), q[r, h, t * P:(t + 1) * P],
                                                      keys_at, start=True, stop=True)
                            mm.then_inc(sem("scores"), 1)
                        if 1 <= i <= N:
                            u = i - 1
                            _, vb = keys(units[u][1])
                            pe.wait_ge(sem("pr_ready"), ub + u + 1)
                            start_at(pe, "prT_ready", ub + u)
                            for m in range(2):
                                for b in range(len(vb)):
                                    mm = nc.tensor.transpose(bank(4 + m, TT, P)[:, b],
                                                             probs[:, u % 2, m, b * P:(b + 1) * P], K["ident"])
                            mm.then_inc(sem("pr_turned"), 1)
                        if i >= 2:
                            u = i - 2
                            h, t = units[u]
                            _, vb = keys(t)
                            g = h // 2
                            pe.wait_ge(sem("prT_ready"), ub + u + 1)
                            if t == 0:
                                start_at(pe, "o_ready", ub // TT + h - 1)
                            for m in range(2):
                                for b, w in enumerate(vb):
                                    mm = nc.tensor.matmul(psum[HD * m:HD * m + HD, 6 + h % 2, t * P:(t + 1) * P],
                                                          v[:, w, g * HD:(g + 1) * HD],
                                                          prT[:, u % 2, m, b * P:(b + 1) * P],
                                                          start=b == 0, stop=b == len(vb) - 1)
                            mm.then_inc(sem("pv_done"), 1)

                @block.vector
                def _(dve):
                    link = Link(dve, "dve_step")
                    for i in range(N + 1):
                        if i < N:
                            h, t = units[i]
                            n = P * len(keys(t)[1])
                            x = neg[:, i % 2]
                            dve.wait_ge(sem("scores"), ub + i + 1)
                            start_at(dve, "pr_turned", ub + i - 1)
                            for m in range(2):
                                s = bank(2 * (i % 2) + m, n)
                                if t == 0:
                                    ins = nc.vector.tensor_scalar(probs[:, i % 2, m, 0:n], s, SCALE, None, ALU.mult)
                                else:
                                    ins = nc.vector.scalar_tensor_tensor(probs[:, i % 2, m], s, SCALE, band[:, t - 1],
                                                                         ALU.mult, ALU.add)
                            link(ins)
                            link(nc.vector.tensor_reduce(x[:, 0:2], probs[:, i % 2, :, 0:n], AX_X, ALU.max, negate=True))
                            link(nc.vector.tensor_tensor(x[:, 2:4], x[:, 0:2], nsink[:, 2 * h:2 * h + 2], ALU.min))
                            nc.vector.tensor_tensor(x[:, 4:6], x[:, 2:4], sink[:, 2 * h:2 * h + 2], ALU.add)\
                                .then_inc(sem("max_ready"), 1)
                        if i >= 1:
                            u = i - 1
                            n = P * len(keys(units[u][1])[1])
                            dve.wait_ge(sem("exp_done"), eb + 3 * (u + 1))
                            link(nc.vector.tensor_tensor(total[:, u % 2, 0:2], total[:, u % 2, 0:2],
                                                         total[:, u % 2, 2:4], ALU.add))
                            link(nc.vector.reciprocal(inv[:, u % 2], total[:, u % 2, 0:2]))
                            for m in range(2):
                                p = probs[:, u % 2, m, 0:n]
                                ins = nc.vector.tensor_scalar(p, p, inv[:, u % 2, m:m + 1], None, ALU.mult)
                            ins.then_inc(sem("pr_ready"), 1)
                    link.close()

                @block.scalar
                def _(act):
                    for i in range(N + 2):
                        if i < N:
                            n = P * len(keys(units[i][1])[1])
                            x = neg[:, i % 2]
                            act.wait_ge(sem("max_ready"), ub + i + 1)
                            start_at(act, "pr_ready", ub + i - 1)
                            for m in range(2):
                                p = probs[:, i % 2, m, 0:n]
                                nc.scalar.activation(p, p, ACT.Exp, bias=x[:, 2 + m:3 + m],
                                                     accum_out=total[:, i % 2, m:m + 1]).then_inc(sem("exp_done"), 1)
                            nc.scalar.activation(total[:, i % 2, 2:4], x[:, 4:6], ACT.Exp).then_inc(sem("exp_done"), 1)
                        if 1 <= i <= N:
                            u = i - 1
                            n = P * len(keys(units[u][1])[1])
                            act.wait_ge(sem("pr_turned"), ub + u + 1)
                            start_at(act, "pv_done", ub + u - 1)
                            nc.scalar.activation(prT[:, u % 2, :, 0:n], psum[:, 4:6, 0:n], ACT.Copy)\
                                .then_inc(sem("prT_ready"), 1)
                        if i >= 2 and units[i - 2][1] == TT - 1:
                            h = units[i - 2][0]
                            act.wait_ge(sem("pv_done"), ub + i - 1)
                            nc.scalar.activation(o[:, h], bank(6 + h % 2, TOK), ACT.Copy).then_inc(sem("o_ready"), 1)
            add(unit=N, exp_done=3 * N)

            with nc.Block() as block:
                @block.sync
                def _(sp):
                    load_phase(sp, f"wo{layer}", following)

                @block.tensor
                def _(pe):
                    wo_pe(pe, f"wo{layer}", o, lambda k: None)

                @block.vector
                def _(dve):
                    wo_dve(dve, f"wo{layer}", layer)
            add(acc_taken=KT)
            stored["kv_stored"] = base("kv_stored")

        V_MU, V_W0, V_A0, V_KK, V_KA, V_RK, V_LNW, V_LNB, V_1KA = 0, 6, 8, 10, 11, 12, 13, 14, 15

        def flat3(ap):
            return ap.rearrange("a v k -> (a v) k")

        S_NEW = {(z, s): 2 * s + z + 1 for z in range(2) for s in range(3)}
        DSTEPS, PSTEPS = 17, 5

        def step_loads(sp, j, stage_in):
            if j == 0:
                sp.wait_ge(run_done, run_after[phases["wo1"][0] - 1])
                sp.wait_ge(sem("stage_zero"), 1)
            else:
                sp.wait_ge(sem("proj"), j * 8)
                sp.wait_ge(sem("s0_turned"), j * 2)
            for i, w in enumerate((I["rwkv_w2"][0].rearrange("z r d -> (z r) d"),
                                   I["rwkv_a2"][0].rearrange("z r d -> (z r) d"), I["rwkv_g2"][0])):
                sp.dma_start(slab[:, 3, i, 0:P], w[:, bass.ds(j * P, P)]).then_inc(sem("l_in"), 16)
            for m in (1, 0, 2):
                sp.dma_start(slab[:, m, :, 0:P],
                             I["rwkv_wrkv"][0, m].rearrange("(k p) n -> p k n", p=P)[:, :, bass.ds(j * P, P)])\
                    .then_inc(sem("w_in"), 16)
            for z in range(2):
                for hh in range(2):
                    r = slice(64 * hh, 64 * hh + 64)
                    sp.dma_start(stage_in[r, z, r], flat3(I["state_rwkv"][0, 0, z, bass.ds(j * 2 + hh, 1)]))\
                        .then_inc(sem("state_in"), 16)

        def rwkv_phases(layer):
            wo_phase(f"wo{layer}", I["rwkv_wo"][0])

        def rwkv(layer, following, room):
            c = Carve(room)
            xs = c(3, KT, TOK)
            mids = c(3, TOK)
            stage_in, stage_out, S = c(2, P), c(2, P), c(2, 2, P)
            shared = c.at
            PAD = TOK + 4
            hP, mixed, delta, w_mid = c(KT, PAD), c(2, 3, TOK), c(2, TOK), c(3, KT, P)
            PADS = (0, CTX + 2)

            with nc.Block() as block:
                @block.gpsimd
                def _(pool):
                    for at in (0, CTX + 1, CTX + 2, PAD - 1):
                        ins = nc.gpsimd.memset(hP[:, :, at:at + 1], 0.0)
                    ins.then_inc(sem("pads_zero"), 1)
                    nc.gpsimd.memset(stage_in, 0.0).then_inc(sem("stage_zero"), 1)
                    nc.gpsimd.memset(S, 0.0)

                @block.scalar
                def _(act):
                    for i, w in enumerate((I["rwkv_w1"][0], I["rwkv_a1"][0])):
                        for z in range(2):
                            act.dma_start(w_mid[:, i, :, 64 * z:64 * z + 64], w[z].rearrange("(k p) r -> p k r", p=P))\
                                .then_inc(sem("w_mid_in"), 16)
                    act.dma_start(w_mid[:, 2], I["rwkv_g1"][0].rearrange("(k p) r -> p k r", p=P))\
                        .then_inc(sem("w_mid_in"), 16)
                    norm_act(act, layer, 0, lambda k, g: hP[:, k, PADS[g] + 1:PADS[g] + 1 + (CTX, LAT)[g]])
                    act.wait_ge(sem("mids_done"), 1)
                    for i, f in enumerate((ACT.Tanh, ACT.Copy, ACT.Sigmoid)):
                        ins = nc.scalar.activation(mids[:, i], bank(2 + i, TOK), f)
                    ins.then_inc(sem("tile_done"), 1)

                @block.vector
                def _(dve):
                    link = Link(dve, "dve_step")
                    norm_dve(dve, link)
                    dve.wait_ge(sem("pads_zero"), 1)
                    for k in range(KT):
                        dve.wait_ge(sem("h_ready"), base("sq_ready") + k + 1)
                        d = delta[:, k % 2]
                        for g, t in GROUPS:
                            n = t.stop - t.start
                            ins = nc.vector.tensor_tensor(d[:, t], hP[:, k, PADS[g]:PADS[g] + n],
                                                          hP[:, k, PADS[g] + 2:PADS[g] + 2 + n], ALU.add)
                        link(ins)
                        for g, t in GROUPS:
                            n = t.stop - t.start
                            ins = nc.vector.scalar_tensor_tensor(d[:, t], d[:, t], 0.5, hP[:, k, PADS[g] + 1:PADS[g] + 1 + n],
                                                                 ALU.mult, ALU.subtract)
                        link(ins)
                        if k >= 2:
                            dve.wait_ge(sem("mix_used"), k - 1)
                        for m in (3, 4, 5, 0, 1, 2):
                            dst = xs[:, m, k] if m < 3 else mixed[:, k % 2, m - 3]
                            for g, t in GROUPS:
                                n = t.stop - t.start
                                ins = nc.vector.scalar_tensor_tensor(
                                    dst[:, t], d[:, t], vecs[:, (V_MU + m) * KT + k:(V_MU + m) * KT + k + 1],
                                    hP[:, k, PADS[g] + 1:PADS[g] + 1 + n], ALU.mult, ALU.add)
                            if m == 5:
                                ins.then_inc(sem("mix_ready"), 1)
                    link.close()

                @block.tensor
                def _(pe):
                    norm_pe(pe)
                    pe.wait_ge(sem("w_mid_in"), 80)
                    for k in range(KT):
                        pe.wait_ge(sem("mix_ready"), k + 1)
                        for i in range(3):
                            mm = nc.tensor.matmul(bank(2 + i, TOK), w_mid[:, i, k], mixed[:, k % 2, i],
                                                  start=k == 0, stop=k == KT - 1)
                        mm.then_inc(sem("mix_used" if k < KT - 1 else "mids_done"), 1)

                @block.sync
                def _(sp):
                    step_loads(sp, 0, stage_in)
            norm_counts()

            c.at = shared
            spare = Carve(ada_slab[:, :, :, :].rearrange("p s k n -> p (s k n)"))
            rT, kT, vtok, vT, gT, kn, bonus = c(TOK), c(TOK), c(TT, P), c(TOK), c(TOK), c(TOK), c(TOK)
            par = c(16)
            sq, inv, yT, tmp = c(TOK), c(TOK), c(TOK), c(TOK)
            decay, rate, kd = c(2, TOK), c(2, TOK), c(2, TOK)
            cum = c(2, TOK)
            pp, pi = c(2, NCH, CH + 1), c(2, TOK)
            AR, bT, kTil = c(2, NCH, 2, CH), c(2, TOK), c(2, TOK)
            LB, MC = spare(2, 6, 2 * CH), spare(2, 6, 2 * CH)
            T, TTr, X = c(2, 6, CH), c(2, 6, CH), c(2, 6, CH)
            LM = spare(2, 2, 6, CH)
            tok = spare(2, 2, TT, P)
            R, U = c(2, 2 * P), c(2, 2 * P)
            fresh = c(2, 2, P)

            def own(ap):
                return ap.rearrange("p (c t) -> p c t", c=NCH)

            PER = dict(raw=9, tile_done=1, proj=8, pj=1, kk_sum=1, kk_sq=1, kk_std=1, kk_max=1, v_turned=1, s0_turned=2,
                       s0_ready=2, scan=2, powers=4, ar_ready=2, r_ready=2, bt_ready=2, kt_ready=2, kd_ready=2,
                       prod1=2, prod2=2, low=2, lb_ready=2, mc_ready=2, t_ready=2, tt_ready=2, lm_ready=10,
                       x_done=10, x_ready=10, inv_done=10, inv_ready=10, tok_turned=2, tok_ready=2,
                       r_done=8, r_in=8, u_done=8, u_in=8, s_done=8, s_new=6, y_in=1, y_sum=1, mean=1, yc=1, yc_sq=1,
                       var=1, gn_std=1, bonus_in=1, bonus_sum=1, fin_turned=1, fin_ready=1, zero=1, bb=2,
                       state_in=64, state_out=64, w_in=48, l_in=48, dstep=0, pstep=0)

            class Step:

                def __init__(self, eng, j):
                    self.eng, self.j, self.made = eng, j, {}

                def wait(self, name, k, back=0):
                    v = self.j * PER[name] + (k + START.get(name, 0) - back * PER[name])
                    self.eng.wait_ge(sem(name), v)

                def inc(self, name, ins):
                    self.made[name] = self.made.get(name, 0) + 1
                    ins.then_inc(sem(name), 1)

                def link(self, name, ins):
                    self.inc(name, ins)
                    self.wait(name, self.made[name])

                def close(self):
                    for n, m in self.made.items():
                        assert m == PER[n], (n, m, PER[n])

            START = {"tile_done": 1}
            PER["dstep"], PER["pstep"] = DSTEPS, PSTEPS

            def chunks(z, s):
                lat = (0, CTX // CH + s if z == 0 else NCH - 1 - s)
                return [lat] + ([(1, s if z == 0 else CTX // CH - 1 - s)] if s < 2 else [])

            def half(z, s):
                cp = s % 2 if z == 0 else 1 - s % 2
                return slice(CH * cp, CH * cp + CH)

            idx = [(hh, tt) for hh in range(2) for tt in range(TT)]

            with nc.Block() as block:
                @block.sync
                def _(sp):
                    sp.wait_ge(sem("proj"), PER["proj"])
                    for j in range(1, KT):
                        step_loads(sp, j, stage_in)
                    sp.wait_ge(sem("proj"), KT * PER["proj"])
                    load_first(sp, f"wo{layer}")

                @block.tensor
                def _(pe):
                    for j in range(KT):
                        st = Step(pe, j)
                        st.wait("tile_done", 0)
                        st.wait("l_in", 48)
                        for i, (kind, z, b) in enumerate(((0, 0, 2), (0, 1, 5), (1, 0, 3), (1, 1, 6), (2, 0, 7))):
                            r = slice(0, P) if kind == 2 else slice(64 * z, 64 * z + 64)
                            st.inc("proj", nc.tensor.matmul(bank(b, TOK), slab[r, 3, kind, 0:P], mids[r, kind],
                                                            start=True, stop=True))
                        st.wait("w_in", 48)
                        for m, b in ((1, 1), (0, 0)):
                            for k in range(KT):
                                mm = nc.tensor.matmul(bank(b, TOK), slab[:, m, k, 0:P], xs[:, m, k],
                                                      start=k == 0, stop=k == KT - 1)
                            st.inc("proj", mm)
                        for t in range(TT):
                            for k in range(KT):
                                mm = nc.tensor.matmul(bank(4, TT, P)[:, t], xs[:, 2, k, t * P:(t + 1) * P],
                                                      slab[:, 2, k, 0:P], start=k == 0, stop=k == KT - 1)
                        st.inc("proj", mm)
                        st.wait("state_in", 64)
                        for z in range(2):
                            st.wait("raw", 4)
                            st.inc("s0_turned", nc.tensor.transpose(bank((2, 6)[z], P), stage_in[:, z], K["ident"]))
                        st.wait("kk_sq", 1)
                        st.wait("raw", 5)
                        st.inc("kk_sum", nc.tensor.matmul(bank(1, TOK), K["blocks"], sq, start=True, stop=True))
                        st.wait("raw", 8)
                        for t in range(TT):
                            mm = nc.tensor.transpose(bank(0, TT, P)[:, t], vtok[:, t], K["ident"])
                        st.inc("v_turned", mm)
                        for z in range(2):
                            st.wait("raw", 9)
                            st.wait("kk_max", 1)
                            st.wait("s0_ready", 2)
                            st.wait("zero", 1)
                            st.wait("bt_ready", z + 1)
                            st.wait("ar_ready", z + 1)
                            st.wait("r_ready", z + 1)
                            for half_, (name, src, b) in enumerate((("prod1", bT, 0), ("prod2", kTil, 2))):
                                if half_:
                                    st.wait("kt_ready", z + 1)
                                for hh in range(2):
                                    r = slice(64 * hh, 64 * hh + 64)
                                    for ch in range(NCH):
                                        q = slice(CH * (ch % 2), CH * (ch % 2) + CH)
                                        at = (ch // 2) * P
                                        mm = nc.tensor.matmul(psum[q, 4 * z + b + hh, at:at + P],
                                                              src[r, z, ch * CH:(ch + 1) * CH],
                                                              AR[r, z, ch].rearrange("p a t -> p (a t)"),
                                                              start=True, stop=True)
                                st.inc(name, mm)
                        for z in range(2):
                            st.wait("lb_ready", z + 1)
                            for hh in range(2):
                                r = slice(64 * hh, 64 * hh + 64)
                                for ch in range(NCH):
                                    q = slice(CH * (ch % 2), CH * (ch % 2) + CH)
                                    at = (ch // 2) * CH
                                    mm = nc.tensor.matmul(psum[q, 4 * z + hh, at:at + CH], AR[r, z, ch, 0],
                                                          bT[r, z, ch * CH:(ch + 1) * CH], start=True, stop=True)
                            st.inc("low", mm)
                        for z in range(2):
                            st.wait("mc_ready", z + 1)
                            for i, src in enumerate((bT, kTil)):
                                for t in range(TT):
                                    mm = nc.tensor.transpose(bank(4 * z + 2 + i, TT, P)[:, t],
                                                             src[:, z, t * P:(t + 1) * P], K["ident"])
                            st.inc("tok_turned", mm)
                        for n in range(1, LEVELS):
                            for z in range(2):
                                m = 2 * (n - 1) + z + 1
                                if n == 1:
                                    st.wait("t_ready", z + 1)
                                    st.wait("tt_ready", z + 1)
                                else:
                                    st.wait("inv_ready", m - 2)
                                    st.wait("x_ready", m - 2)
                                st.wait("lm_ready", m)
                                for i in range(6):
                                    for cp in range(2):
                                        q = slice(CH * cp, CH * cp + CH)
                                        mm = nc.tensor.matmul(psum[q, 4 * z, i * CH:(i + 1) * CH], LM[q, z, n % 2, i],
                                                              T[q, z, i], start=True, stop=True)
                                st.inc("x_done", mm)
                            for z in range(2):
                                m = 2 * (n - 1) + z + 1
                                st.wait("x_ready", m)
                                if n == 1:
                                    st.wait("tok_ready", z + 1)
                                for i in range(6):
                                    for cp in range(2):
                                        q = slice(CH * cp, CH * cp + CH)
                                        if n < LEVELS - 1:
                                            nc.tensor.matmul(psum[q, 4 * z + 2, i * CH:(i + 1) * CH], TTr[q, z, i],
                                                             X[q, z, i], start=True, stop=True)
                                        mm = nc.tensor.matmul(psum[q, 4 * z + 1, i * CH:(i + 1) * CH], X[q, z, i],
                                                              TTr[q, z, i], start=True, stop=True)
                                st.inc("inv_done", mm)
                        new = [0, 0]
                        for s in range(4):
                            for z in range(2):
                                q = half(z, s)
                                st.wait("x_ready", 9 + z)
                                if s:
                                    st.wait("s_new", S_NEW[(z, s - 1)])
                                    st.wait("r_in", 2 * (s - 1) + z + 1)
                                for stream, ch in chunks(z, s):
                                    at = stream * P
                                    nc.tensor.matmul(psum[q, 4 * z, at:at + P], AR[:, z, ch, 0], S[:, z, stream],
                                                     start=True, stop=False)
                                    for hh in range(2):
                                        mm = nc.tensor.matmul(psum[q, 4 * z, at + 64 * hh:at + 64 * hh + 64],
                                                              MC[q, z, 3 * hh + ch // 2, 0:CH],
                                                              vtok[q, ch // 2, 64 * hh:64 * hh + 64],
                                                              start=False, stop=hh == 1)
                                st.inc("r_done", mm)
                            for z in range(2):
                                q = half(z, s)
                                st.wait("r_in", 2 * s + z + 1)
                                st.wait("inv_ready", 9 + z)
                                if s:
                                    st.wait("u_in", 2 * (s - 1) + z + 1)
                                for stream, ch in chunks(z, s):
                                    for hh in range(2):
                                        at = stream * P + 64 * hh
                                        mm = nc.tensor.matmul(psum[q, 4 * z + 1, at:at + 64],
                                                              TTr[q, z, 3 * hh + ch // 2], R[q, z, at:at + 64],
                                                              start=True, stop=True)
                                st.inc("u_done", mm)
                            for z in range(2):
                                q = half(z, s)
                                st.wait("u_in", 2 * s + z + 1)
                                for stream, ch in chunks(z, s):
                                    t, at = ch // 2, ch * CH
                                    nc.tensor.matmul(psum[:, 4 * z + 3, at:at + CH], S[:, z, stream], AR[:, z, ch, 1],
                                                     start=True, stop=False)
                                    for hh in range(2):
                                        r = slice(64 * hh, 64 * hh + 64)
                                        a2 = stream * P + 64 * hh
                                        nc.tensor.matmul(psum[r, 4 * z + 3, at:at + CH], U[q, z, a2:a2 + 64],
                                                         LB[q, z, 3 * hh + t, CH:2 * CH], start=False, stop=False)
                                        mm = nc.tensor.matmul(psum[r, 4 * z + 3, at:at + CH],
                                                              vtok[q, t, 64 * hh:64 * hh + 64],
                                                              MC[q, z, 3 * hh + t, CH:2 * CH], start=False,
                                                              stop=True)
                                    if s < 3:
                                        a2 = stream * P
                                        nc.tensor.matmul(psum[:, 4 * z + 2, a2:a2 + P], tok[q, z, 0, t],
                                                         U[q, z, a2:a2 + P], start=True, stop=False)
                                        mm = nc.tensor.matmul(psum[:, 4 * z + 2, a2:a2 + P], tok[q, z, 1, t],
                                                              vtok[q, t], start=False, stop=True)
                                st.inc("s_done", mm)
                        st.wait("y_in", 1)
                        st.inc("mean", nc.tensor.matmul(bank(0, TOK), K["blocks"], yT, start=True, stop=True))
                        st.wait("bonus_in", 1)
                        st.inc("bonus_sum", nc.tensor.matmul(bank(4, TOK), K["blocks"], bonus, start=True, stop=True))
                        st.wait("s_new", 6)
                        for z in range(2):
                            mm = nc.tensor.transpose(bank(2, 2, P)[:, z], S[:, z, 1], K["ident"])
                        st.inc("fin_turned", mm)
                        st.wait("yc_sq", 1)
                        st.inc("var", nc.tensor.matmul(bank(1, TOK), K["blocks"], sq, start=True, stop=True))
                        st.close()

                @block.scalar
                def _(act):
                    act.wait_ge(sem("ends_one"), 1)
                    for j in range(KT):
                        st = Step(act, j)
                        st.wait("tile_done", 0)
                        st.wait("pj", 1)
                        for i, (dst, v, b) in enumerate(((decay, V_W0, 2), (decay, V_W0, 5), (rate, V_A0, 3), (rate, V_A0, 6))):
                            z = i % 2
                            st.wait("proj", i + 1)
                            st.inc("raw", nc.scalar.activation(dst[:, z], bank(b, TOK), ACT.Sigmoid,
                                                               bias=par[:, v + z:v + z + 1]))
                        st.wait("proj", 6)
                        st.inc("kk_sq", nc.scalar.activation(sq, bank(1, TOK), ACT.Square, scale=par[:, V_KK:V_KK + 1]))
                        st.inc("raw", nc.scalar.activation(kT, bank(1, TOK), ACT.Copy))
                        st.inc("raw", nc.scalar.activation(gT, bank(7, TOK), ACT.Copy))
                        st.wait("proj", 7)
                        st.inc("raw", nc.scalar.activation(rT, bank(0, TOK), ACT.Copy))
                        for z in range(2):
                            st.wait("scan", z + 1)
                            st.inc("powers", nc.scalar.activation(pp[:, z, :, 1 - z:CH + 1 - z], own(cum[:, z]), ACT.Exp,
                                                                  scale=-DECAY))
                            st.inc("powers", nc.scalar.activation(pi[:, z], cum[:, z], ACT.Exp, scale=DECAY))
                        st.wait("kk_max", 1)
                        st.inc("kk_std", nc.scalar.activation(inv, inv, ACT.Sqrt))
                        st.wait("proj", 8)
                        st.inc("raw", nc.scalar.activation(vtok.rearrange("p t c -> p (t c)"), bank(4, TOK), ACT.Copy))
                        for z in range(2):
                            st.wait("s0_turned", z + 1)
                            st.inc("s0_ready", nc.scalar.activation(S[:, z, 0], bank((2, 6)[z], P), ACT.Copy))
                        st.wait("v_turned", 1)
                        st.inc("raw", nc.scalar.activation(vT, bank(0, TOK), ACT.Copy))
                        for z in range(2):
                            st.wait("tok_turned", z + 1)
                            st.inc("tok_ready", nc.scalar.activation(
                                tok[:, z].rearrange("p a t c -> p a (t c)"), psum[:, 4 * z + 2:4 * z + 4, 0:TOK], ACT.Copy))
                        for n in range(1, LEVELS):
                            for z in range(2):
                                m = 2 * (n - 1) + z + 1
                                st.wait("x_done", m)
                                if n > 1:
                                    st.wait("inv_done", m - 2)
                                st.inc("x_ready", nc.scalar.activation(X[:, z].rearrange("p i t -> p (i t)"),
                                                                       bank(4 * z, TOK), ACT.Copy))
                        for s in range(4):
                            for z in range(2):
                                q = half(z, s)
                                n = P * len(chunks(z, s))
                                st.wait("r_done", 2 * s + z + 1)
                                if s:
                                    st.wait("u_done", 2 * (s - 1) + z + 1)
                                st.inc("r_in", nc.scalar.activation(R[q, z, 0:n], psum[q, 4 * z, 0:n], ACT.Copy))
                            for z in range(2):
                                q = half(z, s)
                                n = P * len(chunks(z, s))
                                st.wait("u_done", 2 * s + z + 1)
                                if s:
                                    st.wait("s_done", 2 * (s - 1) + z + 1)
                                st.inc("u_in", nc.scalar.activation(U[q, z, 0:n], psum[q, 4 * z + 1, 0:n], ACT.Copy))
                        st.wait("s_done", 8)
                        st.inc("y_sum", nc.scalar.activation(yT, bank(3, TOK), ACT.Copy))
                        st.wait("yc", 1)
                        st.inc("yc_sq", nc.scalar.activation(sq, tmp, ACT.Square))
                        st.wait("fin_turned", 1)
                        st.inc("fin_ready", nc.scalar.activation(stage_out.rearrange("p z c -> p (z c)"), bank(2, 2 * P),
                                                                 ACT.Copy))
                        st.wait("var", 1)
                        st.inc("gn_std", nc.scalar.activation(inv, bank(1, TOK), ACT.Sqrt, scale=1.0 / HD,
                                                              bias=K["gn_eps"]))
                        st.close()
                        act.wait_ge(sem("fin_ready"), j + 1)
                        for z in range(2):
                            for hh in range(2):
                                r = slice(64 * hh, 64 * hh + 64)
                                act.dma_start(flat3(O["new_state_rwkv"][0, 0, z, bass.ds(j * 2 + hh, 1)]),
                                              stage_out[r, z, r]).then_inc(sem("state_out"), 16)
                        act.wait_ge(sem("state_out"), j * 64 + 64)

                @block.gpsimd
                def _(pool):
                    nc.gpsimd.memset(pp, 1.0).then_inc(sem("ends_one"), 1)
                    vec3 = vecs[:, :].rearrange("p (v k) -> p v k", k=KT)
                    for j in range(KT):
                        st = Step(pool, j)
                        st.wait("tile_done", 0)
                        st.link("pstep", nc.gpsimd.tensor_copy(par[:, 0:15], vec3[:, :, bass.ds(j, 1)].rearrange("p v k -> p (v k)")))
                        st.inc("pj", nc.gpsimd.tensor_scalar(par[:, V_1KA:V_1KA + 1], par[:, V_KA:V_KA + 1], -1.0, 1.0,
                                                             ALU.mult, ALU.add))
                        st.inc("zero", nc.gpsimd.memset(S[:, :, 1], 0.0))
                        st.wait("raw", 5)
                        for z in range(2):
                            st.wait("bb", z + 1)
                            st.inc("kd_ready", nc.gpsimd.tensor_tensor(kd[:, z], kT, kd[:, z], ALU.mult))
                        st.wait("raw", 7)
                        for z in range(2):
                            st.wait("powers", 2 * z + 1)
                            st.inc("r_ready", nc.gpsimd.tensor_tensor(AR[:, z, :, 1], own(rT), pp[:, z, :, 1 - z:CH + 1 - z],
                                                                      ALU.mult))
                        eye = over(K["eye64"], 6)
                        for z in range(2):
                            st.wait("lb_ready", z + 1)
                            st.link("pstep", nc.gpsimd.tensor_tensor(TTr[:, z], LB[:, z, :, 0:CH], over(levels[:, z, 0], 6),
                                                                     ALU.mult))
                            st.inc("tt_ready", nc.gpsimd.tensor_tensor(TTr[:, z], TTr[:, z], eye, ALU.add))
                            st.inc("lm_ready", nc.gpsimd.tensor_tensor(LM[:, z, 1], LB[:, z, :, 0:CH],
                                                                       over(levels[:, z, 1], 6), ALU.mult))
                        for n in range(2, LEVELS):
                            for z in range(2):
                                if n >= 3:
                                    st.wait("x_done", 2 * (n - 3) + z + 1)
                                st.inc("lm_ready", nc.gpsimd.tensor_tensor(LM[:, z, n % 2], LB[:, z, :, 0:CH],
                                                                           over(levels[:, z, n], 6), ALU.mult))
                        st.link("pstep", nc.gpsimd.tensor_tensor(bonus, kd[:, 0], kd[:, 1], ALU.add))
                        st.link("pstep", nc.gpsimd.tensor_tensor(bonus, bonus, rT, ALU.mult))
                        st.inc("bonus_in", nc.gpsimd.tensor_scalar(bonus, bonus, par[:, V_RK:V_RK + 1], None, ALU.mult))
                        st.close()

                @block.vector
                def _(dve):
                    for j in range(KT):
                        st = Step(dve, j)

                        def link(ins):
                            st.link("dstep", ins)

                        st.wait("pj", 1)
                        for z in range(2):
                            st.wait("raw", z + 1)
                            rev = slice(None) if z == 0 else slice(None, None, -1)
                            st.inc("scan", nc.vector.tensor_tensor_scan(cum[:, z, rev], K["restart"], decay[:, z, rev], 0.0,
                                                                        ALU.mult, ALU.add))
                        for z in range(2):
                            st.wait("raw", 3 + z)
                            st.inc("bb", nc.vector.tensor_scalar(kd[:, z], rate[:, z], par[:, V_KA:V_KA + 1],
                                                                 par[:, V_1KA:V_1KA + 1], ALU.mult, ALU.add))
                        st.wait("kk_sum", 1)
                        st.inc("kk_max", nc.vector.tensor_scalar(inv, bank(1, TOK), 1e-24, None, ALU.max))
                        st.wait("kk_std", 1)
                        link(nc.vector.reciprocal(inv, inv))
                        st.wait("raw", 5)
                        link(nc.vector.scalar_tensor_tensor(kn, kT, par[:, V_KK:V_KK + 1], inv, ALU.mult, ALU.mult))
                        for z in range(2):
                            link(nc.vector.tensor_tensor(rate[:, z], rate[:, z], kn, ALU.mult))
                            st.wait("powers", 2 * z + 2)
                            st.inc("bt_ready", nc.vector.tensor_tensor(bT[:, z], rate[:, z], pi[:, z], ALU.mult))
                            before = pp[:, z, :, 0:CH] if z == 0 else pp[:, z, :, 1:CH + 1]
                            st.inc("ar_ready", nc.vector.scalar_tensor_tensor(AR[:, z, :, 0], own(kn), -1.0, before,
                                                                              ALU.mult, ALU.mult))
                            st.wait("kd_ready", z + 1)
                            st.inc("kt_ready", nc.vector.tensor_tensor(kTil[:, z], kd[:, z], pi[:, z], ALU.mult))
                        for z in range(2):
                            for name, dst, b, prod in (("lb_ready", LB, 0, "prod1"), ("mc_ready", MC, 2, "prod2")):
                                st.wait(prod, z + 1)
                                src = psum[:, 4 * z + b:4 * z + b + 2, 0:TOK].rearrange("p h (t c) -> p h t c", t=TT)
                                m = causal[:, z].unsqueeze(1).unsqueeze(1).to_broadcast([P, 2, TT, 2 * CH])
                                st.inc(name, nc.vector.tensor_tensor(
                                    dst[:, z].rearrange("p (h t) c -> p h t c", h=2), src, m, ALU.mult))
                        for z in range(2):
                            st.wait("low", z + 1)
                            src = psum[:, 4 * z:4 * z + 2, 0:TT * CH].rearrange("p h (t c) -> p h t c", t=TT)
                            m = first[:, z].unsqueeze(1).unsqueeze(1).to_broadcast([P, 2, TT, CH])
                            link(nc.vector.tensor_tensor(T[:, z].rearrange("p (h t) c -> p h t c", h=2), src, m, ALU.mult))
                            st.inc("t_ready", nc.vector.tensor_tensor(T[:, z], T[:, z], over(K["eye64"], 6), ALU.add))
                        st.wait("t_ready", 2)
                        for n in range(1, LEVELS):
                            for z in range(2):
                                st.wait("inv_done", 2 * (n - 1) + z + 1)
                                if n == 1:
                                    st.wait("tt_ready", z + 1)
                                else:
                                    st.wait("inv_ready", 2 * (n - 2) + z + 1)
                                if n < LEVELS - 1:
                                    t = T[:, z].rearrange("p i t -> p (i t)")
                                    nc.vector.tensor_tensor(t, bank(4 * z + 2, TOK), t, ALU.add)
                                t = TTr[:, z].rearrange("p i t -> p (i t)")
                                st.inc("inv_ready", nc.vector.tensor_tensor(t, bank(4 * z + 1, TOK), t, ALU.add))
                        for s in range(3):
                            for z in range(2):
                                st.wait("s_done", 2 * s + z + 1)
                                cs = chunks(z, s)
                                end = CH if z == 0 else 0
                                for stream, ch in cs:
                                    pc = pp[:, z, ch, end:end + 1]
                                    ins = nc.vector.scalar_tensor_tensor(fresh[:, z, stream], psum[:, 4 * z + 2, stream * P:(stream + 1) * P],
                                                                         pc, K["blocks"], ALU.mult, ALU.mult)
                                link(ins)
                                for stream, ch in cs:
                                    pc = pp[:, z, ch, end:end + 1]
                                    ins = nc.vector.scalar_tensor_tensor(S[:, z, stream], S[:, z, stream], pc, fresh[:, z, stream],
                                                                         ALU.mult, ALU.add)
                                st.inc("s_new", ins)
                        st.wait("s_done", 8)
                        st.wait("y_sum", 1)
                        st.inc("y_in", nc.vector.tensor_tensor(yT, bank(7, TOK), yT, ALU.add))
                        st.wait("mean", 1)
                        st.inc("yc", nc.vector.scalar_tensor_tensor(tmp, bank(0, TOK), -1.0 / HD, yT, ALU.mult, ALU.add))
                        st.wait("bonus_sum", 1)
                        st.wait("raw", 9)
                        st.wait("yc", 1)
                        link(nc.vector.tensor_tensor(yT, bank(4, TOK), vT, ALU.mult))
                        st.wait("gn_std", 1)
                        link(nc.vector.reciprocal(inv, inv))
                        link(nc.vector.tensor_tensor(tmp, tmp, inv, ALU.mult))
                        link(nc.vector.tensor_scalar(tmp, tmp, par[:, V_LNW:V_LNW + 1], par[:, V_LNB:V_LNB + 1],
                                                     ALU.mult, ALU.add))
                        link(nc.vector.tensor_tensor(tmp, tmp, yT, ALU.add))
                        st.wait("fin_ready", 1)
                        st.inc("tile_done", nc.vector.tensor_tensor(flat(hT[:, bass.ds(j, 1), :]), tmp, gT, ALU.mult))
                        st.close()
            stored["state_out"] = 64 * KT

            with nc.Block() as block:
                @block.sync
                def _(sp):
                    load_phase(sp, f"wo{layer}", following)

                @block.tensor
                def _(pe):
                    wo_pe(pe, f"wo{layer}", hT, lambda k: None)

                @block.vector
                def _(dve):
                    wo_dve(dve, f"wo{layer}", layer)
            add(acc_taken=KT)


        def finish(room):
            carve = Carve(room)
            ytok = carve(TT, D)
            with nc.Block() as block:
                @block.tensor
                def _(pe):
                    for t in range(TT):
                        for q in range(2):
                            n = 2 * t + q
                            if n >= 2:
                                pe.wait_ge(sem("y_taken"), n - 1)
                            for k in range(4):
                                mm = nc.tensor.transpose(bank(n % 2, 4, P)[:, k], xT[:, 4 * q + k, t * P:(t + 1) * P],
                                                         K["ident"])
                            mm.then_inc(sem("y_turned"), 1)

                @block.vector
                def _(dve):
                    for n in range(2 * TT):
                        dve.wait_ge(sem("y_turned"), n + 1)
                        nc.vector.tensor_copy(ytok[:, n // 2, (n % 2) * 512:(n % 2 + 1) * 512], bank(n % 2, 512))\
                            .then_inc(sem("y_taken"), 1)

                @block.sync
                def _(sp):
                    for t in range(TT):
                        sp.wait_ge(sem("y_taken"), 2 * (t + 1))
                        dst = O["y_prompt"][0] if t == 0 else O["y_sample"][0, (t - 1) * P:t * P]
                        sp.dma_start(dst, ytok[:, t]).then_inc(sem("out"), 16)
                    sp.wait_ge(sem("out"), 16 * TT)
                    for n, v in stored.items():
                        sp.wait_ge(sem(n), v)

        stored = {}

        for layer in range(DEPTH):
            (da_phases, rwkv_phases, swa_phases)[layer % 3](layer)
            mlp_phases(layer)
        def room(name):
            return nc.sbuf_tensor(f"room_{name}", [P, ROOM], F32)

        with room("setup") as r:
            setup("qkv0", r[:, :])
        for layer in range(DEPTH):
            with room(layer) as r:
                (da, rwkv, swa)[layer % 3](layer, f"mlp{layer}", r[:, :])
            follow = {0: None, 1: "qkv2", 2: "qkv3", 3: None}[layer]
            mlp(layer, follow)
        with room("finish") as r:
            finish(r[:, :])


INPUTS = ("x_prompt x_sample cache_da_k cache_da_v state_rwkv cache_swa_k cache_swa_v c c_ctx ada_w ada_b mlp_w1 mlp_w2 "
          "da_wqkv da_q_norm da_k_norm da_lambda da_subln da_wo rwkv_mu rwkv_wrkv rwkv_w0 rwkv_w1 rwkv_w2 rwkv_a0 "
          "rwkv_a1 rwkv_a2 rwkv_g1 rwkv_g2 rwkv_k_k rwkv_k_a rwkv_r_k rwkv_ln_w rwkv_ln_b rwkv_wo swa_wqkv "
          "swa_q_norm swa_k_norm swa_sink swa_wo").split()
OUTPUTS = {"y_prompt": (1, CTX, D), "y_sample": (1, LAT, D), "new_da_k": (1, 2, CTX, 8, P), "new_da_v": (1, 2, CTX, 8, P),
           "new_state_rwkv": (1, 1, 2, 16, HD, HD), "new_swa_k": (1, 1, CTX, 4, HD), "new_swa_v": (1, 1, CTX, 4, HD)}


def kernel(**inputs):
    import concourse.bacc as bacc
    from concourse.bass_utils import run_bass_kernel_spmd

    nc = bacc.Bacc("TRN2", target_bir_lowering=False, num_devices=1)
    arrays = {f"in_{n}": np.ascontiguousarray(inputs[n]) for n in INPUTS}
    arrays["in_consts"] = constants()
    I = {n[3:]: nc.dram_tensor(n, a.shape, mybir.dt.from_np(a.dtype), kind="ExternalInput").ap()
         for n, a in arrays.items()}
    O = {n: nc.dram_tensor(f"out_{n}", s, F32, kind="ExternalOutput").ap() for n, s in OUTPUTS.items()}
    build(nc, I, O)
    r = run_bass_kernel_spmd(nc, [arrays], core_ids=[0])
    return tuple(r.results[0][f"out_{n}"] for n in OUTPUTS)
```

```python
import math
from contextlib import ExitStack

import numpy as np

import concourse.bass as bass
from concourse import mybir

F32 = mybir.dt.float32
F32R = mybir.dt.float32r
ACT = mybir.ActivationFunctionType
ALU = mybir.AluOpType
AX_X = mybir.AxisListType.X

P = 128
D = 1024
KT = D // P
CTX, LAT, PAST = 128, 256, 128
TOK = CTX + LAT
TT = TOK // P
DEPTH = 4
FF = 4 * D
FT = FF // P
HD = 64
GRID_W = 64
CH = 64
NCH = TOK // CH
LEVELS = 6
EPS = 1e-6
GN_EPS = 64e-5
DECAY = math.exp(-0.5)
NEG_INF = -1e30
SCALE = HD ** -0.5
GROUPS = ((0, slice(0, CTX)), (1, slice(CTX, TOK)))
SLAB = 256
SLOTS = 4
ADA_SLOTS = 3
ADA_UNITS = 6 * D // SLAB

CONST_COLS = {}
_at = 0
for _name, _n in (("ident", P), ("blocks", P), ("ones", P), ("swap32", P), ("swap64", P), ("cos", LAT), ("sin", LAT),
                  ("band", 2 * TOK), ("first", 2 * 128), ("pairs", 2 * 128), ("levels", 2 * (LEVELS - 1) * 128),
                  ("causal", 2 * 128), ("add_parts", 12), ("restart", TOK), ("eps", 1), ("gn_eps", 1)):
    CONST_COLS[_name] = slice(_at, _at + _n)
    _at += _n
CONST_N = _at


def constants():
    c = np.zeros((P, CONST_N), np.float32)
    p = np.arange(P)[:, None]
    q = np.arange(P)[None, :]
    c[:, CONST_COLS["ident"]] = p == q
    c[:, CONST_COLS["blocks"]] = p // 64 == q // 64
    c[:, CONST_COLS["ones"]] = 1
    c[:, CONST_COLS["swap32"]] = p == (q ^ 32)
    c[:, CONST_COLS["swap64"]] = p == (q ^ 64)
    t = np.arange(LAT)
    n_freq = HD // 4
    inv = (np.float32(10000.0) ** (-np.arange(n_freq, dtype=np.float32) / n_freq)).astype(np.float32)
    ang = np.concatenate([(t // GRID_W).astype(np.float32)[:, None] * inv,
                          (t % GRID_W).astype(np.float32)[:, None] * inv], axis=1).astype(np.float32)
    d = np.arange(P) % HD
    c[:, CONST_COLS["cos"]] = np.cos(ang.astype(np.float64))[:, d % 32].T
    c[:, CONST_COLS["sin"]] = (np.sin(ang.astype(np.float64))[:, d % 32] * np.where(d < 32, -1, 1)).T
    band = np.zeros((P, 2, TOK))
    for b in range(2):
        far = np.abs(np.arange(LAT)[None, :] - (np.arange(P)[:, None] + b * P)) > 128
        band[:, b, :LAT][far] = NEG_INF
    c[:, CONST_COLS["band"]] = band.reshape(P, -1)
    r = np.arange(P)[:, None] % 64
    s = np.arange(64)[None, :]
    first, causal, levels = np.zeros((P, 2, 2, 64)), np.zeros((P, 2, 2, 64)), np.zeros((P, 2, LEVELS, 2, 64))
    for z in range(2):
        row, col = (r, s) if z == 0 else (63 - r, 63 - s)
        mask = (row // 2 == col // 2) & (row > col)
        first[:64, z, 0], first[64:, z, 1] = mask[:64], mask[64:]
        for n in range(LEVELS):
            w = 1 << n
            mask = (row // (2 * w) == col // (2 * w)) & (row // w < col // w)
            levels[:64, z, n, 0] = mask[:64]
            levels[64:, z, n, 1] = mask[64:]
        causal[:, z, 0] = row < col
        causal[:, z, 1] = row <= col
    c[:, CONST_COLS["first"]] = first.reshape(P, -1)
    c[:, CONST_COLS["pairs"]] = levels[:, :, 0].reshape(P, -1)
    c[:, CONST_COLS["levels"]] = levels[:, :, 1:].reshape(P, -1)
    c[:, CONST_COLS["causal"]] = causal.reshape(P, -1)
    c[:, CONST_COLS["add_parts"]] = (p < 24) & (p // 4 == q[:, :12] // 2) & (p % 2 == q[:, :12] % 2)
    c[:, CONST_COLS["restart"]] = (np.arange(TOK) % CH != 0)[None, :]
    c[:, CONST_COLS["eps"]] = EPS
    c[:, CONST_COLS["gn_eps"]] = GN_EPS
    return c


def over(ap, n):
    return ap.unsqueeze(1).to_broadcast([ap.shape[0], n, ap.shape[1]])


def build(nc, I, O):
    ctx = ExitStack()
    with ctx:
        def sb(name, *shape):
            return ctx.enter_context(nc.sbuf_tensor(name, [P, *shape], F32))

        sems = {}

        def sem(name):
            if name not in sems:
                sems[name] = ctx.enter_context(nc.semaphore(name))
            return sems[name]

        const = sb("const", CONST_N)
        K = {n: const[:, s] for n, s in CONST_COLS.items()}
        band = K["band"].rearrange("p (b t) -> p b t", b=2)
        first = K["first"].rearrange("p (z t) -> p z t", z=2)
        pairs = K["pairs"].rearrange("p (z t) -> p z t", z=2)
        levels = K["levels"].rearrange("p (z n t) -> p z n t", z=2, n=LEVELS - 1)
        causal = K["causal"].rearrange("p (z t) -> p z t", z=2)
        xT = sb("xT", KT, TOK)
        hT = sb("hT", KT, TOK)
        slab = sb("slab", SLOTS, KT, SLAB)
        ada_slab = sb("ada_slab", ADA_SLOTS, KT, SLAB)
        mod = sb("mod", DEPTH, 48, 2)
        ada_b = sb("ada_b", DEPTH * 48)
        cond = sb("cond", KT, 2)
        rstd = sb("rstd", TOK)
        small = sb("small", 8)
        vecs = sb("vecs", 120)
        lam = sb("lam", 8)
        ROOM = 27004
        psum = ctx.enter_context(nc.psum_tensor("psum", [P, 8, 512], F32))

        def bank(b, *shape):
            n = int(np.prod(shape))
            v = psum[:, b, 0:n]
            return v if len(shape) == 1 else v.rearrange("p (a b) -> p a b", a=shape[0])

        class Carve:

            def __init__(self, of):
                self.at, self.of = 0, of

            def __call__(self, *shape):
                n = int(np.prod(shape))
                v = self.of[:, self.at:self.at + n]
                self.at += n
                assert self.at <= self.of.shape[1], self.at
                names = "abcd"[:len(shape)]
                if len(shape) > 1:
                    v = v.rearrange(f"p ({' '.join(names)}) -> p {' '.join(names)}",
                                    **dict(zip(names[:-1], shape)))
                return v

        count = {}

        def base(name):
            return count.get(name, 0)

        def add(**kw):
            for k, v in kw.items():
                count[k] = count.get(k, 0) + v

        class Link:

            def __init__(self, eng, name, start=None):
                self.eng, self.name, self.sem, self.n = eng, name, sem(name), 0
                self.start = base(name) if start is None else start

            def __call__(self, ins):
                self.n += 1
                ins.then_inc(self.sem, 1)
                self.eng.wait_ge(self.sem, self.start + self.n)

            def close(self):
                add(**{self.name: self.n})

        def alone(eng):
            eng.wait_ge(sem("const_in"), 16)

        def start_at(eng, name, value):
            if not (isinstance(value, int) and value <= 0):
                eng.wait_ge(sem(name), value)
                if not isinstance(value, int):
                    alone(eng)

        slab_ready = [sem(f"slab_ready{s}") for s in range(SLOTS)]
        run_done, acc_taken, split_ready = sem("run_done"), sem("acc_taken"), sem("split_ready")
        run_after = []
        phases = {}

        def phase(name, runs, src):
            phases[name] = (len(run_after), len(runs), src)
            for r in runs:
                run_after.append((run_after[-1] if run_after else 0) + r)

        def cols(w, at):
            return w.rearrange("(k p) n -> p k n", p=P)[:, :, bass.ds(at, SLAB)]

        def load_unit(sp, name, u):
            start, _, src = phases[name]
            g = start + u
            if g >= SLOTS:
                sp.wait_ge(run_done, run_after[g - SLOTS])
            sp.dma_start(slab[:, g % SLOTS], src(u)).then_inc(slab_ready[g % SLOTS], 16)

        def load_phase(sp, name, following):
            for u in range(SLOTS, phases[name][1]):
                load_unit(sp, name, u)
            load_first(sp, following)

        def load_first(sp, following):
            if following:
                for u in range(min(SLOTS, phases[following][1])):
                    load_unit(sp, following, u)

        def has_slab(pe, u, it=0):
            pe.wait_ge(slab_ready[u % SLOTS], 16 * (u // SLOTS + 1) + it * 16)

        ADA_GROUP = 6
        ADA_GROUPS = ADA_UNITS // ADA_GROUP
        PAD4 = 4 * (ADA_GROUP - 1)
        CONDW = 2 * PAD4 + 4

        def window(cw, k, s):
            return cw[:, k, PAD4 - 4 * s:PAD4 - 4 * s + 4 * ADA_GROUP]

        def ada_load(sp, layer, it, s):
            start_at(sp, "ada_free", layer * ADA_UNITS + s + 1 - ADA_SLOTS + it * ADA_GROUP)
            sp.dma_start(ada_slab[:, s % ADA_SLOTS], cols(I["ada_w"][layer], (it * ADA_GROUP + s) * SLAB))\
                .then_inc(sem(f"ada_ready{s % ADA_SLOTS}"), 16)

        def ada_ready(eng, layer, it, s):
            loads = (layer * ADA_UNITS + s) // ADA_SLOTS + 1
            eng.wait_ge(sem(f"ada_ready{s % ADA_SLOTS}"), loads * 16 + it * (16 * ADA_GROUP // ADA_SLOTS))

        def ada_rows(act, layer, it, done, first, rows):
            act.wait_ge(sem(done), first + it * ADA_GROUP)
            nc.scalar.activation(rows[0:4 * ADA_GROUP, :], psum[0:4 * ADA_GROUP, 6, 0:SLAB], ACT.Copy)\
                .then_inc(sem("rows_ready"), 1)

        def mod_cols(h):
            return psum[:, 2, 2 * ADA_GROUP * h:2 * ADA_GROUP * (h + 1)]

        def ada_turn(pe, layer, it, rows):
            g = layer * ADA_GROUPS + it
            pe.wait_ge(sem("rows_ready"), g + 1)
            start_at(pe, "mod_step", g)
            for h in range(2):
                mm = nc.tensor.matmul(mod_cols(h), rows[0:4 * ADA_GROUP, h * P:(h + 1) * P],
                                      K["add_parts"][0:4 * ADA_GROUP], start=True, stop=True)
            mm.then_inc(sem("rows_turned"), 1)

        def ada_take(dve, layer, it):
            g = layer * ADA_GROUPS + it
            dve.wait_ge(sem("rows_turned"), g + 1)
            n = 2 * ADA_GROUP
            dst = mod[:, layer, bass.ds(it * n, n), :].rearrange("p (s h) g -> p h s g", h=2)
            b = ada_b[:, bass.ds(it * n + layer * 48, n)].rearrange("p (s h) -> p h s", h=2)
            for h in range(2):
                ins = nc.vector.tensor_tensor(dst[:, h], mod_cols(h).rearrange("p (s g) -> p s g", g=2),
                                              b[:, h].unsqueeze(2).to_broadcast([P, ADA_GROUP, 2]), ALU.add)
            ins.then_inc(sem("mod_step"), 1)

        def ada_scale(dve, layer):
            dve.wait_ge(sem("mod_step"), (layer + 1) * ADA_GROUPS)
            for c in (1, 4):
                m = mod[:, layer, c * KT:(c + 1) * KT, :]
                nc.vector.tensor_scalar(m, m, 1.0, None, ALU.add).then_inc(sem("mod_ready"), 1)

        def stat_act(act, k, squares):
            nc.scalar.activation(squares[:, k], xT[:, k], ACT.Square).then_inc(sem("sq_ready"), 1)

        def stat_pe(pe, k, squares):
            pe.wait_ge(sem("sq_ready"), base("sq_ready") + k + 1)
            mm = nc.tensor.matmul(bank(7, TOK), K["ones"], squares[:, k], start=k == 0, stop=k == KT - 1)
            if k == KT - 1:
                mm.then_inc(sem("sum_done"), 1)

        def stat_counts():
            add(sq_ready=KT, sum_done=1)

        def norm_std(act, layer):
            act.wait_ge(sem("sum_done"), base("sum_done"))
            nc.scalar.activation(rstd[:, :], bank(7, TOK), ACT.Sqrt, scale=1.0 / D, bias=K["eps"])\
                .then_inc(sem("std_ready"), 1)

        def norm_act(act, layer, half, out):
            norm_std(act, layer)
            act.wait_ge(sem("mod_ready"), 2 * (layer + 1))
            for k in range(KT):
                act.wait_ge(sem("xn_ready"), base("h_ready") + k + 1)
                for g, t in GROUPS:
                    ins = nc.scalar.activation(out(k, g), hT[:, k, t], ACT.Identity,
                                               scale=mod[:, layer, (3 * half + 1) * KT + k, g:g + 1],
                                               bias=mod[:, layer, 3 * half * KT + k, g:g + 1])
                ins.then_inc(sem("h_ready"), 1)

        def norm_dve(dve, link, layer=None, half=None):
            b = base("h_ready")
            dve.wait_ge(sem("std_ready"), base("sum_done"))
            link(nc.vector.reciprocal(rstd[:, :], rstd[:, :]))
            if layer is not None:
                dve.wait_ge(sem("mod_ready"), 2 * (layer + 1))
            for k in range(KT + 1):
                if k < KT:
                    nc.vector.tensor_tensor(hT[:, k], xT[:, k], rstd[:, :], ALU.mult).then_inc(sem("xn_ready"), 1)
                if k >= 1 and layer is not None:
                    m = k - 1
                    dve.wait_ge(sem("xn_ready"), b + m + 1)
                    for g, t in GROUPS:
                        h = hT[:, m, t]
                        ins = nc.vector.tensor_scalar(h, h, mod[:, layer, (3 * half + 1) * KT + m, g:g + 1],
                                                      mod[:, layer, 3 * half * KT + m, g:g + 1], ALU.mult, ALU.add)
                    ins.then_inc(sem("h_ready"), 1)

        def norm_counts():
            add(h_ready=KT)

        def has_h(pe, k):
            pe.wait_ge(sem("h_ready"), base("h_ready") + k + 1)

        def flat(ap):
            return ap.rearrange("p a b -> p (a b)")

        def residual(layer, half, n, acc):
            for g, t in GROUPS:
                gate = flat(mod[:, layer, bass.ds(n + (3 * half + 2) * KT, 1), g:g + 1])
                x = flat(xT[:, bass.ds(n, 1), t])
                ins = nc.vector.scalar_tensor_tensor(x, acc[:, t], gate, x, ALU.mult, ALU.add)
            return ins

        def lambda_init(i):
            return 0.8 - 0.6 * math.exp(-0.3 * i)

        def setup(following, room):
            carve = Carve(room)
            xtok = carve(TT, D)
            rows = carve(4, P)
            lam_in = carve(2, 4, HD)
            sg = carve(16)
            cond_pad, mod_rows = carve(KT, CONDW), carve(SLAB)
            n_rows = (96, 96, 120, 24)

            def row(v):
                return v.rearrange("(r p) -> r p", p=P)

            ab = row(I["ada_b"].rearrange("l n -> (l n)"))
            loads = [(rows[0:96, 0], ab[0:96]), (rows[0:96, 1], ab[96:192])]
            at = 0
            for v in (I["rwkv_mu"].rearrange("l m d -> (l m d)"), I["rwkv_w0"].rearrange("l z d -> (l z d)"),
                      I["rwkv_a0"].rearrange("l z d -> (l z d)"), I["rwkv_k_k"][0], I["rwkv_k_a"][0],
                      I["rwkv_r_k"][0].rearrange("h d -> (h d)"), I["rwkv_ln_w"][0], I["rwkv_ln_b"][0]):
                m = v.shape[0] // P
                loads.append((rows[at:at + m, 2], row(v)))
                at += m
            assert at == 120
            loads += [(rows[0:8, 3], row(I["c_ctx"])), (rows[8:16, 3], row(I["c"][0]))]
            at = 16
            for v in (I["da_q_norm"][0], I["da_k_norm"][0], I["da_q_norm"][1], I["da_k_norm"][1],
                      I["swa_q_norm"][0], I["swa_k_norm"][0]):
                one = v.unsqueeze(0)
                loads += [(rows[at:at + 1, 3, 0:HD], one), (rows[at:at + 1, 3, HD:P], one)]
                at += 1
            for j in range(2):
                loads.append((rows[at:at + 1, 3], I["da_subln"][j:j + 1]))
                at += 1
            loads.append((lam_in, I["da_lambda"].unsqueeze(0).to_broadcast([P, 2, 4, HD])))
            x_loads = [(xtok[:, 0], I["x_prompt"][0])] + [
                (xtok[:, 1 + t], I["x_sample"][0, t * P:(t + 1) * P]) for t in range(2)]
            with nc.Block() as block:
                @block.sync
                def _(sp):
                    sp.dma_start(const[:, :], I["consts"]).then_inc(sem("const_in"), 16)
                    for s in range(ADA_GROUP):
                        ada_load(sp, 0, 0, s)
                    with sp.Fori(1, ADA_GROUPS) as it:
                        for s in range(ADA_GROUP):
                            ada_load(sp, 0, it, s)
                    load_first(sp, following)

                @block.scalar
                def _(act):
                    for dst, s in loads:
                        act.dma_start(dst, s).then_inc(sem("rows_in"), 16)
                    for dst, s in x_loads:
                        act.dma_start(dst, s).then_inc(sem("x_in"), 16)
                    act.wait_ge(sem("rows_done"), 4)
                    nc.scalar.activation(sg[:, :], bank(3, 24)[:, 0:16], ACT.Sigmoid).then_inc(sem("sig_cond"), 1)
                    for k in range(KT):
                        act.wait_ge(sem("x_taken"), k + 1)
                        stat_act(act, k, hT)
                    for j in range(2):
                        act.wait_ge(sem("lam_dots"), 2 * (j + 1))
                        nc.scalar.activation(lam[:, 4 * j:4 * j + 2], lam[:, 4 * j:4 * j + 2], ACT.Exp)\
                            .then_inc(sem("lam_exps"), 1)
                    with act.Fori(0, ADA_GROUPS) as it:
                        ada_rows(act, 0, it, "ada_free", ADA_GROUP, mod_rows)

                @block.gpsimd
                def _(pool):
                    nc.gpsimd.memset(mod_rows, 0.0).then_inc(sem("ada_mult"), 1)
                    nc.gpsimd.memset(cond_pad, 0.0).then_inc(sem("pad_zero"), 1)

                @block.tensor
                def _(pe):
                    pe.wait_ge(sem("const_in"), 16)
                    pe.wait_ge(sem("rows_in"), 16 * len(loads))
                    for i, n in enumerate(n_rows):
                        nc.tensor.transpose(bank(i, n), rows[0:n, i], K["ident"][0:n, 0:n])\
                            .then_inc(sem("rows_done"), 1)
                    pe.wait_ge(sem("x_in"), 16 * TT)
                    for k in range(KT):
                        if k >= 2:
                            pe.wait_ge(sem("x_taken"), k - 1)
                        for t in range(TT):
                            mm = nc.tensor.transpose(bank(4 + k % 2, TT, P)[:, t], xtok[:, t, k * P:(k + 1) * P],
                                                     K["ident"])
                        mm.then_inc(sem("x_turned"), 1)
                    for k in range(KT):
                        stat_pe(pe, k, hT)
                    pe.wait_ge(sem("cond_ready"), 2)

                    def group(it):
                        for s in range(ADA_GROUP):
                            ada_ready(pe, 0, it, s)
                            for k in range(KT):
                                mm = nc.tensor.matmul(psum[0:4 * ADA_GROUP, 6, 0:SLAB], window(cond_pad, k, s),
                                                      ada_slab[:, s % ADA_SLOTS, k], start=s == 0 and k == 0,
                                                      stop=s == ADA_GROUP - 1 and k == KT - 1)
                            mm.then_inc(sem("ada_free"), 1)
                        ada_turn(pe, 0, it, mod_rows)

                    group(0)
                    with pe.Fori(1, ADA_GROUPS) as it:
                        group(it)

                @block.vector
                def _(dve):
                    link = Link(dve, "dve_step")
                    dve.wait_ge(sem("rows_done"), 4)
                    nc.vector.tensor_copy(ada_b[:, 0:96], bank(0, 96))
                    nc.vector.tensor_copy(ada_b[:, 96:192], bank(1, 96))
                    link(nc.vector.tensor_copy(vecs[:, :], bank(2, 120)))
                    dve.wait_ge(sem("sig_cond"), 1)
                    link(nc.vector.tensor_copy(small[:, :], bank(3, 24)[:, 16:24]))
                    nc.vector.tensor_tensor(cond[:, :, :].rearrange("p k g -> p g k"),
                                            bank(3, 24)[:, 0:16].rearrange("p (g k) -> p g k", g=2),
                                            sg.rearrange("p (g k) -> p g k", g=2), ALU.mult)\
                        .then_inc(sem("cond_ready"), 1)
                    dve.wait_ge(sem("cond_ready"), 1)
                    dve.wait_ge(sem("pad_zero"), 1)
                    nc.vector.tensor_copy(cond_pad[:, :, PAD4:PAD4 + 2], cond[:, :, :]).then_inc(sem("cond_ready"), 1)
                    for k in range(KT):
                        dve.wait_ge(sem("x_turned"), k + 1)
                        nc.vector.tensor_copy(xT[:, k], bank(4 + k % 2, TOK)).then_inc(sem("x_taken"), 1)
                    for j in range(2):
                        s = small[:, 6 + j:7 + j]
                        link(nc.vector.tensor_scalar(s, s, 1.0 - lambda_init(3 * j), None, ALU.mult))
                    for j in range(2):
                        for m in range(2):
                            link(nc.vector.tensor_tensor(lam_in[:, j, 2 * m], lam_in[:, j, 2 * m],
                                                         lam_in[:, j, 2 * m + 1], ALU.mult))
                            nc.vector.tensor_reduce(lam[:, 4 * j + m:4 * j + m + 1], lam_in[:, j, 2 * m], AX_X,
                                                    ALU.add).then_inc(sem("lam_dots"), 1)
                        dve.wait_ge(sem("lam_exps"), j + 1)
                        link(nc.vector.tensor_scalar(lam[:, 4 * j + 2:4 * j + 3], lam[:, 4 * j:4 * j + 1],
                                                     lam[:, 4 * j + 1:4 * j + 2], lambda_init(3 * j),
                                                     ALU.subtract, ALU.add))
                    with dve.Fori(0, ADA_GROUPS) as it:
                        ada_take(dve, 0, it)
                    ada_scale(dve, 0)
                    link.close()
            stat_counts()

        QUARTERS, UNITS = 4, 2 * SLOTS

        def mlp_phases(layer):
            def src(u):
                q, r = divmod(u, UNITS)
                return mlp_slab(layer, q, r)
            phase(f"mlp{layer}", [2] * (QUARTERS * UNITS), src)

        def mlp_slab(layer, q, r):
            if r < SLOTS:
                return cols(I["mlp_w1"][layer], (q * SLOTS + r) * SLAB)
            w2 = I["mlp_w2"][layer].rearrange("(k p) n -> p k n", p=P)
            return w2[:, bass.ds(q * KT, KT), (r - SLOTS) * SLAB:(r - SLOTS + 1) * SLAB]

        def mlp(layer, following):
            more = layer + 1 < DEPTH
            L = layer + 1
            start = phases[f"mlp{layer}"][0]
            runs = run_after[start - 1]
            taken, up_taken, sb, hb = base("acc_taken"), base("up_taken"), base("split_ready"), base("hid_ready")
            LAST = QUARTERS - 1
            ada_base = (L - 1) * ADA_UNITS
            with nc.sbuf_tensor(f"parts{layer}", [P, 4 * KT * TOK + 6 * KT * SLAB + KT * CONDW], F32R) as parts, \
                    nc.sbuf_tensor(f"room_mlp{layer}", [P, SLAB + 4 * TOK], F32) as room:
                c = Carve(parts[:, :])
                h, hid = c(2, KT, TOK), c(2, KT, TOK)
                r = Carve(room[:, :])
                mod_rows, square = r(SLAB), r(4, TOK)
                w, aw, cw = c(2, 2, KT, SLAB), c(2, KT, SLAB), c(KT, CONDW)
                with nc.Block() as block:
                    @block.sync
                    def _(sp):
                        def quarter(i, last):
                            for r in range(UNITS):
                                if not (last and r >= SLOTS):
                                    sp.wait_ge(split_ready, sb + r + 1 + i * UNITS)
                                    if not last:
                                        alone(sp)
                                    q, n = divmod(r + SLOTS, UNITS)
                                    slot = (start + r) % SLOTS
                                    sp.dma_start(slab[:, slot], mlp_slab(layer, i + q, n)).then_inc(slab_ready[slot], 16)
                                if more and r < ADA_GROUP:
                                    ada_load(sp, L, i, r)

                        with sp.Fori(0, LAST) as i:
                            quarter(i, False)
                        quarter(LAST, True)
                        load_first(sp, following)

                    @block.tensor
                    def _(pe):
                        def product(out, x, y, first, last):
                            for n, (a, b) in enumerate(((0, 0), (0, 1), (1, 0))):
                                mm = nc.tensor.matmul(out, x(a), y(b), start=first and n == 0, stop=last and n == 2)
                            return mm

                        def quarter(i, last):
                            stats = last and more
                            for r in range(UNITS):
                                pe.wait_ge(split_ready, sb + r + 1 + i * UNITS)
                                for j in range(2):
                                    n = (2 * r + j) % KT
                                    if (n >= 2) == (r < SLOTS):
                                        pe.wait_ge(sem("up_taken"), up_taken + (n - 1 if r < SLOTS else n + 7) + i * KT)
                                    else:
                                        pe.wait_ge(acc_taken, taken + n - 1 + i * KT)
                                    for k in range(KT):
                                        if r == 0 and j == 0:
                                            pe.wait_ge(sem("h_split"), base("h_split") + k + 1)
                                        if r == SLOTS and j == 0:
                                            pe.wait_ge(sem("hid_ready"), hb + k + 1 + i * KT)
                                        mm = product(bank(j, TOK), lambda a: w[:, r % 2, a, k, j * P:(j + 1) * P],
                                                     lambda b: (h if r < SLOTS else hid)[:, b, k], k == 0, k == KT - 1)
                                    mm.then_inc(run_done, 1)
                                    if stats and r > SLOTS:
                                        stat_pe(pe, 2 * (r - SLOTS) + j - 2, hT)
                                if more and 1 <= r <= ADA_GROUP:
                                    s = r - 1
                                    pe.wait_ge(sem("ada_free"), L * ADA_UNITS + s + 1 + i * ADA_GROUP)
                                    for a in range(2):
                                        for k in range(KT):
                                            mm = nc.tensor.matmul(psum[0:4 * ADA_GROUP, 6, 0:SLAB], window(cw, k, s), aw[:, a, k],
                                                                  start=s == 0 and a == 0 and k == 0,
                                                                  stop=s == ADA_GROUP - 1 and a == 1 and k == KT - 1)
                                    mm.then_inc(sem("ada_mult"), 1)
                            if more:
                                ada_turn(pe, L, i, mod_rows)
                            if stats:
                                for k in (KT - 2, KT - 1):
                                    stat_pe(pe, k, hT)

                        if more:
                            pe.wait_ge(sem("cond_split"), layer + 1)
                        with pe.Fori(0, LAST) as i:
                            quarter(i, False)
                        quarter(LAST, True)

                    @block.scalar
                    def _(act):
                        def hi(r, i):
                            g = start + r
                            act.wait_ge(slab_ready[g % SLOTS], 16 * (g // SLOTS + 1) + i * (16 * UNITS // SLOTS))
                            act.wait_ge(run_done, runs + 2 * max(r - 1, 0) + i * 2 * UNITS)
                            nc.scalar.activation(w[:, r % 2, 0], slab[:, g % SLOTS], ACT.Copy).then_inc(sem("hi_ready"), 1)

                        def hid_hi(n, i):
                            act.wait_ge(run_done, runs + n + 1 + i * 2 * UNITS)
                            nc.scalar.activation(hT[:, n], bank(n % 2, TOK), ACT.Relu).then_inc(sem("up_taken"), 1)
                            act.wait_ge(sem("up_taken"), up_taken + n + 1 + i * KT)
                            nc.scalar.activation(hid[:, 0, n], hT[:, n], ACT.Square).then_inc(sem("hid_hi"), 1)

                        def quarter(i, last):
                            for r in range(UNITS):
                                if 1 <= r <= SLOTS:
                                    hid_hi(2 * r - 1, i)
                                if not (last and r == UNITS - 1):
                                    hi(r + 1, i)
                                if more and 1 <= r <= ADA_GROUP:
                                    s = r - 1
                                    ada_ready(act, L, i, s)
                                    act.wait_ge(sem("ada_mult"), ada_base + 1 + s + i * ADA_GROUP)
                                    nc.scalar.activation(aw[:, 0], ada_slab[:, s % ADA_SLOTS], ACT.Copy)\
                                        .then_inc(sem("ada_hi"), 1)
                                if r < SLOTS:
                                    hid_hi(2 * r, i)
                                if last and more and r >= SLOTS:
                                    for k in range(max(0, 2 * (r - SLOTS) - 1), 2 * (r - SLOTS) + 1):
                                        act.wait_ge(acc_taken, taken + i * KT + k + 1)
                                        stat_act(act, k, hT)
                            if more:
                                ada_rows(act, L, i, "ada_mult", 1 + ada_base + ADA_GROUP, mod_rows)
                            if last and more:
                                act.wait_ge(acc_taken, taken + i * KT + KT)
                                stat_act(act, KT - 1, hT)

                        hi(0, 0)
                        norm_std(act, layer)
                        for k in range(KT):
                            act.wait_ge(sem("h_ready"), base("h_ready") + k + 1)
                            nc.scalar.activation(h[:, 0, k], hT[:, k], ACT.Copy).then_inc(sem("h_hi"), 1)
                        with act.Fori(0, LAST) as i:
                            quarter(i, False)
                        quarter(LAST, True)

                    @block.gpsimd
                    def _(pool):
                        if more:
                            nc.gpsimd.memset(cw.bitcast(F32), 0.0).then_inc(sem("cw_zero"), 1)
                        for k in range(KT):
                            pool.wait_ge(sem("h_hi"), base("h_split") + k + 1)
                            nc.gpsimd.tensor_tensor(h[:, 1, k], hT[:, k], h[:, 0, k].bitcast(F32), ALU.subtract)\
                                .then_inc(sem("h_split"), 1)
                        with pool.Fori(0, QUARTERS) as i:
                            for n in range(KT):
                                pool.wait_ge(sem("hid_hi"), hb + n + 1 + i * KT)
                                pool.wait_ge(sem("hid_sq"), hb + n + 1 + i * KT)
                                nc.gpsimd.tensor_tensor(hid[:, 1, n], square[:, n % 4], hid[:, 0, n].bitcast(F32), ALU.subtract)\
                                    .then_inc(sem("hid_ready"), 1)

                    @block.vector
                    def _(dve):
                        def lo(r, i):
                            dve.wait_ge(sem("hi_ready"), sb + r + 1 + i * UNITS)
                            nc.vector.tensor_tensor(w[:, r % 2, 1], slab[:, (start + r) % SLOTS], w[:, r % 2, 0].bitcast(F32),
                                                    ALU.subtract).then_inc(split_ready, 1)

                        def take(r, j, i):
                            if r < SLOTS:
                                n = 2 * r + j
                                dve.wait_ge(sem("up_taken"), up_taken + n + 1 + i * KT)
                                if n >= 4:
                                    dve.wait_ge(sem("hid_ready"), hb + n - 3 + i * KT)
                                nc.vector.tensor_tensor(square[:, n % 4], hT[:, n], hT[:, n], ALU.mult)\
                                    .then_inc(sem("hid_sq"), 1)
                            else:
                                dve.wait_ge(run_done, runs + 2 * r + j + 1 + i * 2 * UNITS)
                                residual(layer, 1, 2 * (r - SLOTS) + j, bank(j, TOK)).then_inc(acc_taken, 1)

                        def quarter(i, last):
                            for r in range(UNITS):
                                if r >= 1:
                                    take(r - 1, 1, i)
                                if not (last and r == UNITS - 1):
                                    lo(r + 1, i)
                                if more and 1 <= r <= ADA_GROUP:
                                    s = r - 1
                                    dve.wait_ge(sem("ada_hi"), ada_base + s + 1 + i * ADA_GROUP)
                                    nc.vector.tensor_tensor(aw[:, 1], ada_slab[:, s % ADA_SLOTS], aw[:, 0].bitcast(F32),
                                                            ALU.subtract).then_inc(sem("ada_free"), 1)
                                take(r, 0, i)
                            take(UNITS - 1, 1, i)
                            if more:
                                ada_take(dve, L, i)

                        lo(0, 0)
                        link = Link(dve, "dve_step")
                        if more:
                            dve.wait_ge(sem("cw_zero"), layer + 1)
                            own = cw[:, :, CONDW // 2 - 2:CONDW // 2]
                            link(nc.vector.tensor_copy(own, cond[:, :, :]))
                            nc.vector.tensor_tensor(cw[:, :, CONDW // 2:CONDW // 2 + 2], cond[:, :, :], own.bitcast(F32),
                                                    ALU.subtract).then_inc(sem("cond_split"), 1)
                        norm_dve(dve, link, layer, 1)
                        with dve.Fori(0, LAST) as i:
                            quarter(i, False)
                        quarter(LAST, True)
                        if more:
                            ada_scale(dve, L)
                        link.close()
            norm_counts()
            if more:
                stat_counts()
            add(acc_taken=FT, up_taken=FT, hid_ready=FT, split_ready=UNITS * QUARTERS, h_split=KT)

        def wo_phase(name, w):
            phase(name, [2] * (D // SLAB), lambda u: cols(w, u * SLAB))

        WIDE = (0, 1, 4, 5)

        def wo_wide_pe(pe, name, src, ready, squares):
            start = phases[name][0]

            def product(g, k):
                u, j = divmod(g, 2)
                return nc.tensor.matmul(bank(WIDE[g % 4], TOK), slab[:, (start + u) % SLOTS, k, j * P:(j + 1) * P],
                                        src[:, k], start=k == 0, stop=k == KT - 1)

            for u in range(2):
                has_slab(pe, start + u)
            for k in range(KT):
                ready(k)
                for g in range(4):
                    mm = product(g, k)
                    if k == KT - 1:
                        mm.then_inc(run_done, 1)
            for g in range(4, KT):
                if g % 2 == 0:
                    has_slab(pe, start + g // 2)
                pe.wait_ge(acc_taken, base("acc_taken") + g - 3)
                for k in range(KT):
                    mm = product(g, k)
                mm.then_inc(run_done, 1)
                for k in ((0, 1), (2, 3), (4,), (5,))[g - 4]:
                    stat_pe(pe, k, squares)
            for k in (KT - 2, KT - 1):
                stat_pe(pe, k, squares)

        def wo_pe(pe, name, src, ready, squares):
            start, n, _ = phases[name]
            for u in range(n):
                has_slab(pe, start + u)
                for j in range(2):
                    g = 2 * u + j
                    start_at(pe, "acc_taken", base("acc_taken") + g - 1)
                    for k in range(KT):
                        if g == 0:
                            ready(k)
                        mm = nc.tensor.matmul(bank(j, TOK), slab[:, (start + u) % SLOTS, k, j * P:(j + 1) * P],
                                              src[:, k], start=k == 0, stop=k == KT - 1)
                    mm.then_inc(run_done, 1)
                    if g >= 2:
                        stat_pe(pe, g - 2, squares)
            for k in (KT - 2, KT - 1):
                stat_pe(pe, k, squares)

        def wo_act(act, squares):
            for k in range(KT):
                act.wait_ge(acc_taken, base("acc_taken") + k + 1)
                stat_act(act, k, squares)

        def wo_dve(dve, name, layer, banks=(0, 1)):
            runs = run_after[phases[name][0] - 1]
            for g in range(KT):
                dve.wait_ge(run_done, runs + g + 1)
                residual(layer, 0, g, bank(banks[g % len(banks)], TOK)).then_inc(acc_taken, 1)

        def qk_pe(pe, start, n_tiles, dst, ws):
            for n in range(n_tiles + 2):
                if n < n_tiles:
                    if n % 2 == 0:
                        has_slab(pe, start + n // 2)
                    start_at(pe, "acc_taken", base("acc_taken") + n - 1)
                    for k in range(KT):
                        if n == 0:
                            has_h(pe, k)
                        at = (n % 2) * P
                        mm = nc.tensor.matmul(bank(n % 2, TOK), slab[:, (start + n // 2) % SLOTS, k, at:at + P],
                                              hT[:, k], start=k == 0, stop=k == KT - 1)
                    mm.then_inc(run_done, 1)
                if 1 <= n <= n_tiles:
                    m = n - 1
                    pe.wait_ge(sem("head_sq"), base("head_sq") + m + 1)
                    start_at(pe, "head_std", base("head_sq") + m - 1)
                    nc.tensor.matmul(bank(2 + m % 2, TOK), K["blocks"], ws["sq"][:, m % 2], start=True, stop=True)\
                        .then_inc(sem("head_sum"), 1)
                if n >= 2:
                    m = n - 2
                    pe.wait_ge(sem("head_norm"), base("head_sq") + m + 1)
                    start_at(pe, "partner_taken", base("head_sq") + m - 1)
                    nc.tensor.matmul(bank(4 + m % 2, LAT), K["swap32"], dst(m)[:, CTX:TOK], start=True, stop=True)\
                        .then_inc(sem("partner"), 1)

        def qk_act(act, start, n_tiles, ws):
            runs, hb = run_after[start - 1] if start else 0, base("head_sq")
            for n in range(n_tiles + 1):
                if n < n_tiles:
                    act.wait_ge(run_done, runs + n + 1)
                    start_at(act, "head_norm", hb + n - 1)
                    nc.scalar.activation(ws["raw"][:, n % 2], bank(n % 2, TOK), ACT.Copy).then_inc(acc_taken, 1)
                    start_at(act, "head_sum", hb + n - 1)
                    act.wait_ge(acc_taken, base("acc_taken") + n + 1)
                    nc.scalar.activation(ws["sq"][:, n % 2], ws["raw"][:, n % 2], ACT.Square)\
                        .then_inc(sem("head_sq"), 1)
                if n >= 1:
                    m = n - 1
                    act.wait_ge(sem("head_sum"), hb + m + 1)
                    start_at(act, "head_norm", hb + m - 1)
                    nc.scalar.activation(ws["rinv"][:, m % 2], bank(2 + m % 2, TOK), ACT.Sqrt, scale=1.0 / HD,
                                         bias=K["eps"]).then_inc(sem("head_std"), 1)

        def qk_dve(dve, link, n_tiles, dst, gain, ws):
            hb = base("head_sq")
            for n in range(n_tiles + 1):
                if n < n_tiles:
                    dve.wait_ge(sem("head_std"), hb + n + 1)
                    link(nc.vector.reciprocal(ws["rinv"][:, n % 2], ws["rinv"][:, n % 2]))
                    nc.vector.scalar_tensor_tensor(dst(n), ws["raw"][:, n % 2], gain(n), ws["rinv"][:, n % 2],
                                                   ALU.mult, ALU.mult).then_inc(sem("head_norm"), 1)
                if n >= 1:
                    m = n - 1
                    x = dst(m)[:, CTX:TOK]
                    dve.wait_ge(sem("partner"), hb + m + 1)
                    nc.vector.tensor_tensor(ws["turn"][:, m % 2], bank(4 + m % 2, LAT), K["sin"], ALU.mult)\
                        .then_inc(sem("partner_taken"), 1)
                    link(nc.vector.tensor_tensor(x, x, K["cos"], ALU.mult))
                    link(nc.vector.tensor_tensor(x, x, ws["turn"][:, m % 2], ALU.add))

        def v_pe(pe, start, units, g):
            for u in units:
                has_slab(pe, start + u)
                for t in range(TT):
                    start_at(pe, "acc_taken", base("acc_taken") + g - 1)
                    for k in range(KT):
                        mm = nc.tensor.matmul(bank(g % 2, SLAB), hT[:, k, t * P:(t + 1) * P],
                                              slab[:, (start + u) % SLOTS, k], start=k == 0, stop=k == KT - 1)
                    mm.then_inc(run_done, 1)
                    g += 1

        def v_act(act, start, units, g, v):
            runs = run_after[start - 1] if start else 0
            for i, u in enumerate(units):
                for t in range(TT):
                    act.wait_ge(run_done, runs + g + 1)
                    nc.scalar.activation(v[:, t, i * SLAB:(i + 1) * SLAB], bank(g % 2, SLAB), ACT.Copy)\
                        .then_inc(acc_taken, 1)
                    g += 1

        def turn_keys_pe(pe, kc, k, n, before):
            pe.wait_ge(sem("cache_in"), cache_loads[0])
            pe.wait_ge(sem("std_ready"), base("sum_done"))
            pe.wait_ge(sem("head_std"), base("head_sq") + before)
            for src, b0 in ((lambda c: kc[:, c * P:(c + 1) * P], 6), (lambda c: k[:, c, 0:CTX], 2)):
                for c in range(n):
                    mm = nc.tensor.transpose(bank(b0 + c // 4, 4, P)[:, c % 4], src(c), K["ident"])
                mm.then_inc(sem("keys_turned"), 1)

        cache_loads = [0]

        def turn_keys_act(act, k, kout, n):
            b = base("keys_turned")
            for i in range(2):
                act.wait_ge(sem("keys_turned"), b + i + 1)
                for q in range(0, n, 4):
                    m = min(4, n - q)
                    src = bank((6, 2)[i] + q // 4, m, P)
                    dst = k[:, q:q + m, TOK:TOK + PAST] if i == 0 else \
                        kout[:, q * P:(q + m) * P].rearrange("p (c t) -> p c t", c=m)
                    ins = nc.scalar.activation(dst, src, ACT.Copy)
            ins.then_inc(sem("kout_ready"), 1)

        def da_phases(layer):
            j = layer // 3
            phase(f"qkv{layer}", [2] * 8 + [3] * 4, lambda u: cols(I["da_wqkv"][j], u * SLAB))
            wo_phase(f"wo{layer}", I["da_wo"][j])

        def da(layer, following, room):
            j = layer // 3
            c = Carve(room)
            q, k, v, o = c(KT, TOK), c(KT, TOK + PAST), c(TT + 1, D), c(KT, TOK)
            ws = {"raw": c(2, TOK), "sq": c(2, TOK), "rinv": c(2, TOK), "turn": c(2, LAT)}
            kc, kout = c(D), c(D)
            probs, pr, prT = c(2, 2, TOK), c(2, TOK), c(2, TOK)
            neg, total, inv = c(2, 4), c(2, 2), c(2, 2)
            name = f"qkv{layer}"
            start = phases[name][0]
            n_tiles, v_units = 2 * KT, range(8, 12)
            cache_loads[0] += 32

            def dst(n):
                return q[:, n] if n < KT else k[:, n - KT, 0:TOK]

            def gain(n):
                at = 2 * j + n // KT
                return small[:, at:at + 1]

            with nc.Block() as block:
                @block.sync
                def _(sp):
                    load_phase(sp, name, f"wo{layer}")
                    sp.wait_ge(sem("kout_ready"), base("kout_ready") + 1)
                    sp.dma_start(O["new_da_k"][0, j].rearrange("t h d -> t (h d)"), kout).then_inc(sem("kv_stored"), 16)
                    sp.dma_start(O["new_da_v"][0, j].rearrange("t h d -> t (h d)"), v[:, 0])\
                        .then_inc(sem("kv_stored"), 16)

                @block.tensor
                def _(pe):
                    qk_pe(pe, start, n_tiles, dst, ws)
                    v_pe(pe, start, v_units, n_tiles)
                    turn_keys_pe(pe, kc, k, KT, n_tiles)

                @block.scalar
                def _(act):
                    act.dma_start(kc, I["cache_da_k"][0, j].rearrange("t h d -> t (h d)")).then_inc(sem("cache_in"), 16)
                    act.dma_start(v[:, TT], I["cache_da_v"][0, j].rearrange("t h d -> t (h d)"))\
                        .then_inc(sem("cache_in"), 16)
                    norm_std(act, layer)
                    qk_act(act, start, n_tiles, ws)
                    v_act(act, start, v_units, n_tiles, v)
                    turn_keys_act(act, k, kout, KT)

                @block.vector
                def _(dve):
                    link = Link(dve, "dve_step")
                    norm_dve(dve, link, layer, 0)
                    qk_dve(dve, link, n_tiles, dst, gain, ws)
                    link.close()
            norm_counts()
            add(acc_taken=n_tiles + TT * 4, head_sq=n_tiles, keys_turned=2, kout_ready=1, kv_stored=32)

            units = [(h, t) for h in range(KT) for t in range(TT)]
            N = len(units)
            ub, eb = base("unit"), base("exp_done")

            def keys(t):
                return (slice(0, CTX), (0,)) if t == 0 else (slice(CTX, TOK + PAST), (1, 2, 3))

            with nc.Block() as block:
                @block.tensor
                def _(pe):
                    for i in range(N + 3):
                        if i < N:
                            h, t = units[i]
                            ks, vb = keys(t)
                            start_at(pe, "exp_done", eb + 2 * (i - 1))
                            for m in range(2):
                                r = slice(HD * m, HD * m + HD)
                                mm = nc.tensor.matmul(bank(2 * (i % 2) + m, P * len(vb)), q[r, h, t * P:(t + 1) * P],
                                                      k[r, h, ks], start=True, stop=True)
                            mm.then_inc(sem("scores"), 1)
                        if 2 <= i <= N + 1:
                            u = i - 2
                            _, vb = keys(units[u][1])
                            pe.wait_ge(sem("pr_ready"), ub + u + 1)
                            start_at(pe, "prT_ready", ub + u - 1)
                            for b in range(len(vb)):
                                mm = nc.tensor.transpose(bank(4 + u % 2, TT, P)[:, b], pr[:, u % 2, b * P:(b + 1) * P],
                                                         K["ident"])
                            mm.then_inc(sem("pr_turned"), 1)
                        if i >= 3:
                            u = i - 3
                            h, t = units[u]
                            _, vb = keys(t)
                            pe.wait_ge(sem("prT_ready"), ub + u + 1)
                            if t == 0:
                                start_at(pe, "o_ready", ub // TT + h - 1)
                            for b, w in enumerate(vb):
                                mm = nc.tensor.matmul(bank(6 + h % 2, TOK)[:, t * P:(t + 1) * P],
                                                      v[:, w if w else 0, h * P:(h + 1) * P],
                                                      prT[:, u % 2, b * P:(b + 1) * P], start=b == 0, stop=b == len(vb) - 1)
                            mm.then_inc(sem("pv_done"), 1)

                @block.vector
                def _(dve):
                    link = Link(dve, "dve_step")
                    for i in range(N + 1):
                        if i < N:
                            n = P * len(keys(units[i][1])[1])
                            dve.wait_ge(sem("scores"), ub + i + 1)
                            for m in range(2):
                                ins = nc.vector.tensor_reduce(neg[:, i % 2, m:m + 1], bank(2 * (i % 2) + m, n), AX_X,
                                                              ALU.max, negate=True)
                            link(ins)
                            nc.vector.tensor_scalar(neg[:, i % 2, 2:4], neg[:, i % 2, 0:2], SCALE, None, ALU.mult)\
                                .then_inc(sem("max_ready"), 1)
                        if i >= 1:
                            u = i - 1
                            n = P * len(keys(units[u][1])[1])
                            dve.wait_ge(sem("exp_done"), eb + 2 * (u + 1))
                            link(nc.vector.reciprocal(inv[:, u % 2], total[:, u % 2]))
                            link(nc.vector.tensor_scalar(inv[:, u % 2, 1:2], inv[:, u % 2, 1:2],
                                                         lam[:, 4 * j + 2:4 * j + 3], None, ALU.mult))
                            p0, p1 = (probs[:, u % 2, m, 0:n] for m in range(2))
                            link(nc.vector.tensor_scalar(p1, p1, inv[:, u % 2, 1:2], None, ALU.mult))
                            start_at(dve, "pr_turned", ub + u - 1)
                            nc.vector.scalar_tensor_tensor(pr[:, u % 2, 0:n], p0, inv[:, u % 2, 0:1], p1, ALU.mult,
                                                           ALU.subtract).then_inc(sem("pr_ready"), 1)
                    link.close()

                @block.scalar
                def _(act):
                    for i in range(N + 3):
                        if i < N:
                            n = P * len(keys(units[i][1])[1])
                            act.wait_ge(sem("max_ready"), ub + i + 1)
                            start_at(act, "pr_ready", ub + i - 1)
                            for m in range(2):
                                nc.scalar.activation(probs[:, i % 2, m, 0:n], bank(2 * (i % 2) + m, n), ACT.Exp,
                                                     scale=SCALE, bias=neg[:, i % 2, 2 + m:3 + m],
                                                     accum_out=total[:, i % 2, m:m + 1]).then_inc(sem("exp_done"), 1)
                        if 2 <= i <= N + 1:
                            u = i - 2
                            n = P * len(keys(units[u][1])[1])
                            act.wait_ge(sem("pr_turned"), ub + u + 1)
                            start_at(act, "pv_done", ub + u - 1)
                            nc.scalar.activation(prT[:, u % 2, 0:n], bank(4 + u % 2, n), ACT.Copy)\
                                .then_inc(sem("prT_ready"), 1)
                        if i >= 3 and units[i - 3][1] == TT - 1:
                            h = units[i - 3][0]
                            act.wait_ge(sem("pv_done"), ub + i - 2)
                            nc.scalar.activation(o[:, h], bank(6 + h % 2, TOK), ACT.Copy).then_inc(sem("o_ready"), 1)
            add(unit=N, exp_done=2 * N)

            sb_ = base("o_sq")
            with nc.Block() as block:
                @block.sync
                def _(sp):
                    load_phase(sp, f"wo{layer}", following)

                @block.tensor
                def _(pe):
                    for h in range(KT):
                        pe.wait_ge(sem("o_sq"), sb_ + h + 1)
                        start_at(pe, "o_std", sb_ + h - 1)
                        nc.tensor.matmul(bank(2 + h % 2, TOK), K["ones"], hT[:, h], start=True, stop=True)\
                            .then_inc(sem("o_sum"), 1)
                    wo_wide_pe(pe, f"wo{layer}", o, lambda k: pe.wait_ge(sem("o_norm"), sb_ + k + 1), hT)

                @block.scalar
                def _(act):
                    for h in range(KT):
                        nc.scalar.activation(hT[:, h], o[:, h], ACT.Square).then_inc(sem("o_sq"), 1)
                    for h in range(KT):
                        act.wait_ge(sem("o_sum"), sb_ + h + 1)
                        start_at(act, "o_norm", sb_ + h - 1)
                        nc.scalar.activation(ws["rinv"][:, h % 2], bank(2 + h % 2, TOK), ACT.Sqrt, scale=1.0 / P,
                                             bias=K["eps"]).then_inc(sem("o_std"), 1)
                    wo_act(act, hT)

                @block.vector
                def _(dve):
                    link = Link(dve, "dve_step")
                    for h in range(KT):
                        dve.wait_ge(sem("o_std"), sb_ + h + 1)
                        link(nc.vector.reciprocal(ws["rinv"][:, h % 2], ws["rinv"][:, h % 2]))
                        nc.vector.scalar_tensor_tensor(o[:, h], o[:, h], small[:, 6 + j:7 + j], ws["rinv"][:, h % 2],
                                                       ALU.mult, ALU.mult).then_inc(sem("o_norm"), 1)
                    link.close()
                    wo_dve(dve, f"wo{layer}", layer, WIDE)
            add(o_sq=KT, acc_taken=KT)
            stat_counts()
            stored["kv_stored"] = base("kv_stored")

        def swa_phases(layer):
            phase(f"qkv{layer}", [2] * 5 + [3], lambda u: cols(I["swa_wqkv"][0], u * SLAB))
            wo_phase(f"wo{layer}", I["swa_wo"][0])

        def swa(layer, following, room):
            c = Carve(room)
            KV = SLAB
            q, k, k2, v, o = c(KT, TOK), c(2, TOK + PAST), c(2, TOK + PAST), c(TT + 1, KV), c(KT, TOK)
            ws = {"raw": c(2, TOK), "sq": c(2, TOK), "rinv": c(2, TOK), "turn": c(2, LAT)}
            kc, kout = c(KV), c(KV)
            probs, prT = c(2, 2, TOK), c(2, 2, TOK)
            sink, nsink = c(16), c(16)
            neg, total, inv = c(2, 6), c(2, 4), c(2, 2)
            name = f"qkv{layer}"
            start = phases[name][0]
            n_tiles, v_units = KT + 2, (5,)
            cache_loads[0] += 48

            def dst(n):
                return q[:, n] if n < KT else k[:, n - KT, 0:TOK]

            def gain(n):
                at = 4 + n // KT
                return small[:, at:at + 1]

            with nc.Block() as block:
                @block.sync
                def _(sp):
                    load_phase(sp, name, f"wo{layer}")
                    sp.wait_ge(sem("kout_ready"), base("kout_ready") + 1)
                    sp.dma_start(O["new_swa_k"][0, 0].rearrange("t h d -> t (h d)"), kout)\
                        .then_inc(sem("kv_stored"), 16)
                    sp.dma_start(O["new_swa_v"][0, 0].rearrange("t h d -> t (h d)"), v[:, 0])\
                        .then_inc(sem("kv_stored"), 16)

                @block.tensor
                def _(pe):
                    qk_pe(pe, start, n_tiles, dst, ws)
                    v_pe(pe, start, v_units, n_tiles)
                    turn_keys_pe(pe, kc, k, 2, n_tiles)
                    pe.wait_ge(sem("kout_ready"), base("kout_ready") + 1)
                    pe.wait_ge(sem("keys_roped"), 1)
                    for i in range(2):
                        nc.tensor.matmul(bank(2 + i, TOK + PAST), K["swap64"], k[:, i], start=True, stop=True)\
                            .then_inc(sem("keys_swapped"), 1)

                @block.scalar
                def _(act):
                    act.dma_start(kc, I["cache_swa_k"][0, 0].rearrange("t h d -> t (h d)")).then_inc(sem("cache_in"), 16)
                    act.dma_start(v[:, TT], I["cache_swa_v"][0, 0].rearrange("t h d -> t (h d)"))\
                        .then_inc(sem("cache_in"), 16)
                    act.dma_start(sink, I["swa_sink"][0:1].to_broadcast([P, 16])).then_inc(sem("cache_in"), 16)
                    norm_std(act, layer)
                    qk_act(act, start, n_tiles, ws)
                    v_act(act, start, v_units, n_tiles, v)
                    turn_keys_act(act, k, kout, 2)
                    for i in range(2):
                        act.wait_ge(sem("keys_swapped"), i + 1)
                        nc.scalar.activation(k2[:, i], bank(2 + i, TOK + PAST), ACT.Copy)

                @block.vector
                def _(dve):
                    link = Link(dve, "dve_step")
                    norm_dve(dve, link, layer, 0)
                    qk_dve(dve, link, n_tiles, dst, gain, ws)
                    link.close()
                    dve.wait_ge(sem("cache_in"), cache_loads[0])
                    nc.vector.tensor_scalar(nsink, sink, -1.0, None, ALU.mult).then_inc(sem("keys_roped"), 1)
            norm_counts()
            add(acc_taken=n_tiles + TT, head_sq=n_tiles, keys_turned=2, kout_ready=1, kv_stored=32)

            units = [(h, t) for h in range(KT) for t in range(TT)]
            N = len(units)
            ub, eb = base("unit"), base("exp_done")

            def keys(t):
                return (slice(0, CTX), (0,)) if t == 0 else (slice(CTX, TOK + PAST), (1, 2, 3))

            with nc.Block() as block:
                @block.tensor
                def _(pe):
                    for i in range(N + 3):
                        if 2 <= i <= N + 1:
                            u = i - 2
                            _, vb = keys(units[u][1])
                            pe.wait_ge(sem("pr_ready"), ub + u + 1)
                            start_at(pe, "prT_ready", ub + u)
                            for m in range(2):
                                for b in range(len(vb)):
                                    mm = nc.tensor.transpose(bank(4 + m, TT, P)[:, b],
                                                             probs[:, u % 2, m, b * P:(b + 1) * P], K["ident"])
                            mm.then_inc(sem("pr_turned"), 1)
                        if i < N:
                            h, t = units[i]
                            ks, vb = keys(t)
                            g = h // 2
                            start_at(pe, "max_ready", ub + i - 1)
                            for m in range(2):
                                r = slice(HD * m, HD * m + HD)
                                keys_at = (k if g % 2 == m else k2)[r, g // 2, ks]
                                mm = nc.tensor.matmul(bank(2 * (i % 2) + m, P * len(vb)), q[r, h, t * P:(t + 1) * P],
                                                      keys_at, start=True, stop=True)
                            mm.then_inc(sem("scores"), 1)
                        if i >= 3:
                            u = i - 3
                            h, t = units[u]
                            _, vb = keys(t)
                            g = h // 2
                            pe.wait_ge(sem("prT_ready"), ub + u + 1)
                            if t == 0:
                                start_at(pe, "o_ready", ub // TT + h - 1)
                            for m in range(2):
                                for b, w in enumerate(vb):
                                    mm = nc.tensor.matmul(psum[HD * m:HD * m + HD, 6 + h % 2, t * P:(t + 1) * P],
                                                          v[:, w, g * HD:(g + 1) * HD],
                                                          prT[:, u % 2, m, b * P:(b + 1) * P],
                                                          start=b == 0, stop=b == len(vb) - 1)
                            mm.then_inc(sem("pv_done"), 1)

                @block.vector
                def _(dve):
                    link = Link(dve, "dve_step")
                    for i in range(N + 1):
                        if i < N:
                            h, t = units[i]
                            n = P * len(keys(t)[1])
                            x = neg[:, i % 2]
                            dve.wait_ge(sem("scores"), ub + i + 1)
                            start_at(dve, "pr_turned", ub + i - 1)
                            for m in range(2):
                                s = bank(2 * (i % 2) + m, n)
                                if t == 0:
                                    ins = nc.vector.tensor_scalar(probs[:, i % 2, m, 0:n], s, SCALE, None, ALU.mult)
                                else:
                                    ins = nc.vector.scalar_tensor_tensor(probs[:, i % 2, m], s, SCALE, band[:, t - 1],
                                                                         ALU.mult, ALU.add)
                            link(ins)
                            link(nc.vector.tensor_reduce(x[:, 0:2], probs[:, i % 2, :, 0:n], AX_X, ALU.max, negate=True))
                            link(nc.vector.tensor_tensor(x[:, 2:4], x[:, 0:2], nsink[:, 2 * h:2 * h + 2], ALU.min))
                            nc.vector.tensor_tensor(x[:, 4:6], x[:, 2:4], sink[:, 2 * h:2 * h + 2], ALU.add)\
                                .then_inc(sem("max_ready"), 1)
                        if i >= 1:
                            u = i - 1
                            n = P * len(keys(units[u][1])[1])
                            dve.wait_ge(sem("exp_done"), eb + 3 * (u + 1))
                            link(nc.vector.tensor_tensor(total[:, u % 2, 0:2], total[:, u % 2, 0:2],
                                                         total[:, u % 2, 2:4], ALU.add))
                            link(nc.vector.reciprocal(inv[:, u % 2], total[:, u % 2, 0:2]))
                            for m in range(2):
                                p = probs[:, u % 2, m, 0:n]
                                ins = nc.vector.tensor_scalar(p, p, inv[:, u % 2, m:m + 1], None, ALU.mult)
                            ins.then_inc(sem("pr_ready"), 1)
                    link.close()

                @block.scalar
                def _(act):
                    for i in range(N + 3):
                        if 2 <= i <= N + 1:
                            u = i - 2
                            n = P * len(keys(units[u][1])[1])
                            act.wait_ge(sem("pr_turned"), ub + u + 1)
                            start_at(act, "pv_done", ub + u - 1)
                            nc.scalar.activation(prT[:, u % 2, :, 0:n], psum[:, 4:6, 0:n], ACT.Copy)\
                                .then_inc(sem("prT_ready"), 1)
                        if i < N:
                            n = P * len(keys(units[i][1])[1])
                            x = neg[:, i % 2]
                            act.wait_ge(sem("max_ready"), ub + i + 1)
                            start_at(act, "pr_ready", ub + i - 1)
                            for m in range(2):
                                p = probs[:, i % 2, m, 0:n]
                                nc.scalar.activation(p, p, ACT.Exp, bias=x[:, 2 + m:3 + m],
                                                     accum_out=total[:, i % 2, m:m + 1]).then_inc(sem("exp_done"), 1)
                            nc.scalar.activation(total[:, i % 2, 2:4], x[:, 4:6], ACT.Exp).then_inc(sem("exp_done"), 1)
                        if i >= 3 and units[i - 3][1] == TT - 1:
                            h = units[i - 3][0]
                            act.wait_ge(sem("pv_done"), ub + i - 2)
                            nc.scalar.activation(o[:, h], bank(6 + h % 2, TOK), ACT.Copy).then_inc(sem("o_ready"), 1)
            add(unit=N, exp_done=3 * N)

            with nc.Block() as block:
                @block.sync
                def _(sp):
                    load_phase(sp, f"wo{layer}", following)

                @block.tensor
                def _(pe):
                    wo_pe(pe, f"wo{layer}", o, lambda k: None, hT)

                @block.scalar
                def _(act):
                    wo_act(act, hT)

                @block.vector
                def _(dve):
                    wo_dve(dve, f"wo{layer}", layer)
            add(acc_taken=KT)
            stat_counts()
            stored["kv_stored"] = base("kv_stored")

        V_MU, V_W0, V_A0, V_KK, V_KA, V_RK, V_LNW, V_LNB, V_1KA = 0, 6, 8, 10, 11, 12, 13, 14, 15

        def flat3(ap):
            return ap.rearrange("a v k -> (a v) k")

        S_NEW = {(z, s): 2 * s + z + 1 for z in range(2) for s in range(3)}
        DSTEPS, PSTEPS = 17, 5

        def step_loads(sp, j, stage_in):
            if j == 0:
                sp.wait_ge(run_done, run_after[phases["wo1"][0] - 1])
                sp.wait_ge(sem("stage_zero"), 1)
            else:
                sp.wait_ge(sem("lora"), j * 5)
            for i, w in enumerate((I["rwkv_w2"][0].rearrange("z r d -> (z r) d"),
                                   I["rwkv_a2"][0].rearrange("z r d -> (z r) d"), I["rwkv_g2"][0])):
                sp.dma_start(slab[:, 3, i, 0:P], w[:, bass.ds(j * P, P)]).then_inc(sem("l_in"), 16)
            if j:
                sp.wait_ge(sem("v_proj"), j)
            for m in (1, 0, 2):
                sp.dma_start(slab[:, m, :, 0:P],
                             I["rwkv_wrkv"][0, m].rearrange("(k p) n -> p k n", p=P)[:, :, bass.ds(j * P, P)])\
                    .then_inc(sem("w_in"), 16)
            if j:
                sp.wait_ge(sem("s0_turned"), j * 2)
            for z in range(2):
                for hh in range(2):
                    r = slice(64 * hh, 64 * hh + 64)
                    sp.dma_start(stage_in[r, z, r], flat3(I["state_rwkv"][0, 0, z, bass.ds(j * 2 + hh, 1)]))\
                        .then_inc(sem("state_in"), 16)

        def rwkv_phases(layer):
            wo_phase(f"wo{layer}", I["rwkv_wo"][0])

        def rwkv(layer, following, room):
            c = Carve(room)
            xs = c(3, KT, TOK)
            mids = c(3, TOK)
            stage_in, stage_out, S = c(2, P), c(2, P), c(2, 2, P)
            shared = c.at
            PAD = TOK + 4
            hP, mixed, delta, w_mid = c(KT, PAD), c(2, 3, TOK), c(2, TOK), c(3, KT, P)
            PADS = (0, CTX + 2)

            with nc.Block() as block:
                @block.gpsimd
                def _(pool):
                    for at in (0, CTX + 1, CTX + 2, PAD - 1):
                        ins = nc.gpsimd.memset(hP[:, :, at:at + 1], 0.0)
                    ins.then_inc(sem("pads_zero"), 1)
                    nc.gpsimd.memset(stage_in, 0.0).then_inc(sem("stage_zero"), 1)
                    nc.gpsimd.memset(S, 0.0)

                @block.scalar
                def _(act):
                    for i, w in enumerate((I["rwkv_w1"][0], I["rwkv_a1"][0])):
                        for z in range(2):
                            act.dma_start(w_mid[:, i, :, 64 * z:64 * z + 64], w[z].rearrange("(k p) r -> p k r", p=P))\
                                .then_inc(sem("w_mid_in"), 16)
                    act.dma_start(w_mid[:, 2], I["rwkv_g1"][0].rearrange("(k p) r -> p k r", p=P))\
                        .then_inc(sem("w_mid_in"), 16)
                    norm_act(act, layer, 0, lambda k, g: hP[:, k, PADS[g] + 1:PADS[g] + 1 + (CTX, LAT)[g]])
                    act.wait_ge(sem("mids_done"), 1)
                    for i, f in enumerate((ACT.Tanh, ACT.Copy, ACT.Sigmoid)):
                        ins = nc.scalar.activation(mids[:, i], bank(2 + i, TOK), f)
                    ins.then_inc(sem("tile_done"), 1)

                @block.vector
                def _(dve):
                    link = Link(dve, "dve_step")
                    norm_dve(dve, link)
                    dve.wait_ge(sem("pads_zero"), 1)
                    for k in range(KT):
                        dve.wait_ge(sem("h_ready"), base("h_ready") + k + 1)
                        d = delta[:, k % 2]
                        for g, t in GROUPS:
                            n = t.stop - t.start
                            ins = nc.vector.tensor_tensor(d[:, t], hP[:, k, PADS[g]:PADS[g] + n],
                                                          hP[:, k, PADS[g] + 2:PADS[g] + 2 + n], ALU.add)
                        link(ins)
                        for g, t in GROUPS:
                            n = t.stop - t.start
                            ins = nc.vector.scalar_tensor_tensor(d[:, t], d[:, t], 0.5, hP[:, k, PADS[g] + 1:PADS[g] + 1 + n],
                                                                 ALU.mult, ALU.subtract)
                        link(ins)
                        if k >= 2:
                            dve.wait_ge(sem("mix_used"), k - 1)
                        for m in (3, 4, 5, 0, 1, 2):
                            dst = xs[:, m, k] if m < 3 else mixed[:, k % 2, m - 3]
                            for g, t in GROUPS:
                                n = t.stop - t.start
                                ins = nc.vector.scalar_tensor_tensor(
                                    dst[:, t], d[:, t], vecs[:, (V_MU + m) * KT + k:(V_MU + m) * KT + k + 1],
                                    hP[:, k, PADS[g] + 1:PADS[g] + 1 + n], ALU.mult, ALU.add)
                            if m == 5:
                                ins.then_inc(sem("mix_ready"), 1)
                    link.close()

                @block.tensor
                def _(pe):
                    pe.wait_ge(sem("w_mid_in"), 80)
                    for k in range(KT):
                        pe.wait_ge(sem("mix_ready"), k + 1)
                        for i in range(3):
                            mm = nc.tensor.matmul(bank(2 + i, TOK), w_mid[:, i, k], mixed[:, k % 2, i],
                                                  start=k == 0, stop=k == KT - 1)
                        mm.then_inc(sem("mix_used" if k < KT - 1 else "mids_done"), 1)

                @block.sync
                def _(sp):
                    step_loads(sp, 0, stage_in)
            norm_counts()

            c.at = shared
            spare = Carve(ada_slab[:, :, :, :].rearrange("p s k n -> p (s k n)"))
            rT, kT, vtoks, vT, gT, kn, bonus = c(TOK), c(TOK), c(2, TT, P), c(TOK), c(TOK), c(TOK), c(TOK)
            pars = c(2, 16)
            sq, inv, yT, tmp = c(TOK), c(TOK), c(TOK), c(TOK)
            decay, rate, kd = c(2, TOK), c(2, TOK), c(2, TOK)
            cum = c(2, TOK)
            pp, pi = c(2, NCH, CH + 1), c(2, TOK)
            AR, bT, kTil = c(2, NCH, 2, CH), c(2, TOK), c(2, TOK)
            LB, MC = spare(2, 6, 2 * CH), spare(2, 6, 2 * CH)
            LM, T = spare(2, 6, P), c(2, 6, P)
            TTr = [slab[:, z, 0:6, P:2 * P] for z in range(2)]
            X = [slab[:, 2 + z, 0:6, P:2 * P] for z in range(2)]

            def doubled(ap, n):
                return ap.unsqueeze(2).to_broadcast([P, n, 2, CH])

            def masks(ap, n):
                return ap.rearrange("p (h t) -> p h t", h=2).unsqueeze(1).to_broadcast([P, n, 2, CH])

            def pair(ap):
                return ap.rearrange("p i (h t) -> p i h t", h=2)

            def six(ap):
                return ap.rearrange("p (b i) t -> p b i t", b=2)

            def banks(b):
                return psum[:, b:b + 2, 0:TOK].rearrange("p b (i t) -> p b i t", i=3)

            tok = spare(2, 2, TT, P)
            R, U = c(2, 2 * P), c(2, 2 * P)
            fresh = c(2, 2, P)

            def own(ap):
                return ap.rearrange("p (c t) -> p c t", c=NCH)

            PER = dict(raw=6, tile_done=1, lora=5, k_proj=1, r_proj=1, v_proj=1, k_in=1, rec_in=1, v_in=1, pj=1, kk_sum=1, kk_sq=1, kk_std=1, kk_max=1, v_turned=1, s0_turned=2,
                       s0_ready=2, scan=2, powers=4, ar_ready=2, r_ready=2, bt_ready=2, kt_ready=2, kd_ready=2,
                       prod1=2, prod2=2, low=2, lb_ready=2, mc_ready=2, t_ready=2, tt_ready=2, lm_ready=10,
                       x_done=10, x_ready=10, inv_done=10, inv_ready=10, t_new=8, tok_turned=2, tok_ready=2,
                       r_done=8, r_in=8, u_done=8, u_in=8, s_done=8, s_new=6, y_in=1, y_sum=1, mean=1, yc=1, yc_sq=1,
                       var=1, gn_std=1, bonus_in=1, bonus_sum=1, fin_turned=1, fin_ready=1, zero=1, bb=2,
                       state_in=64, state_out=64, w_in=48, l_in=48, dstep=0, pstep=0)

            class Step:

                def __init__(self, eng, j):
                    self.eng, self.j, self.made = eng, j, {}

                def wait(self, name, k, back=0):
                    v = self.j * PER[name] + (k + START.get(name, 0) - back * PER[name])
                    self.eng.wait_ge(sem(name), v)

                def inc(self, name, ins):
                    self.made[name] = self.made.get(name, 0) + 1
                    ins.then_inc(sem(name), 1)

                def link(self, name, ins):
                    self.inc(name, ins)
                    self.wait(name, self.made[name])

                def close(self):
                    for n, m in self.made.items():
                        assert m == PER[n], (n, m, PER[n])

            START = {"tile_done": 1}
            PER["dstep"], PER["pstep"] = DSTEPS, PSTEPS

            def chunks(z, s):
                lat = (0, CTX // CH + s if z == 0 else NCH - 1 - s)
                return [lat] + ([(1, s if z == 0 else CTX // CH - 1 - s)] if s < 2 else [])

            def half(z, s):
                cp = s % 2 if z == 0 else 1 - s % 2
                return slice(CH * cp, CH * cp + CH)

            with nc.Block() as block:
                @block.sync
                def _(sp):
                    for j in range(1, KT):
                        step_loads(sp, j, stage_in)
                    sp.wait_ge(sem("u_done"), KT * PER["u_done"])
                    load_first(sp, f"wo{layer}")

                @block.tensor
                def _(pe):
                    def projections(j):
                        pe.wait_ge(sem("w_in"), 48 * (j + 1))
                        for name, m, b in (("k_proj", 1, 1), ("r_proj", 0, 5)):
                            for k in range(KT):
                                mm = nc.tensor.matmul(bank(b, TOK), slab[:, m, k, 0:P], xs[:, m, k],
                                                      start=k == 0, stop=k == KT - 1)
                                if k == KT - 1:
                                    mm.then_inc(sem(name), 1)
                                yield
                        pe.wait_ge(sem("k_in"), j + 1)
                        for t in range(TT):
                            for k in range(KT):
                                mm = nc.tensor.matmul(bank(1, TT, P)[:, t], xs[:, 2, k, t * P:(t + 1) * P],
                                                      slab[:, 2, k, 0:P], start=k == 0, stop=k == KT - 1)
                                if t == TT - 1 and k == KT - 1:
                                    mm.then_inc(sem("v_proj"), 1)
                                if k % 3 == 2 or k == KT - 1:
                                    yield

                    def lora(st, kinds):
                        for i in kinds:
                            kind, z, b = ((0, 0, 2), (0, 1, 5), (1, 0, 3), (1, 1, 6), (2, 0, 7))[i]
                            r = slice(0, P) if kind == 2 else slice(64 * z, 64 * z + 64)
                            st.inc("lora", nc.tensor.matmul(bank(b, TOK), slab[r, 3, kind, 0:P], mids[r, kind],
                                                            start=True, stop=True))

                    for piece in projections(0):
                        pass
                    st = Step(pe, 0)
                    st.wait("tile_done", 0)
                    st.wait("rec_in", 1)
                    st.wait("l_in", 48)
                    lora(st, range(5))
                    for j in range(KT):
                        vtok = vtoks[:, j % 2]
                        ahead = projections(j + 1) if j < KT - 1 else iter(())

                        def pieces(n):
                            for _ in range(n):
                                next(ahead, None)

                        st.wait("state_in", 64)
                        for z in range(2):
                            st.wait("raw", 4)
                            st.inc("s0_turned", nc.tensor.transpose(bank((2, 6)[z], P), stage_in[:, z], K["ident"]))
                        st.wait("kk_sq", 1)
                        st.wait("v_in", 1)
                        st.inc("kk_sum", nc.tensor.matmul(bank(1, TOK), K["blocks"], sq, start=True, stop=True))
                        for t in range(TT):
                            mm = nc.tensor.transpose(bank(0, TT, P)[:, t], vtok[:, t], K["ident"])
                        st.inc("v_turned", mm)
                        for z in range(2):
                            st.wait("raw", 6)
                            st.wait("kk_max", 1)
                            st.wait("s0_ready", 2)
                            st.wait("zero", 1)
                            st.wait("bt_ready", z + 1)
                            st.wait("ar_ready", z + 1)
                            st.wait("r_ready", z + 1)
                            for half_, (name, src, b) in enumerate((("prod1", bT, 0), ("prod2", kTil, 2))):
                                if half_:
                                    st.wait("kt_ready", z + 1)
                                for hh in range(2):
                                    r = slice(64 * hh, 64 * hh + 64)
                                    for ch in range(NCH):
                                        q = slice(CH * (ch % 2), CH * (ch % 2) + CH)
                                        at = (ch // 2) * P
                                        mm = nc.tensor.matmul(psum[q, 4 * z + b + hh, at:at + P],
                                                              src[r, z, ch * CH:(ch + 1) * CH],
                                                              AR[r, z, ch].rearrange("p a t -> p (a t)"),
                                                              start=True, stop=True)
                                st.inc(name, mm)
                        for z in range(2):
                            st.wait("lb_ready", z + 1)
                            for hh in range(2):
                                r = slice(64 * hh, 64 * hh + 64)
                                for ch in range(NCH):
                                    q = slice(CH * (ch % 2), CH * (ch % 2) + CH)
                                    at = (ch // 2) * CH
                                    mm = nc.tensor.matmul(psum[q, 4 * z + hh, at:at + CH], AR[r, z, ch, 0],
                                                          bT[r, z, ch * CH:(ch + 1) * CH], start=True, stop=True)
                            st.inc("low", mm)
                        for z in range(2):
                            st.wait("mc_ready", z + 1)
                            for i, src in enumerate((bT, kTil)):
                                for t in range(TT):
                                    mm = nc.tensor.transpose(bank(4 * z + 2 + i, TT, P)[:, t],
                                                             src[:, z, t * P:(t + 1) * P], K["ident"])
                            st.inc("tok_turned", mm)
                        for n in range(1, LEVELS):
                            for z in range(2):
                                m = 2 * (n - 1) + z + 1
                                if n == 1:
                                    st.wait("t_ready", z + 1)
                                    st.wait("tt_ready", z + 1)
                                else:
                                    st.wait("t_new", m - 2)
                                    st.wait("x_ready", m - 2)
                                st.wait("lm_ready", m)
                                for i in range(6):
                                    mm = nc.tensor.matmul(psum[:, 4 * z + i // 3, (i % 3) * P:(i % 3 + 1) * P], LM[:, z, i],
                                                          T[:, z, i], start=True, stop=True)
                                st.inc("x_done", mm)
                            for z in range(2):
                                m = 2 * (n - 1) + z + 1
                                st.wait("x_ready", m)
                                if n == 1:
                                    st.wait("tok_ready", z + 1)
                                else:
                                    st.wait("inv_ready", m - 2)
                                for b, x, y in ((0, TTr[z], X[z]), (2, X[z], TTr[z])):
                                    if b or n < LEVELS - 1:
                                        for i in range(6):
                                            mm = nc.tensor.matmul(psum[:, 4 * z + b + i // 3, (i % 3) * P:(i % 3 + 1) * P],
                                                                  x[:, i], y[:, i], start=True, stop=True)
                                st.inc("inv_done", mm)
                        for s in range(4):
                            for z in range(2):
                                q = half(z, s)
                                st.wait("x_ready", 9 + z)
                                if s:
                                    st.wait("s_new", S_NEW[(z, s - 1)])
                                    st.wait("r_in", 2 * (s - 1) + z + 1)
                                for stream, ch in chunks(z, s):
                                    at = stream * P
                                    nc.tensor.matmul(psum[q, 4 * z, at:at + P], AR[:, z, ch, 0], S[:, z, stream],
                                                     start=True, stop=False)
                                    for hh in range(2):
                                        mm = nc.tensor.matmul(psum[q, 4 * z, at + 64 * hh:at + 64 * hh + 64],
                                                              MC[q, z, 3 * hh + ch // 2, 0:CH],
                                                              vtok[q, ch // 2, 64 * hh:64 * hh + 64],
                                                              start=False, stop=hh == 1)
                                st.inc("r_done", mm)
                            pieces(2)
                            for z in range(2):
                                q = half(z, s)
                                st.wait("r_in", 2 * s + z + 1)
                                st.wait("inv_ready", 9 + z)
                                if s:
                                    st.wait("u_in", 2 * (s - 1) + z + 1)
                                for stream, ch in chunks(z, s):
                                    for hh in range(2):
                                        at = stream * P + 64 * hh
                                        mm = nc.tensor.matmul(psum[q, 4 * z, 2 * P + at:2 * P + at + 64],
                                                              TTr[z][q, 3 * hh + ch // 2, q], R[q, z, at:at + 64],
                                                              start=True, stop=True)
                                st.inc("u_done", mm)
                            pieces(2)
                            for z in range(2):
                                q = half(z, s)
                                st.wait("u_in", 2 * s + z + 1)
                                def y_of_state(stream, ch):
                                    nc.tensor.matmul(psum[:, 4 * z + 3, ch * CH:(ch + 1) * CH], S[:, z, stream],
                                                     AR[:, z, ch, 1], start=True, stop=False)

                                def y_of_chunk(stream, ch):
                                    t, at = ch // 2, ch * CH
                                    for hh in range(2):
                                        r = slice(64 * hh, 64 * hh + 64)
                                        a2 = stream * P + 64 * hh
                                        nc.tensor.matmul(psum[r, 4 * z + 3, at:at + CH], U[q, z, a2:a2 + 64],
                                                         LB[q, z, 3 * hh + t, CH:2 * CH], start=False, stop=False)
                                        mm = nc.tensor.matmul(psum[r, 4 * z + 3, at:at + CH],
                                                              vtok[q, t, 64 * hh:64 * hh + 64],
                                                              MC[q, z, 3 * hh + t, CH:2 * CH], start=False, stop=True)
                                    return mm

                                latent, *context = chunks(z, s)
                                for c_ in context:
                                    y_of_state(*c_)
                                    y_of_chunk(*c_)
                                y_of_state(*latent)
                                if s < 3:
                                    for stream, ch in chunks(z, s):
                                        t, a2 = ch // 2, stream * P
                                        nc.tensor.matmul(psum[:, 4 * z + 2, a2:a2 + P], tok[q, z, 0, t],
                                                         U[q, z, a2:a2 + P], start=True, stop=False)
                                        mm = nc.tensor.matmul(psum[:, 4 * z + 2, a2:a2 + P], tok[q, z, 1, t],
                                                              vtok[q, t], start=False, stop=True)
                                    st.inc("s_done", mm)
                                mm = y_of_chunk(*latent)
                                if s == 3:
                                    st.inc("s_done", mm)
                            pieces(3 if s == 3 else 2)
                        nxt = Step(pe, j + 1) if j < KT - 1 else None
                        st.wait("s_new", 6)
                        for z in range(2):
                            mm = nc.tensor.transpose(bank(6, 2, P)[:, z], S[:, z, 1], K["ident"])
                        st.inc("fin_turned", mm)
                        st.wait("y_in", 1)
                        st.inc("mean", nc.tensor.matmul(bank(0, TOK), K["blocks"], yT, start=True, stop=True))
                        st.wait("bonus_in", 1)
                        st.inc("bonus_sum", nc.tensor.matmul(bank(4, TOK), K["blocks"], bonus, start=True, stop=True))
                        if nxt:
                            nxt.wait("rec_in", 1)
                            nxt.wait("l_in", 48)
                            lora(nxt, (0, 1))
                            nxt.wait("v_in", 1)
                        st.wait("yc_sq", 1)
                        st.inc("var", nc.tensor.matmul(bank(1, TOK), K["blocks"], sq, start=True, stop=True))
                        if nxt:
                            st.wait("fin_ready", 1)
                            lora(nxt, (2, 3, 4))
                        st.close()
                        st = nxt

                @block.scalar
                def _(act):
                    act.wait_ge(sem("ends_one"), 1)

                    def take(j, name, done, dst, b):
                        act.wait_ge(sem(done), j + 1)
                        nc.scalar.activation(dst, bank(b, TOK), ACT.Copy).then_inc(sem(name), 1)

                    def take_values(j):
                        take(j, "v_in", "v_proj", vtoks[:, j % 2].rearrange("p t c -> p (t c)"), 1)

                    take(0, "k_in", "k_proj", kT, 1)
                    take(0, "rec_in", "r_proj", rT, 5)
                    take_values(0)

                    def gates(st, which):
                        for i in which:
                            dst, v, b = ((decay, V_W0, 2), (decay, V_W0, 5), (rate, V_A0, 3), (rate, V_A0, 6))[i]
                            z = i % 2
                            st.wait("lora", i + 1)
                            st.inc("raw", nc.scalar.activation(dst[:, z], bank(b, TOK), ACT.Sigmoid,
                                                               bias=pars[:, st.j % 2, v + z:v + z + 1]))

                    def key_squares(st):
                        st.wait("k_in", 1)
                        st.inc("kk_sq", nc.scalar.activation(sq, kT, ACT.Square,
                                                             scale=pars[:, st.j % 2, V_KK:V_KK + 1]))

                    st = Step(act, 0)
                    st.wait("pj", 1)
                    gates(st, range(4))
                    key_squares(st)
                    for j in range(KT):
                        for z in range(2):
                            st.wait("scan", z + 1)
                            st.inc("powers", nc.scalar.activation(pp[:, z, :, 1 - z:CH + 1 - z], own(cum[:, z]), ACT.Exp,
                                                                  scale=-DECAY))
                            st.inc("powers", nc.scalar.activation(pi[:, z], cum[:, z], ACT.Exp, scale=DECAY))
                        st.wait("kk_max", 1)
                        st.inc("kk_std", nc.scalar.activation(inv, inv, ACT.Sqrt))
                        for z in range(2):
                            st.wait("s0_turned", z + 1)
                            st.inc("s0_ready", nc.scalar.activation(S[:, z, 0], bank((2, 6)[z], P), ACT.Copy))
                        st.wait("lora", 5)
                        st.wait("tile_done", 0)
                        st.inc("raw", nc.scalar.activation(gT, bank(7, TOK), ACT.Copy))
                        st.wait("v_turned", 1)
                        st.inc("raw", nc.scalar.activation(vT, bank(0, TOK), ACT.Copy))
                        for z in range(2):
                            st.wait("tok_turned", z + 1)
                            st.inc("tok_ready", nc.scalar.activation(
                                tok[:, z].rearrange("p a t c -> p a (t c)"), psum[:, 4 * z + 2:4 * z + 4, 0:TOK], ACT.Copy))
                        for n in range(1, LEVELS):
                            for z in range(2):
                                m = 2 * (n - 1) + z + 1
                                st.wait("x_done", m)
                                if n > 1:
                                    st.wait("inv_done", m - 2)
                                st.inc("x_ready", nc.scalar.activation(six(X[z]), banks(4 * z), ACT.Copy))
                        for s in range(4):
                            for z in range(2):
                                q = half(z, s)
                                n = P * len(chunks(z, s))
                                st.wait("r_done", 2 * s + z + 1)
                                if s:
                                    st.wait("u_done", 2 * (s - 1) + z + 1)
                                st.inc("r_in", nc.scalar.activation(R[q, z, 0:n], psum[q, 4 * z, 0:n], ACT.Copy))
                            for z in range(2):
                                q = half(z, s)
                                n = P * len(chunks(z, s))
                                st.wait("u_done", 2 * s + z + 1)
                                if s:
                                    st.wait("s_done", 2 * (s - 1) + z + 1)
                                st.inc("u_in", nc.scalar.activation(U[q, z, 0:n], psum[q, 4 * z, 2 * P:2 * P + n], ACT.Copy))
                            if j < KT - 1 and s == 1:
                                take(j + 1, "k_in", "k_proj", kT, 1)
                            if j < KT - 1 and s == 2:
                                st.wait("bonus_in", 1)
                                take(j + 1, "rec_in", "r_proj", rT, 5)
                        st.wait("s_done", 8)
                        st.inc("y_sum", nc.scalar.activation(yT, bank(3, TOK), ACT.Copy))
                        st.wait("fin_turned", 1)
                        if j:
                            act.wait_ge(sem("state_out"), j * 64)
                        st.inc("fin_ready", nc.scalar.activation(stage_out.rearrange("p z c -> p (z c)"), bank(6, 2 * P),
                                                                 ACT.Copy))
                        nxt = Step(act, j + 1) if j < KT - 1 else None
                        if nxt:
                            take_values(j + 1)
                        st.wait("yc", 1)
                        st.inc("yc_sq", nc.scalar.activation(sq, tmp, ACT.Square))
                        if nxt:
                            nxt.wait("pj", 1)
                            gates(nxt, (0, 1))
                        st.wait("var", 1)
                        st.inc("gn_std", nc.scalar.activation(inv, bank(1, TOK), ACT.Sqrt, scale=1.0 / HD,
                                                              bias=K["gn_eps"]))
                        if nxt:
                            gates(nxt, (2, 3))
                            key_squares(nxt)
                        act.wait_ge(sem("fin_ready"), j + 1)
                        for z in range(2):
                            for hh in range(2):
                                r = slice(64 * hh, 64 * hh + 64)
                                act.dma_start(flat3(O["new_state_rwkv"][0, 0, z, bass.ds(j * 2 + hh, 1)]),
                                              stage_out[r, z, r]).then_inc(sem("state_out"), 16)
                        st.close()
                        st = nxt
                    act.wait_ge(sem("state_out"), KT * 64)

                @block.gpsimd
                def _(pool):
                    nc.gpsimd.memset(pp, 1.0).then_inc(sem("ends_one"), 1)
                    vec3 = vecs[:, :].rearrange("p (v k) -> p v k", k=KT)
                    for j in range(KT):
                        st = Step(pool, j)
                        par = pars[:, j % 2]
                        st.wait("tile_done", 0, back=min(j, 1))
                        st.link("pstep", nc.gpsimd.tensor_copy(par[:, 0:15], vec3[:, :, bass.ds(j, 1)].rearrange("p v k -> p (v k)")))
                        st.inc("pj", nc.gpsimd.tensor_scalar(par[:, V_1KA:V_1KA + 1], par[:, V_KA:V_KA + 1], -1.0, 1.0,
                                                             ALU.mult, ALU.add))
                        if j:
                            st.wait("fin_turned", 1, back=1)
                        st.inc("zero", nc.gpsimd.memset(S[:, :, 1], 0.0))
                        st.wait("k_in", 1)
                        for z in range(2):
                            st.wait("bb", z + 1)
                            st.inc("kd_ready", nc.gpsimd.tensor_tensor(kd[:, z], kT, kd[:, z], ALU.mult))
                        st.wait("rec_in", 1)
                        for z in range(2):
                            st.wait("powers", 2 * z + 1)
                            st.inc("r_ready", nc.gpsimd.tensor_tensor(AR[:, z, :, 1], own(rT), pp[:, z, :, 1 - z:CH + 1 - z],
                                                                      ALU.mult))
                        def level(n, z):
                            st.inc("lm_ready", nc.gpsimd.tensor_tensor(
                                pair(LM[:, z]), doubled(LB[:, z, :, 0:CH], 6), masks(levels[:, z, n - 1], 6), ALU.mult))

                        for z in range(2):
                            st.wait("lb_ready", z + 1)
                            st.link("pstep", nc.gpsimd.tensor_tensor(pair(TTr[z]), doubled(LB[:, z, :, 0:CH], 6),
                                                                     masks(pairs[:, z], 6), ALU.mult))
                            st.inc("tt_ready", nc.gpsimd.tensor_tensor(TTr[z], TTr[z], over(K["ident"], 6), ALU.add))
                            level(1, z)
                        for n in range(2, LEVELS):
                            for z in range(2):
                                st.wait("x_done", 2 * (n - 2) + z + 1)
                                level(n, z)
                        st.link("pstep", nc.gpsimd.tensor_tensor(bonus, kd[:, 0], kd[:, 1], ALU.add))
                        st.link("pstep", nc.gpsimd.tensor_tensor(bonus, bonus, rT, ALU.mult))
                        st.inc("bonus_in", nc.gpsimd.tensor_scalar(bonus, bonus, par[:, V_RK:V_RK + 1], None, ALU.mult))
                        st.close()

                @block.vector
                def _(dve):
                    def scans(st):
                        for z in range(2):
                            st.wait("raw", z + 1)
                            rev = slice(None) if z == 0 else slice(None, None, -1)
                            st.inc("scan", nc.vector.tensor_tensor_scan(cum[:, z, rev], K["restart"], decay[:, z, rev], 0.0,
                                                                        ALU.mult, ALU.add))

                    st = Step(dve, 0)
                    scans(st)
                    for j in range(KT):
                        par = pars[:, j % 2]

                        def link(ins):
                            st.link("dstep", ins)

                        st.wait("pj", 1)
                        for z in range(2):
                            st.wait("raw", 3 + z)
                            st.inc("bb", nc.vector.tensor_scalar(kd[:, z], rate[:, z], par[:, V_KA:V_KA + 1],
                                                                 par[:, V_1KA:V_1KA + 1], ALU.mult, ALU.add))
                        st.wait("kk_sum", 1)
                        st.inc("kk_max", nc.vector.tensor_scalar(inv, bank(1, TOK), 1e-24, None, ALU.max))
                        st.wait("kk_std", 1)
                        link(nc.vector.reciprocal(inv, inv))
                        st.wait("k_in", 1)
                        link(nc.vector.scalar_tensor_tensor(kn, kT, par[:, V_KK:V_KK + 1], inv, ALU.mult, ALU.mult))
                        for z in range(2):
                            link(nc.vector.tensor_tensor(rate[:, z], rate[:, z], kn, ALU.mult))
                            st.wait("powers", 2 * z + 2)
                            st.inc("bt_ready", nc.vector.tensor_tensor(bT[:, z], rate[:, z], pi[:, z], ALU.mult))
                            before = pp[:, z, :, 0:CH] if z == 0 else pp[:, z, :, 1:CH + 1]
                            st.inc("ar_ready", nc.vector.scalar_tensor_tensor(AR[:, z, :, 0], own(kn), -1.0, before,
                                                                              ALU.mult, ALU.mult))
                            st.wait("kd_ready", z + 1)
                            st.inc("kt_ready", nc.vector.tensor_tensor(kTil[:, z], kd[:, z], pi[:, z], ALU.mult))
                        for z in range(2):
                            for name, dst, b, prod in (("lb_ready", LB, 0, "prod1"), ("mc_ready", MC, 2, "prod2")):
                                st.wait(prod, z + 1)
                                src = psum[:, 4 * z + b:4 * z + b + 2, 0:TOK].rearrange("p h (t c) -> p h t c", t=TT)
                                m = causal[:, z].unsqueeze(1).unsqueeze(1).to_broadcast([P, 2, TT, 2 * CH])
                                st.inc(name, nc.vector.tensor_tensor(
                                    dst[:, z].rearrange("p (h t) c -> p h t c", h=2), src, m, ALU.mult))
                        for z in range(2):
                            st.wait("low", z + 1)
                            for hh in range(2):
                                src = psum[:, 4 * z + hh, 0:TT * CH].rearrange("p (t c) -> p t c", t=TT)
                                ins = nc.vector.tensor_tensor(pair(T[:, z, 3 * hh:3 * hh + 3]), doubled(src, 3),
                                                              masks(first[:, z], 3), ALU.mult)
                            link(ins)
                            st.inc("t_ready", nc.vector.tensor_tensor(T[:, z], T[:, z], over(K["ident"], 6), ALU.add))
                        st.wait("t_ready", 2)
                        for n in range(1, LEVELS):
                            for z in range(2):
                                st.wait("inv_done", 2 * (n - 1) + z + 1)
                                if n > 1:
                                    st.wait("inv_ready", 2 * (n - 2) + z + 1)
                                else:
                                    st.wait("tt_ready", z + 1)
                                if n < LEVELS - 1:
                                    st.inc("t_new", nc.vector.tensor_tensor(six(T[:, z]), banks(4 * z), six(T[:, z]),
                                                                            ALU.add))
                                st.inc("inv_ready", nc.vector.tensor_tensor(six(TTr[z]), banks(4 * z + 2), six(TTr[z]),
                                                                            ALU.add))
                        for s in range(3):
                            for z in range(2):
                                st.wait("s_done", 2 * s + z + 1)
                                cs = chunks(z, s)
                                end = CH if z == 0 else 0
                                for stream, ch in cs:
                                    pc = pp[:, z, ch, end:end + 1]
                                    ins = nc.vector.scalar_tensor_tensor(fresh[:, z, stream], psum[:, 4 * z + 2, stream * P:(stream + 1) * P],
                                                                         pc, K["blocks"], ALU.mult, ALU.mult)
                                link(ins)
                                for stream, ch in cs:
                                    pc = pp[:, z, ch, end:end + 1]
                                    ins = nc.vector.scalar_tensor_tensor(S[:, z, stream], S[:, z, stream], pc, fresh[:, z, stream],
                                                                         ALU.mult, ALU.add)
                                st.inc("s_new", ins)
                        st.wait("s_done", 8)
                        st.wait("y_sum", 1)
                        st.inc("y_in", nc.vector.tensor_tensor(yT, bank(7, TOK), yT, ALU.add))
                        st.wait("mean", 1)
                        st.inc("yc", nc.vector.scalar_tensor_tensor(tmp, bank(0, TOK), -1.0 / HD, yT, ALU.mult, ALU.add))
                        st.wait("bonus_sum", 1)
                        st.wait("raw", 6)
                        st.wait("yc", 1)
                        link(nc.vector.tensor_tensor(yT, bank(4, TOK), vT, ALU.mult))
                        nxt = Step(dve, j + 1) if j < KT - 1 else None
                        if nxt:
                            scans(nxt)
                        st.wait("gn_std", 1)
                        link(nc.vector.reciprocal(inv, inv))
                        link(nc.vector.tensor_tensor(tmp, tmp, inv, ALU.mult))
                        link(nc.vector.tensor_scalar(tmp, tmp, par[:, V_LNW:V_LNW + 1], par[:, V_LNB:V_LNB + 1],
                                                     ALU.mult, ALU.add))
                        link(nc.vector.tensor_tensor(tmp, tmp, yT, ALU.add))
                        st.wait("fin_ready", 1)
                        st.inc("tile_done", nc.vector.tensor_tensor(flat(hT[:, bass.ds(j, 1), :]), tmp, gT, ALU.mult))
                        st.close()
                        st = nxt
            stored["state_out"] = 64 * KT

            with nc.Block() as block:
                @block.sync
                def _(sp):
                    load_phase(sp, f"wo{layer}", following)

                @block.tensor
                def _(pe):
                    wo_pe(pe, f"wo{layer}", hT, lambda k: None, xs[:, 0])

                @block.scalar
                def _(act):
                    wo_act(act, xs[:, 0])

                @block.vector
                def _(dve):
                    wo_dve(dve, f"wo{layer}", layer)
            add(acc_taken=KT)
            stat_counts()


        def finish(room):
            carve = Carve(room)
            ytok = carve(TT, D)
            with nc.Block() as block:
                @block.tensor
                def _(pe):
                    for t in range(TT):
                        for q in range(2):
                            n = 2 * t + q
                            if n >= 2:
                                pe.wait_ge(sem("y_taken"), n - 1)
                            for k in range(4):
                                mm = nc.tensor.transpose(bank(n % 2, 4, P)[:, k], xT[:, 4 * q + k, t * P:(t + 1) * P],
                                                         K["ident"])
                            mm.then_inc(sem("y_turned"), 1)

                @block.vector
                def _(dve):
                    for n in range(2 * TT):
                        dve.wait_ge(sem("y_turned"), n + 1)
                        nc.vector.tensor_copy(ytok[:, n // 2, (n % 2) * 512:(n % 2 + 1) * 512], bank(n % 2, 512))\
                            .then_inc(sem("y_taken"), 1)

                @block.sync
                def _(sp):
                    for t in range(TT):
                        sp.wait_ge(sem("y_taken"), 2 * (t + 1))
                        dst = O["y_prompt"][0] if t == 0 else O["y_sample"][0, (t - 1) * P:t * P]
                        sp.dma_start(dst, ytok[:, t]).then_inc(sem("out"), 16)
                    sp.wait_ge(sem("out"), 16 * TT)
                    for n, v in stored.items():
                        sp.wait_ge(sem(n), v)

        stored = {}

        for layer in range(DEPTH):
            (da_phases, rwkv_phases, swa_phases)[layer % 3](layer)
            mlp_phases(layer)
        def room(name):
            return nc.sbuf_tensor(f"room_{name}", [P, ROOM], F32)

        with room("setup") as r:
            setup("qkv0", r[:, :])
        for layer in range(DEPTH):
            with room(layer) as r:
                (da, rwkv, swa)[layer % 3](layer, f"mlp{layer}", r[:, :])
            follow = {0: None, 1: "qkv2", 2: "qkv3", 3: None}[layer]
            mlp(layer, follow)
        with room("finish") as r:
            finish(r[:, :])


INPUTS = ("x_prompt x_sample cache_da_k cache_da_v state_rwkv cache_swa_k cache_swa_v c c_ctx ada_w ada_b mlp_w1 mlp_w2 "
          "da_wqkv da_q_norm da_k_norm da_lambda da_subln da_wo rwkv_mu rwkv_wrkv rwkv_w0 rwkv_w1 rwkv_w2 rwkv_a0 "
          "rwkv_a1 rwkv_a2 rwkv_g1 rwkv_g2 rwkv_k_k rwkv_k_a rwkv_r_k rwkv_ln_w rwkv_ln_b rwkv_wo swa_wqkv "
          "swa_q_norm swa_k_norm swa_sink swa_wo").split()
OUTPUTS = {"y_prompt": (1, CTX, D), "y_sample": (1, LAT, D), "new_da_k": (1, 2, CTX, 8, P), "new_da_v": (1, 2, CTX, 8, P),
           "new_state_rwkv": (1, 1, 2, 16, HD, HD), "new_swa_k": (1, 1, CTX, 4, HD), "new_swa_v": (1, 1, CTX, 4, HD)}


def kernel(**inputs):
    import concourse.bacc as bacc
    from concourse.bass_utils import run_bass_kernel_spmd

    nc = bacc.Bacc("TRN2", target_bir_lowering=False, num_devices=1)
    arrays = {f"in_{n}": np.ascontiguousarray(inputs[n]) for n in INPUTS}
    arrays["in_consts"] = constants()
    I = {n[3:]: nc.dram_tensor(n, a.shape, mybir.dt.from_np(a.dtype), kind="ExternalInput").ap()
         for n, a in arrays.items()}
    O = {n: nc.dram_tensor(f"out_{n}", s, F32, kind="ExternalOutput").ap() for n, s in OUTPUTS.items()}
    build(nc, I, O)
    r = run_bass_kernel_spmd(nc, [arrays], core_ids=[0])
    return tuple(r.results[0][f"out_{n}"] for n in OUTPUTS)
```
